# Optimizing a Trainium2 kernel written in Bass

```python
import math
import jax, jax.numpy as jnp
from jax import lax
import numpy as np

D_MODEL = 2048
BATCH = 1
SEQ = 512
DEPTH = 1

N_MEM = 256
MEM_HEADS = 4
MEM_HEAD_DIM = 128
MEM_WIDTH = MEM_HEADS * MEM_HEAD_DIM

MLA_HEADS = 8
QK_NOPE = 128
QK_ROPE = 64
V_HEAD = 128
Q_LORA = 512
KV_LORA = 512
ROPE_THETA = 10000.0
MAX_POS_OFFSET = 4096
Q_BLOCK = 128
MLA_WIDTH = MLA_HEADS * V_HEAD

LRU_WIDTH = 1024
LRU_BLOCKS = 8
LRU_BLOCK_DIM = LRU_WIDTH // LRU_BLOCKS
CONV_WIDTH = 4
CONV_PAD_LEFT = 2
LRU_C = 8.0

MIX_WIDTH = MLA_WIDTH + LRU_WIDTH
SPLIT_CQ = Q_LORA
SPLIT_CKV = SPLIT_CQ + KV_LORA
SPLIT_KPE = SPLIT_CKV + QK_ROPE
SPLIT_LRUX = SPLIT_KPE + LRU_WIDTH
IN_WIDTH = SPLIT_LRUX + LRU_WIDTH

PEER_HEADS = 8
N_KEYS = 128
N_EXPERTS = N_KEYS * N_KEYS
PEER_QUERY = 256
PEER_HALF = PEER_QUERY // 2
PEER_TOPK = 16
TOKEN_BLOCK = 128

DN_ALPHA = (2.0 * DEPTH) ** 0.25
DN_BETA = (8.0 * DEPTH) ** -0.25
LN_EPS = 1e-5
RMS_EPS = 1e-6

kernel_name = "hybrid_mla_rglru_peer_encoder"

def layer_norm(x, g, b):
    xf = x.astype(jnp.float32)
    mu = jnp.mean(xf, axis=-1, keepdims=True)
    var = jnp.mean(jnp.square(xf - mu), axis=-1, keepdims=True)
    return ((xf - mu) * lax.rsqrt(var + LN_EPS)).astype(x.dtype) * g + b

def rms_norm(x, g):
    xf = x.astype(jnp.float32)
    return (xf * lax.rsqrt(jnp.mean(xf * xf, axis=-1, keepdims=True) + RMS_EPS)).astype(x.dtype) * g

def rope_tables(positions, dtype):
    inv_freq = ROPE_THETA ** (-jnp.arange(0, QK_ROPE, 2, dtype=jnp.float32) / QK_ROPE)
    ang = positions.astype(jnp.float32)[..., None] * inv_freq
    return jnp.cos(ang).astype(dtype), jnp.sin(ang).astype(dtype)

def apply_rope(t, cos, sin):
    t1, t2 = jnp.split(t, 2, axis=-1)
    return jnp.concatenate([t1 * cos - t2 * sin, t2 * cos + t1 * sin], axis=-1)

def mla_attention(c_q, c_kv, k_pe, cos, sin, q_norm_g, w_uq, kv_norm_g, w_ukv):
    B, S, _ = c_q.shape
    q = (rms_norm(c_q, q_norm_g) @ w_uq).reshape(B, S, MLA_HEADS, QK_NOPE + QK_ROPE)
    q_nope = q[..., :QK_NOPE]
    q_pe = apply_rope(q[..., QK_NOPE:], cos[:, :, None, :], sin[:, :, None, :])
    kv = (rms_norm(c_kv, kv_norm_g) @ w_ukv).reshape(B, S, MLA_HEADS, QK_NOPE + V_HEAD)
    k_nope = kv[..., :QK_NOPE]
    v = kv[..., QK_NOPE:]
    k_rot = apply_rope(k_pe, cos, sin)
    scale = (QK_NOPE + QK_ROPE) ** -0.5
    nb = S // Q_BLOCK

    def to_blocks(t):
        return t.reshape(B, nb, Q_BLOCK, *t.shape[2:]).swapaxes(0, 1)

    def attend(blk):
        qn, qp = blk
        s = (jnp.einsum('bqhd,bkhd->bhqk', qn, k_nope)
             + jnp.einsum('bqhr,bkr->bhqk', qp, k_rot))
        p = jax.nn.softmax(s.astype(jnp.float32) * scale, axis=-1).astype(v.dtype)
        return jnp.einsum('bhqk,bkhd->bqhd', p, v)

    o = lax.map(attend, (to_blocks(q_nope), to_blocks(q_pe)))
    return o.swapaxes(0, 1).reshape(B, S, MLA_WIDTH)

def centred_depthwise_conv(x, w, b):
    S = x.shape[1]
    xp = jnp.pad(x, ((0, 0), (CONV_PAD_LEFT, CONV_WIDTH - 1 - CONV_PAD_LEFT), (0, 0)))
    out = b + xp[:, 0:S] * w[0]
    for k in range(1, CONV_WIDTH):
        out = out + xp[:, k:k + S] * w[k]
    return out

def rg_lru(xc, wa, ba, wx, bx, lam, reverse):
    B, S, _ = xc.shape
    xb = xc.reshape(B, S, LRU_BLOCKS, LRU_BLOCK_DIM)
    r = jax.nn.sigmoid(jnp.einsum('bsni,nij->bsnj', xb, wa).reshape(B, S, LRU_WIDTH) + ba)
    i = jax.nn.sigmoid(jnp.einsum('bsni,nij->bsnj', xb, wx).reshape(B, S, LRU_WIDTH) + bx)
    log_a = -LRU_C * r.astype(jnp.float32) * jax.nn.softplus(-lam.astype(jnp.float32))
    a = jnp.exp(log_a)
    b_in = jnp.sqrt(-jnp.expm1(2.0 * log_a)) * (i * xc).astype(jnp.float32)

    def combine(e1, e2):
        a1, b1 = e1
        a2, b2 = e2
        return a1 * a2, a2 * b1 + b2

    _, h = lax.associative_scan(combine, (a, b_in), axis=1, reverse=reverse)
    return h.astype(xc.dtype)

def memory_cross_attention(x, mem, wq, wk, wv, wo):
    B, S, _ = x.shape
    M = mem.shape[1]
    q = (x @ wq).reshape(B, S, MEM_HEADS, MEM_HEAD_DIM)
    k = (mem @ wk).reshape(B, M, MEM_HEADS, MEM_HEAD_DIM)
    v = (mem @ wv).reshape(B, M, MEM_HEADS, MEM_HEAD_DIM)
    s = jnp.einsum('bshd,bmhd->bhsm', q, k).astype(jnp.float32) * (MEM_HEAD_DIM ** -0.5)
    p = jax.nn.softmax(s, axis=-1).astype(v.dtype)
    o = jnp.einsum('bhsm,bmhd->bshd', p, v).reshape(B, S, MEM_WIDTH)
    return o @ wo

def peer_ffn(x, w_pq, sub_keys1, sub_keys2, peer_u, peer_v):
    B, S, D = x.shape
    T = B * S
    xt = x.reshape(T, D)
    q = (xt @ w_pq).reshape(T, PEER_HEADS, PEER_QUERY)
    s1 = jnp.einsum('thd,nd->thn', q[..., :PEER_HALF], sub_keys1).astype(jnp.float32)
    s2 = jnp.einsum('thd,nd->thn', q[..., PEER_HALF:], sub_keys2).astype(jnp.float32)
    v1, i1 = lax.top_k(s1, PEER_TOPK)
    v2, i2 = lax.top_k(s2, PEER_TOPK)
    cand_s = (v1[..., :, None] + v2[..., None, :]).reshape(T, PEER_HEADS, PEER_TOPK * PEER_TOPK)
    cand_i = (i1[..., :, None] * N_KEYS + i2[..., None, :]).reshape(T, PEER_HEADS, PEER_TOPK * PEER_TOPK)
    top_s, pos = lax.top_k(cand_s, PEER_TOPK)
    idx = jnp.take_along_axis(cand_i, pos, axis=-1)
    gate = jax.nn.softmax(top_s, axis=-1).astype(x.dtype)
    nb = T // TOKEN_BLOCK

    def experts(blk):
        xb, ib, gb = blk
        u_sel = jnp.take(peer_u, ib, axis=0)
        act = jax.nn.gelu(jnp.einsum('thkd,td->thk', u_sel, xb), approximate=False) * gb
        v_sel = jnp.take(peer_v, ib, axis=0)
        return jnp.einsum('thk,thkd->td', act, v_sel)

    out = lax.map(experts, (xt.reshape(nb, TOKEN_BLOCK, D),
                            idx.reshape(nb, TOKEN_BLOCK, PEER_HEADS, PEER_TOPK),
                            gate.reshape(nb, TOKEN_BLOCK, PEER_HEADS, PEER_TOPK)))
    return out.reshape(B, S, D)

def setup_inputs(seed: int = 0) -> dict:
    key = jax.random.key(seed)
    ks = iter(jax.random.split(key, 48))

    def nrm(shape, scale):
        return jax.random.normal(next(ks), shape, jnp.float32) * scale

    def gain(shape):
        return 1.0 + nrm(shape, 0.02)

    L = DEPTH
    x = nrm((BATCH, SEQ, D_MODEL), 1.0)
    mem = nrm((BATCH, N_MEM, D_MODEL), 1.0)
    offsets = jax.random.randint(next(ks), (BATCH, 1), 0, MAX_POS_OFFSET, dtype=jnp.int32)
    positions = offsets + jnp.arange(SEQ, dtype=jnp.int32)[None, :]
    in_ln_g = gain((D_MODEL,))
    in_ln_b = nrm((D_MODEL,), 0.02)
    w_in = nrm((L, D_MODEL, IN_WIDTH), D_MODEL ** -0.5)
    q_norm_g = gain((L, Q_LORA))
    w_uq = nrm((L, Q_LORA, MLA_HEADS * (QK_NOPE + QK_ROPE)), Q_LORA ** -0.5)
    kv_norm_g = gain((L, KV_LORA))
    w_ukv = nrm((L, KV_LORA, MLA_HEADS * (QK_NOPE + V_HEAD)), KV_LORA ** -0.5)
    conv_w = nrm((L, CONV_WIDTH, LRU_WIDTH), CONV_WIDTH ** -0.5)
    conv_b = nrm((L, LRU_WIDTH), 0.02)
    lru_wa = nrm((L, 2, LRU_BLOCKS, LRU_BLOCK_DIM, LRU_BLOCK_DIM), LRU_BLOCK_DIM ** -0.5)
    lru_ba = nrm((L, 2, LRU_WIDTH), 0.02)
    lru_wx = nrm((L, 2, LRU_BLOCKS, LRU_BLOCK_DIM, LRU_BLOCK_DIM), LRU_BLOCK_DIM ** -0.5)
    lru_bx = nrm((L, 2, LRU_WIDTH), 0.02)
    a0 = jax.random.uniform(next(ks), (L, 2, LRU_WIDTH), jnp.float32, 0.9, 0.999)
    s0 = a0 ** (1.0 / LRU_C)
    lru_lambda = jnp.log(s0) - jnp.log1p(-s0)
    attn_out_g = gain((L, MLA_WIDTH))
    lru_out_g = gain((L, LRU_WIDTH))
    w_out = nrm((L, MIX_WIDTH, D_MODEL), DN_BETA * MIX_WIDTH ** -0.5)
    ln1_g = gain((L, D_MODEL))
    ln1_b = nrm((L, D_MODEL), 0.02)
    w_mq = nrm((L, D_MODEL, MEM_WIDTH), D_MODEL ** -0.5)
    w_mk = nrm((L, D_MODEL, MEM_WIDTH), D_MODEL ** -0.5)
    w_mv = nrm((L, D_MODEL, MEM_WIDTH), D_MODEL ** -0.5)
    w_mo = nrm((L, MEM_WIDTH, D_MODEL), DN_BETA * MEM_WIDTH ** -0.5)
    ln2_g = gain((L, D_MODEL))
    ln2_b = nrm((L, D_MODEL), 0.02)
    w_pq = nrm((L, D_MODEL, PEER_HEADS * PEER_QUERY), D_MODEL ** -0.5)
    sub_keys1 = nrm((L, N_KEYS, PEER_HALF), PEER_HALF ** -0.5)
    sub_keys2 = nrm((L, N_KEYS, PEER_HALF), PEER_HALF ** -0.5)
    peer_u = nrm((L, N_EXPERTS, D_MODEL), D_MODEL ** -0.5)
    peer_v = nrm((L, N_EXPERTS, D_MODEL), DN_BETA)
    ln3_g = gain((L, D_MODEL))
    ln3_b = nrm((L, D_MODEL), 0.02)
    return {
        "x": x, "mem": mem, "positions": positions,
        "in_ln_g": in_ln_g, "in_ln_b": in_ln_b,
        "w_in": w_in, "q_norm_g": q_norm_g, "w_uq": w_uq, "kv_norm_g": kv_norm_g, "w_ukv": w_ukv,
        "conv_w": conv_w, "conv_b": conv_b,
        "lru_wa": lru_wa, "lru_ba": lru_ba, "lru_wx": lru_wx, "lru_bx": lru_bx, "lru_lambda": lru_lambda,
        "attn_out_g": attn_out_g, "lru_out_g": lru_out_g, "w_out": w_out,
        "ln1_g": ln1_g, "ln1_b": ln1_b,
        "w_mq": w_mq, "w_mk": w_mk, "w_mv": w_mv, "w_mo": w_mo,
        "ln2_g": ln2_g, "ln2_b": ln2_b,
        "w_pq": w_pq, "sub_keys1": sub_keys1, "sub_keys2": sub_keys2,
        "peer_u": peer_u, "peer_v": peer_v,
        "ln3_g": ln3_g, "ln3_b": ln3_b,
    }

def reference(x, mem, positions, in_ln_g, in_ln_b, w_in, q_norm_g, w_uq, kv_norm_g, w_ukv,
              conv_w, conv_b, lru_wa, lru_ba, lru_wx, lru_bx, lru_lambda,
              attn_out_g, lru_out_g, w_out, ln1_g, ln1_b,
              w_mq, w_mk, w_mv, w_mo, ln2_g, ln2_b,
              w_pq, sub_keys1, sub_keys2, peer_u, peer_v, ln3_g, ln3_b):
    cos, sin = rope_tables(positions, x.dtype)
    x = layer_norm(x, in_ln_g, in_ln_b)
    for l in range(DEPTH):
        h = x @ w_in[l]
        c_q = h[..., :SPLIT_CQ]
        c_kv = h[..., SPLIT_CQ:SPLIT_CKV]
        k_pe = h[..., SPLIT_CKV:SPLIT_KPE]
        lru_x = h[..., SPLIT_KPE:SPLIT_LRUX]
        lru_gate = h[..., SPLIT_LRUX:]
        y_attn = mla_attention(c_q, c_kv, k_pe, cos, sin, q_norm_g[l], w_uq[l], kv_norm_g[l], w_ukv[l])
        xc = centred_depthwise_conv(lru_x, conv_w[l], conv_b[l])
        h_fwd = rg_lru(xc, lru_wa[l, 0], lru_ba[l, 0], lru_wx[l, 0], lru_bx[l, 0], lru_lambda[l, 0], False)
        h_bwd = rg_lru(xc, lru_wa[l, 1], lru_ba[l, 1], lru_wx[l, 1], lru_bx[l, 1], lru_lambda[l, 1], True)
        y_lru = (h_fwd + h_bwd) * jax.nn.gelu(lru_gate)
        y_mix = jnp.concatenate([rms_norm(y_attn, attn_out_g[l]), rms_norm(y_lru, lru_out_g[l])], axis=-1)
        x = layer_norm(DN_ALPHA * x + y_mix @ w_out[l], ln1_g[l], ln1_b[l])
        y_mem = memory_cross_attention(x, mem, w_mq[l], w_mk[l], w_mv[l], w_mo[l])
        x = layer_norm(DN_ALPHA * x + y_mem, ln2_g[l], ln2_b[l])
        y_ffn = peer_ffn(x, w_pq[l], sub_keys1[l], sub_keys2[l], peer_u[l], peer_v[l])
        x = layer_norm(DN_ALPHA * x + y_ffn, ln3_g[l], ln3_b[l])
    return x


_drawn_inputs = setup_inputs


def setup_inputs(seed=0):
    import zlib

    import numpy as np

    out = dict(_drawn_inputs(seed))
    spreads = {}
    factors = {'q_norm_g': 2.681,
     'lru_ba': 5.804,
     'lru_bx': 4.269,
     'attn_out_g': 2.675,
     'ln3_g': 8.077,
     'ln3_b': 8.147,
     'lru_out_g': 3.074}
    for name, (base, spread) in spreads.items():
        noise = np.random.default_rng([zlib.crc32(name.encode()), seed]).standard_normal(out[name].shape)
        drawn = base * np.exp(spread * noise) if base else spread * noise
        out[name] = __import__('jax').numpy.asarray(drawn.astype(out[name].dtype))
    for name, factor in factors.items():
        out[name] = (out[name] * factor).astype(out[name].dtype)
    return out
```

```python
import math
from contextlib import ExitStack

import numpy as np

import concourse.bass as bass
from concourse import mybir

F32 = mybir.dt.float32
I32 = mybir.dt.int32
U32 = mybir.dt.uint32
ALU = mybir.AluOpType
ACT = mybir.ActivationFunctionType
AX = mybir.AxisListType.X

P = 128
D = 2048
S = 512
NB = S // P
KT = D // P
MEM = 256
MH = 4
HEADS = 8
NOPE = 128
ROPE = 64
LORA = 512
LW = 1024
NL = LW // P
PH = 8
NK = 128
TOPK = 16
HK = PH * TOPK
HALVES = 2 * PH
CQ, CKV, KPE, LRUX = 512, 1024, 1088, 2112
ALPHA = 2.0 ** 0.25
LN_EPS = 1e-5
RMS_EPS = 1e-6
ATT_SCALE = (NOPE + ROPE) ** -0.5
MEM_SCALE = 128.0 ** -0.5

TW = 1024
NW = 4
BANK = 512
ARENA = 53 * 1000

C_CONVW, C_CONVB, C_BA, C_BX, C_LAM, C_QG, C_KVG, C_AG, C_LG, C_FREQ, C_SIGN = 0, 32, 40, 56, 72, 88, 92, 96, 104, 112, 113
NCOL = 114

TWO_PI_A = 6.28125
TWO_PI_B = float(np.float32(round((2 * math.pi - TWO_PI_A) * 2 ** 20) / 2 ** 20))
TWO_PI_C = float(2 * math.pi - TWO_PI_A - TWO_PI_B)
ROUND = 12582912.0

QUAD = [0, 1, 2, 3]
PE_ORDER = ([f"x1T{q}" for q in QUAD] + ["q", "qT", "sc", "pT", "pv"] + [f"wo{c}" for c in QUAD]
            + [f"x2T{q}" for q in QUAD]
            + ["pq0", "pq1", "pqT0", "pq2", "key0", "pqT1", "pq3", "key1", "pqT2", "key2", "pqT3", "key3"])
TILES_AT = {"q": 8, "wo0": 10, "wo1": 12, "wo2": 14, "wo3": 16, "pq0": 24, "pq1": 32, "pq2": 40, "pq3": 48}
PE_STEPS = [n for n in PE_ORDER if n not in TILES_AT]
ACT_STEPS = (["xs"] + [f"x1T{q}" for q in QUAD] + ["q", "qT", "exp", "pT", "pv"] + [f"x2T{q}" for q in QUAD]
             + ["pq0", "pq1", "pqT0", "pq2", "key0", "pqT1", "pq3", "key1", "pqT2", "key2", "pqT3", "key3", "gate"])
DVE_STEPS = ["max", "prob"] + [f"wo{c}" for c in QUAD] + ["x2", "top", "idx"]
PE_AT = {n: k + 1 for k, n in enumerate(PE_STEPS)}
ACT_AT = {n: k + 1 for k, n in enumerate(ACT_STEPS)}
DVE_AT = {n: k + 1 for k, n in enumerate(DVE_STEPS)}


class InOrder:

    def __init__(self, eng, sem):
        self.eng, self.sem, self.base, self.k, self.outer = eng, sem, 0, 0, []

    def __call__(self, ins, tick=None):
        ins.then_inc(self.sem, 1)
        self.k += 1
        self.eng.wait_ge(self.sem, self.base + self.k)
        if tick is not None:
            self.eng.sem_inc(tick, 1)

    def enter(self, i, per):
        self.outer.append((self.base + self.k, per))
        self.base, self.k = self.base + self.k + i * per, 0

    def leave(self, count):
        start, per = self.outer.pop()
        assert self.k == per, (self.k, per)
        self.base, self.k = start + count * per, 0


def build(nc, x, memT, pos, cols_d, w_once, w_block, wq_pairs, lru_w, keysT, gains, peer_u, peer_v, out):
    N_ONCE = w_once.shape[0]
    N_BLOCK = w_block.shape[0]
    with ExitStack() as ctx:
        def sem(name):
            return ctx.enter_context(nc.semaphore(name))

        base = nc.sbuf_base
        arena = ctx.enter_context(nc.sbuf_tensor("arena", [P, ARENA], F32))
        at0 = [0]

        def place(name, cols, at=None, dt=F32):
            at = at0[0] if at is None else at
            at0[0] = at + cols
            assert at + cols <= ARENA
            v = arena[:, at:at + cols]
            return v if dt == F32 else v.bitcast(dt)

        X = place("X", NB * D, 0)
        A = place("A", KT * S, 8192)
        KN, V = A[:, 0:4096], A[:, 4096:8192]
        U_RING = A
        Y = place("Y", KT * S, 16384)
        MEMT = Y[:, 0:KT * MEM]
        V_RING = Y
        W = place("W", NW * TW, 24576)
        KM = place("KM", MH * MEM, 28672)
        VM = place("VM", 2 * 512, 29696)
        C = place("C", 8 * S, 30720)
        GAIN_G, GAIN_B = C[:, 0:D], C[:, D:2 * D]
        at0[0] = 34816
        COLS = place("cols", NCOL)
        IDENT = place("ident", P)
        ALPHA_I = place("alpha_i", P)
        ONES = place("ones", P)
        KEYS = place("keys", 2 * NK)
        IOTA = place("iota", TOPK)
        C4 = place("c4", 16)
        SM = place("small", 256)
        SC = at0[0]
        COS, SINS, KR = (place(n, S) for n in ("cos", "sins", "kr"))
        RS = place("rs", S)
        SQ = [place(f"sq{e}", S) for e in range(2)]
        TMP, TMP2 = place("tmp", S), place("tmp2", S)
        SC2 = at0[0]
        LX = [place(f"lx{e}", S + 4) for e in range(2)]
        XC1 = [place(f"xc{e}", S) for e in range(2)]
        LWT = [place(f"lw{e}", 4 * P) for e in range(2)]
        R_ = [place(f"r{d}", S) for d in range(2)]
        I_ = [place(f"i{d}", S) for d in range(2)]
        D_ = [place(f"d{d}", S) for d in range(2)]
        H_ = [place(f"h{d}", S) for d in range(2)]
        at0[0] = SC2
        WQ = place("wq", 2048)
        QN = [place(f"qn{e}", S) for e in range(2)]
        QR = place("qr", S)
        PM = [place(f"pm{e}", S) for e in range(2)]
        PT = place("pt", 4 * S)
        VH = [place(f"vh{e}", 4 * P) for e in range(2)]
        at0[0] = SC
        G3G, G3B = place("g3g", D), place("g3b", D)
        XC = place("xc", D)
        XS = place("xs", D)
        CAND = XS
        XT = place("xT", D)
        EQ = XT
        SK = place("keys scores", HALVES * NK)
        PR, PRT = SK[:, 0:1024], SK[:, 1024:2048]
        QB_AT = at0[0]
        QB = [place(f"qb{e}", 512) for e in range(2)]
        QT = place("qT", 512)
        OT = place("oT", 512)
        DIAG = [place(f"diag{e}", 4 * P) for e in range(2)]
        IDX = place("idx", HK, dt=I32)
        GATE = place("gate", HK)
        IU = [place(f"iu{e}", 4, dt=I32) for e in range(2)]
        IV = [place(f"iv{e}", 4, dt=I32) for e in range(2)]
        DOT = [place(f"dot{e}", 4) for e in range(2)]
        GEL = [place(f"gel{e}", 4) for e in range(2)]
        AV = [place(f"act{e}", 4) for e in range(2)]
        at0[0] = QB_AT
        TV = place("top values", HALVES * TOPK)
        TI = place("top index", HALVES * TOPK, dt=U32)
        TIF = place("top index as float", HALVES * TOPK)
        CV = place("chosen sums", HK)
        CP = place("chosen places", HK, dt=U32)
        CA = place("first part", HK, dt=U32)
        CB = place("second part", HK, dt=U32)
        CAF, CBF = place("caf", HK), place("cbf", HK)
        S1, S2 = place("s1", HK), place("s2", HK)
        assert at0[0] <= QB_AT + 2048

        STATS, MV, RSTD, NEWTON = SM[:, 0:24], SM[:, 24:26], SM[:, 26:27], SM[:, 27:28]
        MX, NMX, RSUM, RINV = SM[:, 32:36], SM[:, 36:40], SM[:, 40:44], SM[:, 44:48]
        LM = [SM[:, 64 + 16 * k:80 + 16 * k] for k in range(6)]
        GS, GR = SM[:, 48:56], SM[:, 56:64]
        MX2 = [SM[:, 160 + 8 * e:161 + 8 * e] for e in range(2)]
        NM2 = [SM[:, 161 + 8 * e:162 + 8 * e] for e in range(2)]
        RSM2 = [SM[:, 162 + 8 * e:163 + 8 * e] for e in range(2)]
        RI2 = [SM[:, 163 + 8 * e:164 + 8 * e] for e in range(2)]

        ps = ctx.enter_context(nc.psum_tensor("ps", [P, 8, BANK], F32))

        def bank(k, n=BANK):
            return ps[:, k, 0:n]

        def col(k):
            return COLS[:, k:k + 1]

        consts_set = sem("consts_set")
        consts2_set = sem("consts2_set")
        cols_in = sem("cols_in")
        keys_in = sem("keys_in")
        x_in = [sem(f"x_in{b}") for b in range(NB)]
        mem_in = sem("mem_in")
        pos_in = sem("pos_in")
        gain0_in, gain1_in, gain2_in, gain3_in = (sem(f"gain{k}_in") for k in range(4))
        w_full = [sem(f"w_full{s}") for s in range(NW)]
        w_used = sem("w_used")
        mem_ev = sem("mem_ev")
        ln0_done = sem("ln0_done")
        x0T_mm, x0T_ev = sem("x0T_mm"), sem("x0T_ev")
        lw_full = [sem(f"lw_full{e}") for e in range(2)]
        r_mm = sem("r_mm")
        xbank_free, gbank_free, rbank_free = sem("xbank_free"), sem("gbank_free"), sem("rbank_free")
        conv_done, lru_done, u_ready = sem("conv_done"), sem("lru_done"), sem("u_ready")
        tanh_done, lam_abs, lam_exp = sem("tanh_done"), sem("lam_abs"), sem("lam_exp")
        angle, rope_tab = sem("angle"), sem("rope_tab")
        l2_ev = sem("l2_ev")
        rms_sq, rms_mm, rms_done = sem("rms_sq"), sem("rms_mm"), sem("rms_done")
        kr_done = sem("kr_done")
        kv_ev = sem("kv_ev")
        wq_full = sem("wq_full")
        qpe_mm, qn_mm, qn_ev, qr_done = sem("qpe_mm"), sem("qn_mm"), sem("qn_ev"), sem("qr_done")
        s_mm, nmx_done, exp_done, p_done = sem("s_mm"), sem("nmx_done"), sem("exp_done"), sem("p_done")
        t_mm, pt_ev, pv_mm, o_ev, vh_done = sem("t_mm"), sem("pt_ev"), sem("pv_mm"), sem("o_ev"), sem("vh_done")
        o_added = sem("o_added")
        ln1_done = sem("ln1_done")
        e_mm, e_ev, e_dv = sem("e_mm"), sem("e_ev"), sem("e_dv")
        u_full = [sem(f"u_full{s}") for s in range(4)]
        v_full = [sem(f"v_full{s}") for s in range(4)]
        u_free, v_free = sem("u_free"), sem("v_free")
        gel_done, act_done, diag_done = sem("gel_done"), sem("act_done"), sem("diag_done")
        y_ready, y_out, xc_free = sem("y_ready"), sem("y_out"), sem("xc_free")
        iu_set, iv_set, pool_tick = sem("iu_set"), sem("iv_set"), sem("pool_tick")
        dve_done, dve_tick, act_tick = sem("dve_done"), sem("dve_tick"), sem("act_tick")

        block = ctx.enter_context(nc.Block())

        @block.sync
        def _(sp):
            sp.dma_start(COLS, cols_d).then_inc(cols_in, 16)
            sp.dma_start(MEMT, memT).then_inc(mem_in, 16)
            for s in range(NW):
                sp.dma_start(W[:, s * TW:(s + 1) * TW], w_once[s]).then_inc(w_full[s], 16)
            for b in range(NB):
                sp.dma_start(X[:, b * D:(b + 1) * D], x[b * P:(b + 1) * P, :]).then_inc(x_in[b], 16)
                if b == 0:
                    sp.dma_start(GAIN_G, gains[0:1, :].partition_broadcast(P)).then_inc(gain0_in, 16)
                    sp.dma_start(GAIN_B, gains[1:2, :].partition_broadcast(P)).then_inc(gain0_in, 16)
            sp.dma_start(KEYS, keysT).then_inc(keys_in, 16)
            sp.dma_start(TMP.bitcast(I32), pos.partition_broadcast(P)).then_inc(pos_in, 16)
            with sp.Fori(1, N_ONCE // NW) as i:
                for s in range(NW):
                    sp.wait_ge(w_used, i * NW + (s - NW + 1))
                    sp.dma_start(W[:, s * TW:(s + 1) * TW],
                                 w_once[bass.ds(i * NW + s, 1), :, :].rearrange("t p n -> p (t n)")
                                 ).then_inc(w_full[s], 16)
            with sp.Fori(0, NB) as b:
                with sp.Fori(0, N_BLOCK // NW) as i:
                    for s in range(NW):
                        sp.wait_ge(w_used, b * N_BLOCK + i * NW + (N_ONCE + s - NW + 1))
                        sp.dma_start(W[:, s * TW:(s + 1) * TW],
                                     w_block[bass.ds(i * NW + s, 1), :, :].rearrange("t p n -> p (t n)")
                                     ).then_inc(w_full[s], 16)

        @block.gpsimd
        def _(pool):
            pool.sem_inc(xc_free, 1)
            pool.memset(IDENT, 0.0).then_inc(consts_set, 1)
            pool.memset(ONES, 1.0).then_inc(consts_set, 1)
            pool.memset(ALPHA_I, 0.0).then_inc(consts_set, 1)
            for e in range(2):
                pool.memset(LX[e], 0.0).then_inc(consts_set, 1)
            pool.iota(IOTA, pattern=[[1, TOPK]], base=0, channel_multiplier=0,
                      allow_small_or_imprecise_dtypes=True).then_inc(consts_set, 1)
            pool.wait_ge(consts_set, 6)
            pool.affine_select(out=IDENT, in_=IDENT, compare_op=ALU.not_equal, fill=1.0, base=0,
                               pattern=[[-1, P]], channel_multiplier=1).then_inc(consts2_set, 1)
            pool.affine_select(out=ALPHA_I, in_=ALPHA_I, compare_op=ALU.not_equal, fill=ALPHA, base=0,
                               pattern=[[-1, P]], channel_multiplier=1).then_inc(consts2_set, 1)
            for n in range(NL):
                if n >= 2:
                    pool.wait_ge(r_mm, n - 1)
                pool.dma_start(LWT[n % 2], lru_w[n]).then_inc(lw_full[n % 2], 16)
            pool.wait_ge(lru_done, NL + 1)
            pool.dma_start(WQ, wq_pairs[0]).then_inc(wq_full, 16)
            pool.wait_ge(kv_ev, 16)

            def copy_v(hp):
                for e in range(2):
                    pool.wait_ge(pv_mm, hp * 2 + (e + 1))
                    pool.sem_inc(pool_tick, 1)
                    pool.tensor_copy(VH[e].rearrange("p (t v) -> p t v", t=4),
                                     V.rearrange("p (t w) -> p t w", t=4)[:, :, bass.ds(hp * 256 + e * P, P)]
                                     ).then_inc(vh_done, 1)

            with pool.Fori(0, HEADS // 2 - 1) as hp:
                copy_v(hp)
                pool.wait_ge(qn_mm, hp * 2 + 2)
                pool.sem_inc(pool_tick, 1)
                pool.dma_start(WQ, wq_pairs[bass.ds(hp + 1, 1), :, :].rearrange("a p n -> p (a n)")
                               ).then_inc(wq_full, 16)
            copy_v(HEADS // 2 - 1)
            pool.wait_ge(qn_mm, HEADS)
            pool.dma_start(GAIN_G, gains[2:3, :].partition_broadcast(P)).then_inc(gain1_in, 16)
            pool.dma_start(GAIN_B, gains[3:4, :].partition_broadcast(P)).then_inc(gain1_in, 16)
            pool.wait_ge(ln1_done, NB)
            pool.dma_start(GAIN_G, gains[4:5, :].partition_broadcast(P)).then_inc(gain2_in, 16)
            pool.dma_start(GAIN_B, gains[5:6, :].partition_broadcast(P)).then_inc(gain2_in, 16)
            pool.dma_start(G3G, gains[6:7, :].partition_broadcast(P)).then_inc(gain3_in, 16)
            pool.dma_start(G3B, gains[7:8, :].partition_broadcast(P)).then_inc(gain3_in, 16)

            def index(dst, j, ready, n):
                pool.tensor_copy(dst, IDX[:, bass.ds(j * 4, 4)]).then_inc(ready, 1)
                pool.wait_ge(ready, n)
                pool.sem_inc(pool_tick, 1)

            def row(ring, table, idx, s, full, free, need):
                pool.wait_ge(free, need)
                pool.sem_inc(pool_tick, 1)
                pool.indirect_dma_start(ring[:, s * D:(s + 1) * D], None, table,
                                        bass.IndirectOffsetOnAxis(ap=idx[:, s:s + 1], axis=0)
                                        ).then_inc(full[s], 16)

            def rows(b, j, par, last=False):
                if not last:
                    index(IU[1 - par], j + 1, iu_set, b * 32 + (j + 2))
                index(IV[par], j, iv_set, b * 32 + (j + 1))
                for s in range(4):
                    if not last:
                        row(U_RING, peer_u, IU[1 - par], s, u_full, u_free, b * HK + (j * 4 + (s + 5)))
                    row(V_RING, peer_v, IV[par], s, v_full, v_free, b * HK + (j * 4 + (s + 5)))

            with pool.Fori(0, NB) as b:
                pool.wait_ge(e_dv, b * len(DVE_STEPS) + DVE_AT["idx"])
                pool.sem_inc(pool_tick, 1)
                index(IU[0], 0, iu_set, b * 32 + 1)
                for s in range(4):
                    row(U_RING, peer_u, IU[0], s, u_full, u_free, b * HK + (s + 1))
                with pool.Fori(0, 15) as jj:
                    for par in range(2):
                        rows(b, jj * 2 + par, par)
                rows(b, 30, 0)
                rows(b, 31, 1, last=True)
                pool.wait_ge(y_ready, b + 2)
                pool.sem_inc(pool_tick, 1)
                pool.dma_start(out[bass.ds(b * P, P), :], XC).then_inc(y_out, 16)
                pool.wait_ge(y_out, b * 16 + 16)
                pool.sem_inc(xc_free, 1)
            pool.wait_ge(y_out, 16 * NB)

        @block.tensor
        def _(pe):
            def tile_wait(t, groups=0):
                pe.wait_ge(w_full[t % NW], groups * 16 + 16 * (t // NW + 1))

            def tile(t):
                return W[:, (t % NW) * TW:(t % NW + 1) * TW]

            pe.sem_inc(t_mm, 2)
            pe.sem_inc(pv_mm, 2)
            pe.sem_inc(v_free, 8)
            pe.wait_ge(mem_in, 16)
            t = 0
            for h in range(MH):
                for half in range(2):
                    tile_wait(t)
                    for k in range(8):
                        kt = half * 8 + k
                        last = pe.matmul(bank(h, MEM), tile(t)[:, k * P:(k + 1) * P], MEMT[:, kt * MEM:(kt + 1) * MEM],
                                         start=(kt == 0), stop=(kt == KT - 1))
                    last.then_inc(w_used, 1)
                    t += 1
            for j in range(8):
                tile_wait(t)
                for m in range(2):
                    for k in range(2):
                        kt = 2 * j + k
                        last = pe.matmul(bank(4 + m), MEMT[:, kt * MEM + m * P:kt * MEM + (m + 1) * P],
                                         tile(t)[:, k * 512:(k + 1) * 512], start=(kt == 0), stop=(kt == KT - 1))
                last.then_inc(w_used, 1)
                t += 1
            pe.wait_ge(consts2_set, 2)
            for b in range(NB):
                pe.wait_ge(ln0_done, b + 1)
                for q in range(4):
                    n = 4 * b + q
                    if n >= 2:
                        pe.wait_ge(x0T_ev, n - 1)
                    for k in range(4):
                        kt = 4 * q + k
                        last = pe.transpose(ps[:, 6 + n % 2, k * P:(k + 1) * P],
                                            X[:, b * D + kt * P:b * D + (kt + 1) * P], IDENT)
                    last.then_inc(x0T_mm, 1)
            pe.wait_ge(x0T_ev, 4 * NB)
            pe.wait_ge(mem_ev, 6)

            def from_x0(out_ap, t, groups):
                for half in range(2):
                    tile_wait(t + half, groups)
                    for k in range(8):
                        kt = half * 8 + k
                        last = pe.matmul(out_ap, tile(t + half)[:, k * P:(k + 1) * P], A[:, kt * S:(kt + 1) * S],
                                         start=(kt == 0), stop=(kt == KT - 1))
                    last.then_inc(w_used, 1)

            with pe.Fori(0, NL // 2) as i:
                for e in range(2):
                    pe.wait_ge(xbank_free, i * 2 + (e + 1))
                    from_x0(bank(e), t + 2 * e, i * 2)
                for e in range(2):
                    pe.wait_ge(gbank_free, i * 2 + (e + 1))
                    from_x0(bank(2 + e), t + 4 + 2 * e, i * 2)
                    pe.wait_ge(conv_done, i * 2 + (e + 3))
                    pe.wait_ge(rbank_free, i * 2 + (e + 1))
                    pe.wait_ge(lw_full[e], i * 16 + 16)
                    for q in range(4):
                        last = pe.matmul(bank(4 + q), LWT[e][:, q * P:(q + 1) * P], XC1[e], start=True, stop=True)
                    last.then_inc(r_mm, 1)
            t += 8 * (NL // 2)
            pe.wait_ge(xbank_free, NL + 2)
            pe.wait_ge(gbank_free, NL + 2)
            pe.wait_ge(rbank_free, NL + 1)
            with pe.Fori(0, 2) as i:
                for j in range(4):
                    from_x0(ps[:, bass.ds(i * 4 + j, 1), :].rearrange("p a n -> p (a n)"), t + 2 * j, i * 2)
            t += 16
            pe.wait_ge(l2_ev, 2)
            for j in range(2):
                from_x0(bank(j), t + 2 * j, 0)
            t += 4

            def squares(first, count, b):
                for r in range(count):
                    pe.wait_ge(rms_sq, first + r + 1)
                    pe.matmul(bank(b), ONES, SQ[(first + r) % 2], start=(r == 0), stop=(r == count - 1)
                              ).then_inc(rms_mm, 1)

            pe.wait_ge(l2_ev, 8)
            squares(0, 4, 2)
            squares(4, 4, 3)
            pe.wait_ge(rms_done, 1)
            for hh in range(HEADS // 2):
                if hh >= 2:
                    pe.wait_ge(kv_ev, 2 * hh - 2)
                tile_wait(t)
                for e in range(2):
                    for k in range(4):
                        last = pe.matmul(bank(4 + (2 * hh + e) % 4), tile(t)[:, e * 512 + k * P:e * 512 + (k + 1) * P],
                                         C[:, k * S:(k + 1) * S], start=(k == 0), stop=(k == 3))
                last.then_inc(w_used, 1)
                t += 1
            pe.wait_ge(rms_done, 2)
            pe.wait_ge(kr_done, 1)
            for half in range(2):
                if half:
                    pe.wait_ge(kv_ev, 12)
                for j in range(2):
                    tile_wait(t)
                    for b in range(NB):
                        for k in range(2):
                            kt = 2 * j + k
                            last = pe.matmul(bank(b), C[:, kt * S + b * P:kt * S + (b + 1) * P],
                                             tile(t)[:, k * 512:(k + 1) * 512], start=(kt == 0), stop=(kt == 3))
                    last.then_inc(w_used, 1)
                    t += 1
            pe.wait_ge(kv_ev, 16)
            with pe.Fori(0, HEADS // 2) as hp:
                pe.wait_ge(wq_full, hp * 16 + 16)
                pe.wait_ge(qr_done, hp + 1)
                pe.wait_ge(o_ev, hp * 2 + 2)
                for part, done in ((2, None), (3, qpe_mm), (0, qn_mm), (1, qn_mm)):
                    for k in range(4):
                        last = pe.matmul(bank(part), WQ[:, part * 512 + k * P:part * 512 + (k + 1) * P],
                                         C[:, (4 + k) * S:(5 + k) * S], start=(k == 0), stop=(k == 3))
                    if done is not None:
                        last.then_inc(done, 1)

                def scores(n):
                    e, qb = n // 4, n % 4
                    pe.wait_ge(exp_done, hp * 8 + (n + 1))
                    if n == 0:
                        pe.wait_ge(qr_done, hp + 2)
                        pe.wait_ge(qn_ev, hp * 2 + 1)
                    if n == 4:
                        pe.wait_ge(qn_ev, hp * 2 + 2)
                    pe.matmul(bank(4 + n % 2), QN[e][:, qb * P:(qb + 1) * P], KN[:, bass.ds(hp * 1024 + e * S, S)],
                              start=True, stop=False)
                    pe.matmul(bank(4 + n % 2), QR[e * 64:(e + 1) * 64, qb * P:(qb + 1) * P],
                              KR[e * 64:(e + 1) * 64, :], start=False, stop=True).then_inc(s_mm, 1)

                def turn(n):
                    pe.wait_ge(p_done, hp * 8 + (n + 1))
                    pe.wait_ge(pt_ev, hp * 8 + (n + 1))
                    for k in range(4):
                        last = pe.transpose(ps[:, 6 + n % 2, k * P:(k + 1) * P], PM[n % 2][:, k * P:(k + 1) * P], IDENT)
                    last.then_inc(t_mm, 1)

                def values(e):
                    pe.wait_ge(pt_ev, hp * 8 + (4 * e + 6))
                    pe.wait_ge(vh_done, hp * 2 + (e + 1))
                    for k in range(4):
                        last = pe.matmul(bank(e), VH[e][:, k * P:(k + 1) * P], PT[:, k * S:(k + 1) * S],
                                         start=(k == 0), stop=(k == 3))
                    last.then_inc(pv_mm, 1)

                pe.wait_ge(qn_ev, hp * 2 + 2)
                scores(0)
                for n in range(1, 8):
                    scores(n)
                    turn(n - 1)
                    if n == 4:
                        values(0)
                turn(7)
                values(1)
            squares(8, 8, 2)
            squares(16, 8, 3)
            pe.wait_ge(rms_done, 4)
            pe.wait_ge(o_ev, HEADS + 2)
            with pe.Fori(0, 2) as i:
                for cc in range(2):
                    pe.wait_ge(o_added, i * 8 + (4 * cc + 4))
                    for j in range(8):
                        tile_wait(t + 8 * cc + j, i * 4)
                        for b in range(NB):
                            for k in range(2):
                                kt = 2 * j + k
                                last = pe.matmul(bank(4 * cc + b), Y[:, kt * S + b * P:kt * S + (b + 1) * P],
                                                 tile(t + 8 * cc + j)[:, k * 512:(k + 1) * 512],
                                                 start=(kt == 0), stop=(kt == KT - 1))
                        last.then_inc(w_used, 1)
            t += 32
            assert t == N_ONCE

            with pe.Fori(0, NB) as b:
                def did(ins, name):
                    ins.then_inc(e_mm, 1)
                    order.append(name)

                def seen(name):
                    pe.wait_ge(e_ev, b * len(ACT_STEPS) + ACT_AT[name])

                def told(name):
                    pe.wait_ge(e_dv, b * len(DVE_STEPS) + DVE_AT[name])

                order = []
                tt = [N_ONCE]

                def wtile():
                    tile_wait(tt[0], b * (N_BLOCK // NW))
                    return tile(tt[0])

                def used(ins):
                    ins.then_inc(w_used, 1)
                    tt[0] += 1

                def turned(src, q, name):
                    for k in range(4):
                        kt = 4 * q + k
                        last = pe.transpose(ps[:, 4 + q, k * P:(k + 1) * P], src[:, kt * P:(kt + 1) * P], IDENT)
                    did(last, name)

                seen("xs")
                pe.wait_ge(o_added, 24)
                for q in QUAD:
                    turned(XS, q, f"x1T{q}")
                seen("x1T3")
                for name in PE_ORDER[4:]:
                    if name in ("q", "pq0", "pq1", "pq2", "pq3"):
                        if name == "pq0":
                            seen("x2T3")
                        if name == "pq2":
                            seen("pq0")
                        if name == "pq3":
                            seen("pq1")
                        to = 4 if name == "q" else 4 + int(name[2]) % 2
                        for j in range(8):
                            w = wtile()
                            for k in range(2):
                                kt = 2 * j + k
                                last = pe.matmul(bank(to), XT[:, kt * P:(kt + 1) * P], w[:, k * 512:(k + 1) * 512],
                                                 start=(kt == 0), stop=(kt == KT - 1))
                            used(last)
                    elif name == "qT" or name[:3] == "pqT":
                        c = 0 if name == "qT" else int(name[3])
                        seen("q" if name == "qT" else f"pq{c}")
                        if c:
                            seen(f"pqT{c - 1}")
                        for k in range(4):
                            last = pe.transpose(ps[:, 5 if name == "qT" else 6, k * P:(k + 1) * P],
                                                QB[c % 2][:, k * P:(k + 1) * P], IDENT)
                        did(last, name)
                    elif name == "sc":
                        seen("qT")
                        for h in range(MH):
                            last = pe.matmul(ps[:, 6 + h // 2, (h % 2) * MEM:(h % 2 + 1) * MEM],
                                             QT[:, h * P:(h + 1) * P], KM[:, h * MEM:(h + 1) * MEM],
                                             start=True, stop=True)
                        did(last, name)
                    elif name == "pT":
                        told("prob")
                        for n in range(8):
                            last = pe.transpose(ps[:, 4 + n // 4, (n % 4) * P:(n % 4 + 1) * P],
                                                PR[:, n * P:(n + 1) * P], IDENT)
                        did(last, name)
                    elif name == "pv":
                        seen("pT")
                        for h in range(MH):
                            for m in range(2):
                                last = pe.matmul(ps[:, 6, h * P:(h + 1) * P],
                                                 VM[:, m * 512 + h * P:m * 512 + (h + 1) * P],
                                                 PRT[:, (2 * h + m) * P:(2 * h + m + 1) * P],
                                                 start=(m == 0), stop=(m == 1))
                        did(last, name)
                    elif name[:2] == "wo":
                        c = int(name[2])
                        if c == 0:
                            seen("pv")
                        for j in range(2):
                            w = wtile()
                            for k in range(2):
                                kt = 2 * j + k
                                last = pe.matmul(bank(4 + c), OT[:, kt * P:(kt + 1) * P], w[:, k * 512:(k + 1) * 512],
                                                 start=(kt == 0), stop=(kt == 3))
                            used(last)
                    elif name[:3] == "x2T":
                        q = int(name[3])
                        if q == 0:
                            told("x2")
                        turned(XC, q, name)
                    elif name[:3] == "key":
                        c = int(name[3])
                        seen(f"pqT{c}")
                        if c:
                            seen(f"key{c - 1}")
                        for k in range(4):
                            last = pe.matmul(ps[:, 7, k * P:(k + 1) * P], QT[:, k * P:(k + 1) * P],
                                             KEYS[:, (k % 2) * NK:(k % 2 + 1) * NK], start=True, stop=True)
                        did(last, name)
                assert order == PE_STEPS and tt[0] == N_ONCE + N_BLOCK
                pe.wait_ge(y_ready, b + 1)
                for q in QUAD:
                    pe.matmul(bank(q), ALPHA_I, XC[:, q * 512:(q + 1) * 512], start=True, stop=False)

                def add_rows(j, par, last_group=False):
                    for s in range(4):
                        pe.wait_ge(diag_done, b * HK + (j * 4 + (s + 1)))
                        pe.wait_ge(v_full[s], b * (32 * 16) + (j * 16 + 16))
                        for q in QUAD:
                            last = pe.matmul(bank(q), DIAG[par][:, s * P:(s + 1) * P],
                                             V_RING[:, s * D + q * 512:s * D + (q + 1) * 512],
                                             start=False, stop=(last_group and s == 3))
                        last.then_inc(v_free, 1)

                with pe.Fori(0, 15) as jj:
                    for par in range(2):
                        add_rows(jj * 2 + par, par)
                add_rows(30, 0)
                add_rows(31, 1, last_group=True)

        @block.scalar
        def _(act):
            def tick():
                act.sem_inc(act_tick, 1)

            def evict(dst, src):
                return act.activation(dst, src, ACT.Copy)

            act.sem_inc(xbank_free, 2)
            act.sem_inc(gbank_free, 2)
            act.sem_inc(rbank_free, 1)
            act.sem_inc(exp_done, 2)
            act.sem_inc(pt_ev, 2)
            act.sem_inc(o_ev, 2)
            act.wait_ge(lam_abs, 1)
            act.activation(LM[1], LM[0], ACT.Exp, scale=-1.0).then_inc(lam_exp, 1)
            act.wait_ge(angle, 1)
            act.activation(SINS, RS, ACT.Sin, scale=col(C_SIGN))
            act.activation(COS, COS, ACT.Sin).then_inc(rope_tab, 1)
            for h in range(MH):
                act.wait_ge(w_used, 2 * (h + 1))
                evict(KM[:, h * MEM:(h + 1) * MEM], bank(h, MEM)).then_inc(mem_ev, 1)
            act.wait_ge(w_used, 16)
            for m in range(2):
                evict(VM[:, m * 512:(m + 1) * 512], bank(4 + m)).then_inc(mem_ev, 1)
            for n in range(4 * NB):
                b, q = n // 4, n % 4
                act.wait_ge(x0T_mm, n + 1)
                evict(A.rearrange("p (k s) -> p k s", k=KT)[:, 4 * q:4 * q + 4, b * P:(b + 1) * P],
                      bank(6 + n % 2).rearrange("p (k s) -> p k s", k=4)).then_inc(x0T_ev, 1)
            act.wait_ge(consts_set, 6)
            with act.Fori(0, NL // 2) as i:
                for e in range(2):
                    act.wait_ge(w_used, i * 8 + (16 + 2 * e + 2))
                    act.wait_ge(conv_done, i * 2 + (e + 1))
                    evict(LX[e][:, 2:2 + S], bank(e)).then_inc(xbank_free, 1)
                for e in range(2):
                    act.wait_ge(w_used, i * 8 + (20 + 2 * e + 2))
                    tick()
                    act.activation(Y[:, bass.ds(i * 1024 + (8 + e) * S, S)], bank(2 + e), ACT.Gelu
                                   ).then_inc(gbank_free, 1)
                    act.wait_ge(r_mm, i * 2 + (e + 1))
                    act.wait_ge(lru_done, i * 2 + (e + 1))
                    tick()
                    for q in range(4):
                        dst = (R_ + I_)[q]
                        first = C_BA if q < 2 else C_BX
                        last = act.activation(dst, bank(4 + q), ACT.Sigmoid,
                                              bias=COLS[:, bass.ds(i * 2 + (first + (q % 2) * NL + e), 1)])
                    last.then_inc(rbank_free, 1)
                    act.wait_ge(rbank_free, i * 2 + (e + 2))
                    tick()
                    for d in range(2):
                        last = act.activation(R_[d], R_[d], ACT.Tanh, scale=C4[:, bass.ds(i * 2 + (d * NL + e), 1)])
                    last.then_inc(tanh_done, 1)
                    act.wait_ge(tanh_done, i * 2 + (e + 1))
                    for d in range(2):
                        last = act.activation(H_[d], R_[d], ACT.Sqrt)
                    last.then_inc(u_ready, 1)
            with act.Fori(0, 2) as i:
                for j in range(4):
                    act.wait_ge(w_used, i * 8 + (48 + 2 * j + 2))
                    tick()
                    evict(C[:, bass.ds(i * 2048 + j * S, S)], ps[:, bass.ds(i * 4 + j, 1), :].rearrange("p a n -> p (a n)")
                          ).then_inc(l2_ev, 1)

            def squares(first, count, src):
                for r in range(first, first + count):
                    if r >= 2:
                        act.wait_ge(rms_mm, r - 1)
                    act.activation(SQ[r % 2], src[:, (r - first) * S:(r - first + 1) * S], ACT.Square
                                   ).then_inc(rms_sq, 1)

            act.wait_ge(l2_ev, 8)
            squares(0, 4, C)
            squares(4, 4, C[:, 4 * S:8 * S])
            for hh in range(HEADS // 2):
                act.wait_ge(w_used, 68 + hh + 1)
                for h in (2 * hh, 2 * hh + 1):
                    evict(KN[:, h * S:(h + 1) * S], bank(4 + h % 4)).then_inc(kv_ev, 1)
            for half in range(2):
                act.wait_ge(w_used, 72 + 2 * half + 2)
                for b in range(NB):
                    evict(V[:, b * 1024 + half * 512:b * 1024 + (half + 1) * 512], bank(b)).then_inc(kv_ev, 1)
            act.wait_ge(lru_done, NL + 1)
            with act.Fori(0, HEADS // 2) as hp:
                for e in range(2):
                    act.wait_ge(qn_mm, hp * 2 + (e + 1))
                    evict(QN[e], bank(e)).then_inc(qn_ev, 1)

                def exp(n):
                    act.wait_ge(nmx_done, hp * 8 + (n + 1))
                    act.wait_ge(t_mm, hp * 8 + (n + 1))
                    act.activation(PM[n % 2], bank(4 + n % 2), ACT.Exp, bias=NM2[n % 2], scale=ATT_SCALE,
                                   accum_out=RSM2[n % 2]).then_inc(exp_done, 1)

                def turned(n):
                    act.wait_ge(t_mm, hp * 8 + (n + 3))
                    if n % 4 == 0:
                        act.wait_ge(pv_mm, hp * 2 + (n // 4 + 2))
                    qb = n % 4
                    evict(PT.rearrange("p (k s) -> p k s", k=4)[:, :, qb * P:(qb + 1) * P],
                          bank(6 + n % 2).rearrange("p (k s) -> p k s", k=4)).then_inc(pt_ev, 1)

                def output(e):
                    act.wait_ge(pv_mm, hp * 2 + (e + 3))
                    tick()
                    evict(Y[:, bass.ds(hp * 1024 + e * S, S)], bank(e)).then_inc(o_ev, 1)

                exp(0)
                for n in range(1, 8):
                    exp(n)
                    if n == 5:
                        output(0)
                    turned(n - 1)
                turned(7)
                output(1)
            act.wait_ge(o_ev, HEADS + 2)
            squares(8, 8, Y)
            squares(16, 8, Y[:, 8 * S:16 * S])
            act.wait_ge(ln1_done, NB)

            with act.Fori(0, NB) as b:
                def product(name):
                    if name in TILES_AT:
                        act.wait_ge(w_used, b * N_BLOCK + (N_ONCE + TILES_AT[name]))
                    else:
                        act.wait_ge(e_mm, b * len(PE_STEPS) + PE_AT[name])

                for name in ACT_STEPS:
                    if name == "xs":
                        last = evict(XS, X[:, bass.ds(b * D, D)])
                    elif name[:3] in ("x1T", "x2T"):
                        q = int(name[3])
                        product(name)
                        last = evict(XT[:, q * 512:(q + 1) * 512], bank(4 + q))
                    elif name in ("q", "pq0", "pq1", "pq2", "pq3"):
                        product(name)
                        c = 0 if name == "q" else int(name[2]) % 2
                        last = evict(QB[c], bank(4 + c))
                    elif name == "qT":
                        product(name)
                        last = evict(QT, bank(5))
                    elif name[:3] == "pqT":
                        product(name)
                        last = evict(QT, bank(6))
                    elif name == "exp":
                        act.wait_ge(e_dv, b * len(DVE_STEPS) + DVE_AT["max"])
                        for h in range(MH):
                            last = act.activation(PR[:, h * MEM:(h + 1) * MEM],
                                                  ps[:, 6 + h // 2, (h % 2) * MEM:(h % 2 + 1) * MEM], ACT.Exp,
                                                  bias=NMX[:, h:h + 1], scale=MEM_SCALE, accum_out=RSUM[:, h:h + 1])
                    elif name == "pT":
                        product(name)
                        last = evict(PRT, ps[:, 4:6, :].rearrange("p a n -> p (a n)"))
                    elif name == "pv":
                        product(name)
                        last = evict(OT, bank(6))
                    elif name[:3] == "key":
                        product(name)
                        c = int(name[3])
                        last = evict(SK[:, c * 512:(c + 1) * 512], bank(7))
                    elif name == "gate":
                        act.wait_ge(e_dv, b * len(DVE_STEPS) + DVE_AT["top"])
                        last = act.activation(GATE, GATE, ACT.Exp)
                    last.then_inc(e_ev, 1)
                with act.Fori(0, 16) as jj:
                    for par in range(2):
                        j = jj * 2 + par
                        act.wait_ge(u_free, b * HK + (j * 4 + 8))
                        act.activation(GEL[par], DOT[par], ACT.Gelu).then_inc(gel_done, 1)
                        act.wait_ge(act_done, b * 32 + (j + 1))
                        act.wait_ge(v_free, b * HK + (j * 4 + 4))
                        tick()
                        for s in range(4):
                            act.activation(DIAG[par][:, s * P:(s + 1) * P], IDENT, ACT.Copy,
                                           scale=AV[par][:, s:s + 1]).then_inc(diag_done, 1)

        @block.vector
        def _(dve):
            link = InOrder(dve, dve_done)

            def tick():
                dve.sem_inc(dve_tick, 1)

            def rsqrt(y, v, t):
                link(dve.tensor_scalar(y.bitcast(I32), v.bitcast(I32), 1, None, ALU.logical_shift_right))
                link(dve.tensor_scalar(y.bitcast(I32), y.bitcast(I32), -1.0, float(0x5f3759df), ALU.mult, ALU.add))
                for _ in range(3):
                    link(dve.tensor_tensor(t, y, y, ALU.mult))
                    link(dve.tensor_tensor(t, t, v, ALU.mult))
                    link(dve.tensor_scalar(t, t, -0.5, 1.5, ALU.mult, ALU.add))
                    link(dve.tensor_tensor(y, y, t, ALU.mult))

            def norm(src, dst, gain, bias, hold=None):
                for k in range(4):
                    last = dve.bn_stats(STATS[:, 6 * k:6 * k + 6], src[:, k * 512:(k + 1) * 512])
                link(last, hold)
                link(dve.bn_aggr(MV, STATS))
                link(dve.tensor_scalar(MV[:, 1:2], MV[:, 1:2], LN_EPS, None, ALU.add))
                rsqrt(RSTD, MV[:, 1:2], NEWTON)
                link(dve.tensor_scalar(dst, src, MV[:, 0:1], RSTD, ALU.subtract, ALU.mult))
                link(dve.tensor_tensor(dst, dst, gain, ALU.mult))
                return dve.tensor_tensor(dst, dst, bias, ALU.add)

            dve.sem_inc(conv_done, 2)
            dve.sem_inc(lru_done, 1)
            dve.sem_inc(qr_done, 1)
            dve.sem_inc(o_added, 8)
            dve.sem_inc(y_ready, 1)
            dve.sem_inc(u_free, 4)
            lam = COLS[:, C_LAM:C_LAM + 16]
            dve.wait_ge(cols_in, 16)
            dve.scalar_tensor_tensor(out=LM[0], in0=lam, scalar=-1.0, in1=lam, op0=ALU.mult, op1=ALU.max
                                     ).then_inc(lam_abs, 1)
            link(dve.tensor_scalar(LM[2], lam, -4.0, 0.0, ALU.mult, ALU.max))
            dve.wait_ge(lam_exp, 1)
            link(dve.tensor_scalar(LM[3], LM[1], 2.0, None, ALU.add))
            link(dve.reciprocal(LM[4], LM[3]))
            link(dve.tensor_tensor(LM[3], LM[1], LM[4], ALU.mult))
            link(dve.tensor_tensor(LM[4], LM[3], LM[3], ALU.mult))
            link(dve.tensor_scalar(LM[5], LM[4], 1.0 / 15, None, ALU.mult))
            for odd in (13, 11, 9, 7, 5, 3):
                link(dve.scalar_tensor_tensor(out=LM[5], in0=LM[5], scalar=1.0 / odd, in1=LM[4],
                                              op0=ALU.add, op1=ALU.mult))
            link(dve.scalar_tensor_tensor(out=LM[5], in0=LM[5], scalar=1.0, in1=LM[3], op0=ALU.add, op1=ALU.mult))
            link(dve.scalar_tensor_tensor(out=C4, in0=LM[5], scalar=8.0, in1=LM[2], op0=ALU.mult, op1=ALU.add))
            dve.wait_ge(pos_in, 16)
            link(dve.tensor_copy(RS, TMP.bitcast(I32)))
            link(dve.tensor_scalar(RS, RS, col(C_FREQ), None, ALU.mult))
            link(dve.tensor_scalar(COS, RS, 1.0 / (2 * math.pi), ROUND, ALU.mult, ALU.add))
            link(dve.tensor_scalar(COS, COS, ROUND, None, ALU.subtract))
            for part in (TWO_PI_A, TWO_PI_B, TWO_PI_C):
                link(dve.scalar_tensor_tensor(out=RS, in0=COS, scalar=-part, in1=RS, op0=ALU.mult, op1=ALU.add))
            link(dve.tensor_scalar(RS, RS, 3.1415925, -3.1415925, ALU.min, ALU.max))
            link(dve.scalar_tensor_tensor(out=COS, in0=RS, scalar=-1.0, in1=RS, op0=ALU.mult, op1=ALU.max))
            dve.tensor_scalar(COS, COS, -1.0, math.pi / 2, ALU.mult, ALU.add).then_inc(angle, 1)
            dve.wait_ge(gain0_in, 32)
            for b in range(NB):
                dve.wait_ge(x_in[b], 16)
                xb = X[:, b * D:(b + 1) * D]
                norm(xb, xb, GAIN_G, GAIN_B).then_inc(ln0_done, 1)

            dve.wait_ge(consts_set, 6)
            with dve.Fori(0, NL // 2) as i:
                link.enter(i, 18)
                for e in range(2):
                    dve.wait_ge(xbank_free, i * 2 + (e + 3))

                    def cw(k):
                        return COLS[:, bass.ds(i * 2 + (C_CONVW + k * NL + e), 1)]

                    link(dve.tensor_scalar(XC1[e], LX[e][:, 0:S], cw(0), COLS[:, bass.ds(i * 2 + (C_CONVB + e), 1)],
                                           ALU.mult, ALU.add))
                    for k in range(1, 4):
                        last = dve.scalar_tensor_tensor(out=XC1[e], in0=LX[e][:, k:k + S], scalar=cw(k), in1=XC1[e],
                                                        op0=ALU.mult, op1=ALU.add)
                        if k < 3:
                            link(last)
                    last.then_inc(conv_done, 1)
                for e in range(2):
                    dve.wait_ge(u_ready, i * 2 + (e + 1))
                    dve.wait_ge(conv_done, i * 2 + 4)
                    for d in range(2):
                        dve.tensor_tensor(I_[d], I_[d], XC1[e], ALU.mult)
                        last = dve.tensor_scalar(D_[d], R_[d], 1.0, None, ALU.add)
                    link(last)
                    for d in range(2):
                        dve.scalar_tensor_tensor(out=I_[d], in0=I_[d], scalar=2.0, in1=H_[d], op0=ALU.mult, op1=ALU.mult)
                        last = dve.reciprocal(D_[d], D_[d])
                    link(last)
                    for d in range(2):
                        last = dve.tensor_tensor(I_[d], I_[d], D_[d], ALU.mult)
                    link(last)
                    for d in range(2):
                        last = dve.tensor_scalar(D_[d], D_[d], 2.0, -1.0, ALU.mult, ALU.add)
                    link(last)
                    dve.tensor_tensor_scan(H_[0], D_[0], I_[0], 0.0, ALU.mult, ALU.add)
                    link(dve.tensor_tensor_scan(H_[1][:, ::-1], D_[1][:, ::-1], I_[1][:, ::-1], 0.0, ALU.mult, ALU.add))
                    link(dve.tensor_tensor(H_[0], H_[0], H_[1], ALU.add))
                    dve.wait_ge(gbank_free, i * 2 + (e + 3))
                    gate = Y[:, bass.ds(i * 1024 + (8 + e) * S, S)]
                    dve.tensor_tensor(gate, gate, H_[0], ALU.mult).then_inc(lru_done, 1)
                link.leave(NL // 2)

            def rms(units, b, count, gains_at, region):
                dve.wait_ge(rms_mm, units)
                link(dve.tensor_scalar(TMP2, bank(b), 1.0 / (count * P), RMS_EPS, ALU.mult, ALU.add))
                rsqrt(RS, TMP2, TMP)
                for k in range(count):
                    r = region[:, k * S:(k + 1) * S]
                    last = dve.scalar_tensor_tensor(out=r, in0=r, scalar=col(gains_at + k), in1=RS,
                                                    op0=ALU.mult, op1=ALU.mult)
                last.then_inc(rms_done, 1)

            dve.wait_ge(rope_tab, 1)
            rms(4, 2, 4, C_KVG, C)
            rms(8, 3, 4, C_QG, C[:, 4 * S:8 * S])
            dve.wait_ge(w_used, 68)
            dve.tensor_tensor(KR, bank(0), COS, ALU.mult)
            link(dve.tensor_tensor(TMP, bank(1), SINS, ALU.mult))
            dve.tensor_tensor(KR, KR, TMP, ALU.add).then_inc(kr_done, 1)
            with dve.Fori(0, HEADS // 2) as hp:
                link.enter(hp, 1 + 8 * 2)
                dve.wait_ge(qpe_mm, hp + 1)
                dve.tensor_tensor(QR, bank(2), COS, ALU.mult)
                link(dve.tensor_tensor(TMP, bank(3), SINS, ALU.mult))
                dve.tensor_tensor(QR, QR, TMP, ALU.add).then_inc(qr_done, 1)

                def row_max(n):
                    dve.wait_ge(s_mm, hp * 8 + (n + 1))
                    link(dve.tensor_reduce(MX2[n % 2], bank(4 + n % 2), AX, ALU.max))
                    dve.tensor_scalar(NM2[n % 2], MX2[n % 2], -ATT_SCALE, None, ALU.mult).then_inc(nmx_done, 1)

                row_max(0)
                for n in range(8):
                    if n < 7:
                        row_max(n + 1)
                    dve.wait_ge(exp_done, hp * 8 + (n + 3))
                    link(dve.reciprocal(RI2[n % 2], RSM2[n % 2]))
                    dve.tensor_scalar(PM[n % 2], PM[n % 2], RI2[n % 2], None, ALU.mult).then_inc(p_done, 1)
                link.leave(HEADS // 2)
            rms(16, 2, 8, C_AG, Y)
            rms(24, 3, 8, C_LG, Y[:, 8 * S:16 * S])
            with dve.Fori(0, 2) as i:
                for cc in range(2):
                    dve.wait_ge(w_used, i * 16 + (76 + 8 * cc + 8))
                    for b in range(NB):
                        xs = X[:, bass.ds(i * 1024 + (b * D + cc * 512), 512)]
                        dve.scalar_tensor_tensor(out=xs, in0=xs, scalar=ALPHA, in1=bank(4 * cc + b),
                                                 op0=ALU.mult, op1=ALU.add).then_inc(o_added, 1)
            dve.wait_ge(o_added, 24)
            dve.wait_ge(gain1_in, 32)
            for b in range(NB):
                xb = X[:, b * D:(b + 1) * D]
                norm(xb, xb, GAIN_G, GAIN_B).then_inc(ln1_done, 1)
            dve.wait_ge(gain2_in, 32)
            dve.wait_ge(gain3_in, 32)

            with dve.Fori(0, NB) as b:
                link.enter(b, 62)

                def evicted(name):
                    dve.wait_ge(e_ev, b * len(ACT_STEPS) + ACT_AT[name])

                dve.wait_ge(e_mm, b * len(PE_STEPS) + PE_AT["sc"])
                link(dve.tensor_reduce(MX, ps[:, 6:8, :].rearrange("p a (c m) -> p (a c) m", m=MEM), AX, ALU.max))
                dve.tensor_scalar(NMX, MX, -MEM_SCALE, None, ALU.mult).then_inc(e_dv, 1)
                evicted("exp")
                link(dve.reciprocal(RINV, RSUM))
                pr = PR.rearrange("p (h m) -> p h m", h=MH)
                dve.tensor_tensor(pr, pr, RINV.unsqueeze(2).broadcast_to([P, MH, MEM]), ALU.mult).then_inc(e_dv, 1)
                for c in QUAD:
                    dve.wait_ge(w_used, b * N_BLOCK + (N_ONCE + TILES_AT[f"wo{c}"]))
                    xs = XS[:, c * 512:(c + 1) * 512]
                    dve.scalar_tensor_tensor(out=xs, in0=xs, scalar=ALPHA, in1=bank(4 + c),
                                             op0=ALU.mult, op1=ALU.add).then_inc(e_dv, 1)
                dve.wait_ge(e_dv, b * len(DVE_STEPS) + DVE_AT["wo3"])
                dve.wait_ge(xc_free, b + 1)
                norm(XS, XC, GAIN_G, GAIN_B, dve_tick).then_inc(e_dv, 1)

                def top16(src, width, vals, idxs, count):
                    for half in range(2):
                        def at(t, n):
                            return t[:, n * TOPK + half * 8:n * TOPK + half * 8 + 8]
                        for n in range(count):
                            last = dve.max(at(vals, n), src[:, n * width:(n + 1) * width])
                        link(last, dve_tick)
                        for n in range(count):
                            last = dve.max_index(at(idxs, n), at(vals, n), src[:, n * width:(n + 1) * width])
                        link(last, dve_tick)
                        if half == 0:
                            for n in range(count):
                                w = src[:, n * width:(n + 1) * width]
                                last = dve.match_replace(w, at(vals, n), w, -3.0e38)
                            link(last, dve_tick)

                evicted("key3")
                tick()
                top16(SK, NK, TV, TI, HALVES)
                tv = TV.rearrange("p (h t k) -> p h t k", t=2, k=TOPK)
                shape = [P, PH, TOPK, TOPK]

                def four(t):
                    return t.rearrange("p (h k a) -> p h k a", h=PH, k=TOPK)

                link(dve.tensor_tensor(four(CAND), tv[:, :, 0, :].unsqueeze(3).broadcast_to(shape),
                                       tv[:, :, 1, :].unsqueeze(2).broadcast_to(shape), ALU.add), dve_tick)
                top16(CAND, TOPK * TOPK, CV, CP, PH)
                cv = CV.rearrange("p (h k) -> p h k", k=TOPK)
                gate = GATE.rearrange("p (h k) -> p h k", k=TOPK)
                dve.tensor_tensor(gate, cv, cv[:, :, 0:1].broadcast_to([P, PH, TOPK]), ALU.subtract).then_inc(e_dv, 1)
                dve.tensor_scalar(CA, CP, 4, None, ALU.logical_shift_right)
                dve.tensor_scalar(CB, CP, 15, None, ALU.bitwise_and)
                link(dve.tensor_copy(TIF, TI))
                dve.tensor_copy(CAF, CA)
                link(dve.tensor_copy(CBF, CB))
                tif = TIF.rearrange("p (h t k) -> p h t k", t=2, k=TOPK)
                iota = IOTA.unsqueeze(1).unsqueeze(1).broadcast_to(shape)
                for half, place_f, number in ((0, CAF, S1), (1, CBF, S2)):
                    link(dve.tensor_tensor(four(EQ), place_f.rearrange("p (h k) -> p h k", k=TOPK).unsqueeze(3)
                                           .broadcast_to(shape), iota, ALU.is_equal))
                    link(dve.tensor_tensor(four(EQ), four(EQ), tif[:, :, half, :].unsqueeze(2).broadcast_to(shape),
                                           ALU.mult))
                    link(dve.tensor_reduce(number, EQ.rearrange("p (n a) -> p n a", a=TOPK), AX, ALU.add))
                dve.scalar_tensor_tensor(out=IDX, in0=S1, scalar=float(NK), in1=S2, op0=ALU.mult, op1=ALU.add
                                         ).then_inc(e_dv, 1)
                evicted("gate")
                link(dve.tensor_reduce(GS, gate, AX, ALU.add))
                link(dve.reciprocal(GR, GS))
                link(dve.tensor_tensor(gate, gate, GR.unsqueeze(2).broadcast_to([P, PH, TOPK]), ALU.mult))

                def dot(j, par, s):
                    dve.wait_ge(u_full[s], b * (32 * 16) + (j * 16 + 16))
                    row = U_RING[:, s * D:(s + 1) * D]
                    dve.tensor_tensor_reduce(row, row, XC, 1.0, 0.0, ALU.mult, ALU.add,
                                             DOT[par][:, s:s + 1]).then_inc(u_free, 1)

                def weigh(j, par):
                    dve.wait_ge(gel_done, b * 32 + (j + 1))
                    dve.tensor_tensor(AV[par], GEL[par], GATE[:, bass.ds(j * 4, 4)], ALU.mult).then_inc(act_done, 1)

                def group(j, par):
                    dot(j, par, 0)
                    weigh(j - 1, 1 - par)
                    for s in range(1, 4):
                        dot(j, par, s)

                for s in range(4):
                    dot(0, 0, s)
                with dve.Fori(0, 15) as jj:
                    group(jj * 2 + 1, 1)
                    group(jj * 2 + 2, 0)
                group(31, 1)
                weigh(31, 1)
                dve.wait_ge(v_free, b * HK + (HK + 8))
                norm(ps[:, 0:4, :].rearrange("p a n -> p (a n)"), XC, G3G, G3B, dve_tick).then_inc(y_ready, 1)
                link.leave(NB)


def kernel(**a):
    import concourse.bacc as bacc
    from concourse.bass_utils import run_bass_kernel_spmd as run

    def f(name):
        return np.asarray(a[name])

    def tiles(w):
        k, n = w.shape[0] // P, w.shape[1]
        t = w.reshape(k, P, n).transpose(1, 0, 2).reshape(P, k * n)
        return t.reshape(P, -1, TW).transpose(1, 0, 2)

    def columns(v):
        return v.reshape(-1, P).T

    w_in, w_uq, w_ukv, w_out = f("w_in")[0], f("w_uq")[0], f("w_ukv")[0], f("w_out")[0]
    kpe = w_in[:, CKV:KPE]
    swap = np.concatenate([kpe[:, ROPE // 2:], kpe[:, :ROPE // 2]], 1)
    once = [tiles(f("w_mk")[0][:, h * P:(h + 1) * P]) for h in range(MH)] + [tiles(f("w_mv")[0])]
    for n in range(0, NL, 2):
        for first in (KPE, LRUX):
            for m in (n, n + 1):
                once.append(tiles(w_in[:, first + m * P:first + (m + 1) * P]))
    for first in (CQ, 0):
        for j in range(4):
            once.append(tiles(w_in[:, first + j * P:first + (j + 1) * P]))
    once += [tiles(np.concatenate([kpe, kpe], 1)), tiles(np.concatenate([swap, swap], 1))]
    ukv = w_ukv.reshape(LORA, HEADS, 2 * P)
    for h in range(0, HEADS, 2):
        once.append(np.concatenate([ukv[:, h + e, :P].reshape(4, P, P).transpose(1, 0, 2).reshape(1, P, 512)
                                    for e in range(2)], 2))
    v_cols = ukv[:, :, P:].reshape(LORA, HEADS * P)
    once += [tiles(v_cols[:, half * 512:(half + 1) * 512]) for half in range(2)]
    once += [tiles(w_out[:, c * 512:(c + 1) * 512]) for c in range(4)]
    w_once = np.concatenate(once, 0)
    w_mo, w_pq = f("w_mo")[0], f("w_pq")[0]
    w_block = np.concatenate([tiles(f("w_mq")[0])] + [tiles(w_mo[:, c * 512:(c + 1) * 512]) for c in range(4)]
                             + [tiles(w_pq[:, c * 512:(c + 1) * 512]) for c in range(4)], 0)
    uq = w_uq.reshape(4, P, HEADS, NOPE + ROPE).transpose(1, 2, 0, 3)
    pairs = []
    for h in range(0, HEADS, 2):
        half = ROPE // 2
        pe = np.concatenate([uq[:, h, :, NOPE:], uq[:, h + 1, :, NOPE:]], 2)
        sw = np.concatenate([uq[:, h + e, :, NOPE + o:NOPE + o + half] for e in range(2) for o in (half, 0)], 2)
        pairs.append(np.stack([uq[:, h, :, :NOPE], uq[:, h + 1, :, :NOPE], pe, sw], 1).reshape(P, 2048))
    wa, wx = f("lru_wa")[0], f("lru_wx")[0]
    lru_w = np.stack([wa[0], wa[1], wx[0], wx[1]], 1).transpose(0, 2, 1, 3).reshape(NL, P, 4 * P)
    part = np.arange(P) % ROPE
    freq = np.float32(10000.0) ** (-(np.arange(0, ROPE, 2, dtype=np.float32)) / np.float32(ROPE))
    consts = np.stack([freq[part % (ROPE // 2)], np.where(part < ROPE // 2, -1.0, 1.0)], 1).astype(np.float32)
    cols = np.concatenate([columns(f(n)[0]) for n in ("conv_w", "conv_b", "lru_ba", "lru_bx", "lru_lambda", "q_norm_g",
                                                      "kv_norm_g", "attn_out_g", "lru_out_g")] + [consts], 1)
    arrays = {
        "x": f("x")[0],
        "memT": f("mem")[0].T.reshape(KT, P, MEM).transpose(1, 0, 2).reshape(P, KT * MEM),
        "pos": f("positions")[0],
        "cols": cols, "w_once": w_once, "w_block": w_block, "wq_pairs": np.stack(pairs), "lru_w": lru_w,
        "keysT": np.concatenate([f("sub_keys1")[0].T, f("sub_keys2")[0].T], 1),
        "gains": np.stack([f("in_ln_g"), f("in_ln_b"), f("ln1_g")[0], f("ln1_b")[0], f("ln2_g")[0], f("ln2_b")[0],
                           f("ln3_g")[0], f("ln3_b")[0]]),
        "peer_u": f("peer_u")[0], "peer_v": f("peer_v")[0],
    }
    arrays = {k: np.ascontiguousarray(v) for k, v in arrays.items()}
    nc = bacc.Bacc("TRN2", target_bir_lowering=False, num_devices=1)
    args = [nc.dram_tensor(k, v.shape, mybir.dt.from_np(v.dtype), kind="ExternalInput").ap() for k, v in arrays.items()]
    out = nc.dram_tensor("y", (S, D), F32, kind="ExternalOutput").ap()
    build(nc, *args, out)
    r = run(nc, [arrays], core_ids=[0])
    return r.results[0]["y"].reshape(1, S, D)
```

```python
import math
from contextlib import ExitStack

import numpy as np

import concourse.bass as bass
from concourse import mybir

F32 = mybir.dt.float32
I32 = mybir.dt.int32
U32 = mybir.dt.uint32
ALU = mybir.AluOpType
ACT = mybir.ActivationFunctionType
AX = mybir.AxisListType.X

P = 128
D = 2048
S = 512
NB = S // P
KT = D // P
MEM = 256
MH = 4
HEADS = 8
NOPE = 128
ROPE = 64
LORA = 512
LW = 1024
NL = LW // P
PH = 8
NK = 128
TOPK = 16
HK = PH * TOPK
HALVES = 2 * PH
CQ, CKV, KPE, LRUX = 512, 1024, 1088, 2112
ALPHA = 2.0 ** 0.25
LN_EPS = 1e-5
RMS_EPS = 1e-6
ATT_SCALE = (NOPE + ROPE) ** -0.5
MEM_SCALE = 128.0 ** -0.5

TW = 1024
NW = 8
BANK = 512
ARENA = 53 * 1000

C_CONVW, C_CONVB, C_BA, C_BX, C_LAM, C_QG, C_KVG, C_AG, C_LG, C_FREQ, C_SIGN = 0, 32, 40, 56, 72, 88, 92, 96, 104, 112, 113
NCOL = 114

TWO_PI_A = 6.28125
TWO_PI_B = float(np.float32(round((2 * math.pi - TWO_PI_A) * 2 ** 20) / 2 ** 20))
TWO_PI_C = float(2 * math.pi - TWO_PI_A - TWO_PI_B)
ROUND = 12582912.0

QUAD = [0, 1, 2, 3]
PE_ORDER = ([f"x1T{q}" for q in QUAD] + ["q", "qT", "sc", "pT", "pv"] + [f"wo{c}" for c in QUAD]
            + [f"x2T{q}" for q in QUAD]
            + ["pq0", "pq1", "pqT0", "pq2", "key0", "pqT1", "pq3", "key1", "pqT2", "key2", "pqT3", "key3"])
TILES_AT = {"q": 8, "wo0": 10, "wo1": 12, "wo2": 14, "wo3": 16, "pq0": 24, "pq1": 32, "pq2": 40, "pq3": 48}
PE_STEPS = [n for n in PE_ORDER if n not in TILES_AT]
ACT_STEPS = (["xs"] + [f"x1T{q}" for q in QUAD] + ["q", "qT", "exp", "pT", "pv"] + [f"x2T{q}" for q in QUAD]
             + ["keep", "pq0", "pq1", "pqT0", "pq2", "key0", "pqT1", "pq3", "key1", "pqT2", "key2", "pqT3", "key3"])
DVE_STEPS = ["max", "prob"] + [f"wo{c}" for c in QUAD] + ["x2"]
PE_AT = {n: k + 1 for k, n in enumerate(PE_STEPS)}
ACT_AT = {n: k + 1 for k, n in enumerate(ACT_STEPS)}
DVE_AT = {n: k + 1 for k, n in enumerate(DVE_STEPS)}

DB = 2
DT = DB * P
ET = 4
GROUPS = P // ET
JG = (NB - DB) * HK // 4
JB = HK // 4
TG = 32


class InOrder:

    def __init__(self, eng, sem):
        self.eng, self.sem, self.base, self.k, self.outer = eng, sem, 0, 0, []

    def __call__(self, ins, tick=None):
        ins.then_inc(self.sem, 1)
        self.k += 1
        self.eng.wait_ge(self.sem, self.base + self.k)
        if tick is not None:
            self.eng.sem_inc(tick, 1)

    def enter(self, i, per):
        self.outer.append((self.base + self.k, per))
        self.base, self.k = self.base + self.k + i * per, 0

    def leave(self, count):
        start, per = self.outer.pop()
        assert self.k == per, (self.k, per)
        self.base, self.k = start + count * per, 0


def build(nc, x, memT, pos, cols_d, w_once, w_block, wq_pairs, lru_w, keysT, gains, peer_u, peer_v, peer_ut,
          gates_d, out):
    N_ONCE = w_once.shape[0]
    N_BLOCK = w_block.shape[0]
    DENSE0 = N_ONCE + NB * N_BLOCK
    with ExitStack() as ctx:
        def sem(name):
            return ctx.enter_context(nc.semaphore(name))

        base = nc.sbuf_base
        arena = ctx.enter_context(nc.sbuf_tensor("arena", [P, ARENA], F32))
        at0 = [0]

        def place(name, cols, at=None, dt=F32):
            at = at0[0] if at is None else at
            at0[0] = at + cols
            assert at + cols <= ARENA
            v = arena[:, at:at + cols]
            return v if dt == F32 else v.bitcast(dt)

        X = place("X", NB * D, 0)
        A = place("A", KT * S, 8192)
        KN, V = A[:, 0:4096], A[:, 4096:8192]
        XTA = A
        U_RING = A
        Y = place("Y", KT * S, 16384)
        MEMT = Y[:, 0:KT * MEM]
        V_RING = Y
        W = place("W", NW * TW, 24576)
        KM = place("KM", MH * MEM, 32768)
        VM = place("VM", 2 * 512, 33792)
        WD = [place(f"wd{e}", ET * DT, 32768 + e * ET * DT) for e in range(2)]
        C = place("C", 8 * S, 34816)
        GAIN_G, GAIN_B = C[:, 0:D], C[:, D:2 * D]
        at0[0] = 38912
        COLS = place("cols", NCOL)
        IDENT = place("ident", P)
        ONES = place("ones", P)
        KEYS = place("keys", 2 * NK)
        IOTA = place("iota", NK)
        C4 = place("c4", 16)
        SM = place("small", 256)
        IU = [place(f"iu{e}", 4, dt=I32) for e in range(2)]
        IV = [place(f"iv{e}", 4, dt=I32) for e in range(2)]
        DOT = [place(f"dot{e}", 4) for e in range(2)]
        GEL = [place(f"gel{e}", 4) for e in range(2)]
        AV = [place(f"act{e}", 4) for e in range(2)]
        SC = at0[0]
        COS, SINS, KR = (place(n, S) for n in ("cos", "sins", "kr"))
        RS = place("rs", S)
        SQ = [place(f"sq{e}", S) for e in range(2)]
        TMP, TMP2 = place("tmp", S), place("tmp2", S)
        SC2 = at0[0]
        LX = [place(f"lx{e}", S + 4) for e in range(2)]
        XC1 = [place(f"xc{e}", S) for e in range(2)]
        LWT = [place(f"lw{e}", 4 * P) for e in range(2)]
        R_ = [place(f"r{d}", S) for d in range(2)]
        I_ = [place(f"i{d}", S) for d in range(2)]
        D_ = [place(f"d{d}", S) for d in range(2)]
        H_ = [place(f"h{d}", S) for d in range(2)]
        at0[0] = SC2
        WQ = place("wq", 2048)
        QN = [place(f"qn{e}", S) for e in range(2)]
        QR = place("qr", S)
        PM = [place(f"pm{e}", S) for e in range(2)]
        PT = place("pt", 4 * S)
        VH = [place(f"vh{e}", 4 * P) for e in range(2)]
        at0[0] = SC
        XC = place("xc", D)
        XS = place("xs", D)
        XT = place("xT", D)
        BUF = at0[0]
        PR, PRT = place("pr", 1024), place("prT", 1024)
        QB = [place(f"qb{e}", 512) for e in range(2)]
        QT = place("qT", 512)
        OT = place("oT", 512)
        IDX4 = place("idx", NB * HK, dt=I32)
        GATE4 = place("gates", NB * HK)
        S14, S24 = place("first keys", NB * HK), place("second keys", NB * HK)
        at0[0] = 16384
        SK = place("key scores", HALVES * NK)
        CAND = place("cand", D)
        EQ = CAND
        TV = place("top values", HALVES * TOPK)
        TI = place("top index", HALVES * TOPK, dt=U32)
        TIF = place("top index as float", HALVES * TOPK)
        CV = place("chosen sums", HK)
        CP = place("chosen places", HK, dt=U32)
        CA = place("first part", HK, dt=U32)
        CB = place("second part", HK, dt=U32)
        CAF, CBF = place("caf", HK), place("cbf", HK)
        S1, S2, GATE = place("s1", HK), place("s2", HK), place("gate", HK)
        TB = place("turned", 3 * DT, BUF)
        OH = [place(f"one-hot{e}", 4 * 2 * NK) for e in range(2)]
        GL = place("gelu", ET * DT)
        assert at0[0] <= BUF + 4096
        G = OH
        WS = [place(f"ws{e}", NK * TG, 16384 + e * NK * TG) for e in range(2)]
        XT2 = place("xT dense", DB * D, SC)
        ACC = place("acc", D)

        STATS, MV, RSTD, NEWTON = SM[:, 0:24], SM[:, 24:26], SM[:, 26:27], SM[:, 27:28]
        MX, NMX, RSUM, RINV = SM[:, 32:36], SM[:, 36:40], SM[:, 40:44], SM[:, 44:48]
        LM = [SM[:, 64 + 16 * k:80 + 16 * k] for k in range(6)]
        GS, GR = SM[:, 48:56], SM[:, 56:64]
        MX2 = [SM[:, 160 + 8 * e:161 + 8 * e] for e in range(2)]
        NM2 = [SM[:, 161 + 8 * e:162 + 8 * e] for e in range(2)]
        RSM2 = [SM[:, 162 + 8 * e:163 + 8 * e] for e in range(2)]
        RI2 = [SM[:, 163 + 8 * e:164 + 8 * e] for e in range(2)]

        ps = ctx.enter_context(nc.psum_tensor("ps", [P, 8, BANK], F32))

        def bank(k, n=BANK):
            return ps[:, k, 0:n]

        def col(k):
            return COLS[:, k:k + 1]

        consts_set = sem("consts_set")
        consts2_set = sem("consts2_set")
        cols_in = sem("cols_in")
        keys_in = sem("keys_in")
        x_in = [sem(f"x_in{b}") for b in range(NB)]
        mem_in = sem("mem_in")
        pos_in = sem("pos_in")
        gain0_in, gain1_in, gain2_in, gain3_in = (sem(f"gain{k}_in") for k in range(4))
        w_full = [sem(f"w_full{s}") for s in range(NW)]
        w_used = sem("w_used")
        mem_ev = sem("mem_ev")
        ln0_done = sem("ln0_done")
        x0T_mm, x0T_ev = sem("x0T_mm"), sem("x0T_ev")
        lw_full = [sem(f"lw_full{e}") for e in range(2)]
        r_mm = sem("r_mm")
        xbank_free, gbank_free, rbank_free = sem("xbank_free"), sem("gbank_free"), sem("rbank_free")
        conv_done, lru_done, u_ready = sem("conv_done"), sem("lru_done"), sem("u_ready")
        tanh_done, lam_abs, lam_exp = sem("tanh_done"), sem("lam_abs"), sem("lam_exp")
        angle, rope_tab = sem("angle"), sem("rope_tab")
        l2_ev = sem("l2_ev")
        rms_sq, rms_mm, rms_done = sem("rms_sq"), sem("rms_mm"), sem("rms_done")
        kr_done = sem("kr_done")
        kv_ev = sem("kv_ev")
        wq_full = sem("wq_full")
        qpe_mm, qn_mm, qn_ev, qr_done = sem("qpe_mm"), sem("qn_mm"), sem("qn_ev"), sem("qr_done")
        s_mm, nmx_done, exp_done, p_done = sem("s_mm"), sem("nmx_done"), sem("exp_done"), sem("p_done")
        t_mm, pt_ev, pv_mm, o_ev, vh_done = sem("t_mm"), sem("pt_ev"), sem("pv_mm"), sem("o_ev"), sem("vh_done")
        o_added = sem("o_added")
        ln1_done = sem("ln1_done")
        e_mm, e_ev, e_dv = sem("e_mm"), sem("e_ev"), sem("e_dv")
        u_full = [sem(f"u_full{s}") for s in range(4)]
        v_full = [sem(f"v_full{s}") for s in range(4)]
        u_free, v_free = sem("u_free"), sem("v_free")
        gel_done, act_done = sem("gel_done"), sem("act_done")
        sk_free, top_done, gate_exp, routed = sem("sk_free"), sem("top_done"), sem("gate_exp"), sem("routed")
        tb_mm, tb_ev, xt2_ready, scaled = sem("tb_mm"), sem("tb_ev"), sem("xt2_ready"), sem("scaled")
        oh_ready, oh_free, ws_ev, ws_free = sem("oh_ready"), sem("oh_free"), sem("ws_ev"), sem("ws_free")
        gates_out = sem("gates_out")
        wd_in = [sem(f"wd_in{e}") for e in range(2)]
        gl_done, g_ready, x_added, acc_ready = sem("gl_done"), sem("g_ready"), sem("x_added"), sem("acc_ready")
        y_ready, y_out = sem("y_ready"), sem("y_out")
        iu_set, iv_set, pool_tick = sem("iu_set"), sem("iv_set"), sem("pool_tick")
        dve_done, dve_tick, act_tick = sem("dve_done"), sem("dve_tick"), sem("act_tick")

        block = ctx.enter_context(nc.Block())

        @block.sync
        def _(sp):
            sp.sem_inc(ws_free, 2)
            sp.dma_start(COLS, cols_d).then_inc(cols_in, 16)
            sp.dma_start(MEMT, memT).then_inc(mem_in, 16)
            for s in range(NW):
                sp.dma_start(W[:, s * TW:(s + 1) * TW], w_once[s]).then_inc(w_full[s], 16)
            for b in range(NB):
                sp.dma_start(X[:, b * D:(b + 1) * D], x[b * P:(b + 1) * P, :]).then_inc(x_in[b], 16)
                if b == 0:
                    sp.dma_start(GAIN_G, gains[0:1, :].partition_broadcast(P)).then_inc(gain0_in, 16)
                    sp.dma_start(GAIN_B, gains[1:2, :].partition_broadcast(P)).then_inc(gain0_in, 16)
            sp.dma_start(KEYS, keysT).then_inc(keys_in, 16)
            sp.dma_start(TMP.bitcast(I32), pos.partition_broadcast(P)).then_inc(pos_in, 16)
            with sp.Fori(1, N_ONCE // NW) as i:
                for s in range(NW):
                    sp.wait_ge(w_used, i * NW + (s - NW + 1))
                    sp.dma_start(W[:, s * TW:(s + 1) * TW],
                                 w_once[bass.ds(i * NW + s, 1), :, :].rearrange("t p n -> p (t n)")
                                 ).then_inc(w_full[s], 16)
            done = N_ONCE // NW * NW
            for t in range(done, N_ONCE):
                sp.wait_ge(w_used, t - NW + 1)
                sp.dma_start(W[:, (t - done) * TW:(t - done + 1) * TW], w_once[t]).then_inc(w_full[t - done], 16)
            with sp.Fori(0, NB) as b:
                with sp.Fori(0, N_BLOCK // NW) as i:
                    for k in range(NW):
                        s = (N_ONCE + k) % NW
                        sp.wait_ge(w_used, b * N_BLOCK + i * NW + (N_ONCE + k - NW + 1))
                        sp.dma_start(W[:, s * TW:(s + 1) * TW],
                                     w_block[bass.ds(i * NW + k, 1), :, :].rearrange("t p n -> p (t n)")
                                     ).then_inc(w_full[s], 16)

            def ring(k, before, src, split=False):
                s = (DENSE0 + k) % NW
                dst = W[:, s * TW:(s + 1) * TW]
                if split:
                    dst = dst.rearrange("p (t n) -> p t n", t=2)
                sp.wait_ge(w_used, before + (k - NW + 1))
                sp.dma_start(dst, src).then_inc(w_full[s], 16)

            def load_u(g, before):
                for k in range(NW):
                    ring(k, before, peer_ut[bass.ds(g * NW + k, 1), :, :].rearrange("t p n -> p (t n)"))

            def load_v(g, before):
                for k in range(NW):
                    c, m = k // 2, k % 2
                    ring(k, before, v_tiles[bass.ds(g * ET + 2 * m, 2), :, c * 512:(c + 1) * 512
                                            ].rearrange("t p n -> p t n"), True)

            def load_gates(g, par):
                sp.dma_start(WD[par].rearrange("p (g n) -> p g n", g=DT // TG),
                             gates_d[:, :, bass.ds(g * (ET * TG), ET * TG)].rearrange("g p n -> p g n")
                             ).then_inc(wd_in[par], 16)

            v_tiles = peer_v.rearrange("(t p) d -> t p d", p=P)
            load_u(0, DENSE0)
            with sp.Fori(0, DT // TG // 2) as i:
                for par in range(2):
                    sp.wait_ge(ws_ev, i * 16 + (par * 8 + 10))
                    sp.dma_start(gates_d[bass.ds(i * 2 + par, 1), :, :].rearrange("g p n -> p (g n)"), WS[par]
                                 ).then_inc(gates_out, 16)
                    sp.wait_ge(gates_out, i * 32 + (par * 16 + 16))
                    sp.sem_inc(ws_free, 1)
            load_gates(0, 0)
            load_gates(1, 1)
            load_u(1, DENSE0 + NW)
            load_v(0, DENSE0 + 2 * NW)
            with sp.Fori(1, GROUPS // 2) as i:
                for par in range(2):
                    g = i * 2 + par
                    sp.wait_ge(g_ready, g)
                    load_gates(g, par)
                    load_u(g, i * (4 * NW) + (DENSE0 - NW + par * 2 * NW))
                    load_v(g - 1, i * (4 * NW) + (DENSE0 + par * 2 * NW))
            load_v(GROUPS - 1, DENSE0 + (2 * GROUPS - 1) * NW)
            for b in range(NB):
                sp.wait_ge(y_ready, b + 1)
                sp.dma_start(out[b * P:(b + 1) * P, :], X[:, b * D:(b + 1) * D]).then_inc(y_out, 16)
            sp.wait_ge(y_out, 16 * NB)

        @block.gpsimd
        def _(pool):
            pool.memset(IDENT, 0.0).then_inc(consts_set, 1)
            pool.memset(ONES, 1.0).then_inc(consts_set, 1)
            for e in range(2):
                pool.memset(LX[e], 0.0).then_inc(consts_set, 1)
            pool.iota(IOTA, pattern=[[1, NK]], base=0, channel_multiplier=0,
                      allow_small_or_imprecise_dtypes=True).then_inc(consts_set, 1)
            pool.wait_ge(consts_set, 5)
            pool.affine_select(out=IDENT, in_=IDENT, compare_op=ALU.not_equal, fill=1.0, base=0,
                               pattern=[[-1, P]], channel_multiplier=1).then_inc(consts2_set, 1)
            for n in range(NL):
                if n >= 2:
                    pool.wait_ge(r_mm, n - 1)
                pool.dma_start(LWT[n % 2], lru_w[n]).then_inc(lw_full[n % 2], 16)
            pool.wait_ge(lru_done, NL + 1)
            pool.dma_start(WQ, wq_pairs[0]).then_inc(wq_full, 16)
            pool.wait_ge(kv_ev, 16)

            def copy_v(hp):
                for e in range(2):
                    pool.wait_ge(pv_mm, hp * 2 + (e + 1))
                    pool.sem_inc(pool_tick, 1)
                    pool.tensor_copy(VH[e].rearrange("p (t v) -> p t v", t=4),
                                     V.rearrange("p (t w) -> p t w", t=4)[:, :, bass.ds(hp * 256 + e * P, P)]
                                     ).then_inc(vh_done, 1)

            with pool.Fori(0, HEADS // 2 - 1) as hp:
                copy_v(hp)
                pool.wait_ge(qn_mm, hp * 2 + 2)
                pool.sem_inc(pool_tick, 1)
                pool.dma_start(WQ, wq_pairs[bass.ds(hp + 1, 1), :, :].rearrange("a p n -> p (a n)")
                               ).then_inc(wq_full, 16)
            copy_v(HEADS // 2 - 1)
            pool.wait_ge(qn_mm, HEADS)
            pool.dma_start(GAIN_G, gains[2:3, :].partition_broadcast(P)).then_inc(gain1_in, 16)
            pool.dma_start(GAIN_B, gains[3:4, :].partition_broadcast(P)).then_inc(gain1_in, 16)
            pool.wait_ge(ln1_done, NB)
            pool.dma_start(GAIN_G, gains[4:5, :].partition_broadcast(P)).then_inc(gain2_in, 16)
            pool.dma_start(GAIN_B, gains[5:6, :].partition_broadcast(P)).then_inc(gain2_in, 16)

            def index(dst, j, ready, n):
                pool.tensor_copy(dst, IDX4[:, bass.ds(j * 4, 4)]).then_inc(ready, 1)
                pool.wait_ge(ready, n)
                pool.sem_inc(pool_tick, 1)

            def row(ring, table, idx, s, full, free, need):
                pool.wait_ge(free, need)
                pool.sem_inc(pool_tick, 1)
                pool.indirect_dma_start(ring[:, s * D:(s + 1) * D], None, table,
                                        bass.IndirectOffsetOnAxis(ap=idx[:, s:s + 1], axis=0)
                                        ).then_inc(full[s], 16)

            def rows(j, par, last=False):
                if not last:
                    index(IU[1 - par], j + 1, iu_set, j + 2)
                index(IV[par], j, iv_set, j + 1)
                for s in range(4):
                    if not last:
                        row(U_RING, peer_u, IU[1 - par], s, u_full, u_free, j * 4 + (s + 5))
                    row(V_RING, peer_v, IV[par], s, v_full, v_free, j * 4 + (s + 1))

            pool.wait_ge(routed, NB)
            pool.dma_start(GAIN_G, gains[6:7, :].partition_broadcast(P)).then_inc(gain3_in, 16)
            pool.dma_start(GAIN_B, gains[7:8, :].partition_broadcast(P)).then_inc(gain3_in, 16)
            pool.wait_ge(xt2_ready, 1)
            index(IU[0], 0, iu_set, 1)
            for s in range(4):
                row(U_RING, peer_u, IU[0], s, u_full, u_free, s + 1)
            pool.wait_ge(gates_out, 16 * (DT // TG))
            with pool.Fori(0, JG // 2 - 1) as i:
                for par in range(2):
                    rows(i * 2 + par, par)
            rows(JG - 2, 0)
            rows(JG - 1, 1, last=True)

        @block.tensor
        def _(pe):
            def tile_wait(t, ahead=0):
                pe.wait_ge(w_full[t % NW], ahead * (16 // NW) + 16 * (t // NW + 1))

            def tile(t):
                return W[:, (t % NW) * TW:(t % NW + 1) * TW]

            pe.sem_inc(t_mm, 2)
            pe.sem_inc(pv_mm, 2)
            pe.sem_inc(oh_free, 2)
            pe.wait_ge(mem_in, 16)
            t = 0
            for h in range(MH):
                for half in range(2):
                    tile_wait(t)
                    for k in range(8):
                        kt = half * 8 + k
                        last = pe.matmul(bank(h, MEM), tile(t)[:, k * P:(k + 1) * P], MEMT[:, kt * MEM:(kt + 1) * MEM],
                                         start=(kt == 0), stop=(kt == KT - 1))
                    last.then_inc(w_used, 1)
                    t += 1
            for j in range(8):
                tile_wait(t)
                for m in range(2):
                    for k in range(2):
                        kt = 2 * j + k
                        last = pe.matmul(bank(4 + m), MEMT[:, kt * MEM + m * P:kt * MEM + (m + 1) * P],
                                         tile(t)[:, k * 512:(k + 1) * 512], start=(kt == 0), stop=(kt == KT - 1))
                last.then_inc(w_used, 1)
                t += 1
            pe.wait_ge(consts2_set, 1)
            for b in range(NB):
                pe.wait_ge(ln0_done, b + 1)
                for q in range(4):
                    n = 4 * b + q
                    if n >= 2:
                        pe.wait_ge(x0T_ev, n - 1)
                    for k in range(4):
                        kt = 4 * q + k
                        last = pe.transpose(ps[:, 6 + n % 2, k * P:(k + 1) * P],
                                            X[:, b * D + kt * P:b * D + (kt + 1) * P], IDENT)
                    last.then_inc(x0T_mm, 1)
            pe.wait_ge(x0T_ev, 4 * NB)
            pe.wait_ge(mem_ev, 6)

            def from_x0(out_ap, t, ahead):
                for half in range(2):
                    tile_wait(t + half, ahead)
                    for k in range(8):
                        kt = half * 8 + k
                        last = pe.matmul(out_ap, tile(t + half)[:, k * P:(k + 1) * P], A[:, kt * S:(kt + 1) * S],
                                         start=(kt == 0), stop=(kt == KT - 1))
                    last.then_inc(w_used, 1)

            with pe.Fori(0, NL // 2) as i:
                for e in range(2):
                    pe.wait_ge(xbank_free, i * 2 + (e + 1))
                    from_x0(bank(e), t + 2 * e, i * 8)
                for e in range(2):
                    pe.wait_ge(gbank_free, i * 2 + (e + 1))
                    from_x0(bank(2 + e), t + 4 + 2 * e, i * 8)
                    pe.wait_ge(conv_done, i * 2 + (e + 3))
                    pe.wait_ge(rbank_free, i * 2 + (e + 1))
                    pe.wait_ge(lw_full[e], i * 16 + 16)
                    for q in range(4):
                        last = pe.matmul(bank(4 + q), LWT[e][:, q * P:(q + 1) * P], XC1[e], start=True, stop=True)
                    last.then_inc(r_mm, 1)
            t += 8 * (NL // 2)
            pe.wait_ge(xbank_free, NL + 2)
            pe.wait_ge(gbank_free, NL + 2)
            pe.wait_ge(rbank_free, NL + 1)
            with pe.Fori(0, 2) as i:
                for j in range(4):
                    from_x0(ps[:, bass.ds(i * 4 + j, 1), :].rearrange("p a n -> p (a n)"), t + 2 * j, i * 8)
            t += 16
            pe.wait_ge(l2_ev, 2)
            for j in range(2):
                from_x0(bank(j), t + 2 * j, 0)
            t += 4

            def squares(first, count, b):
                for r in range(count):
                    pe.wait_ge(rms_sq, first + r + 1)
                    pe.matmul(bank(b), ONES, SQ[(first + r) % 2], start=(r == 0), stop=(r == count - 1)
                              ).then_inc(rms_mm, 1)

            pe.wait_ge(l2_ev, 8)
            squares(0, 4, 2)
            squares(4, 4, 3)
            pe.wait_ge(rms_done, 1)
            for hh in range(HEADS // 2):
                if hh >= 2:
                    pe.wait_ge(kv_ev, 2 * hh - 2)
                tile_wait(t)
                for e in range(2):
                    for k in range(4):
                        last = pe.matmul(bank(4 + (2 * hh + e) % 4), tile(t)[:, e * 512 + k * P:e * 512 + (k + 1) * P],
                                         C[:, k * S:(k + 1) * S], start=(k == 0), stop=(k == 3))
                last.then_inc(w_used, 1)
                t += 1
            pe.wait_ge(rms_done, 2)
            pe.wait_ge(kr_done, 1)
            for half in range(2):
                if half:
                    pe.wait_ge(kv_ev, 12)
                for j in range(2):
                    tile_wait(t)
                    for b in range(NB):
                        for k in range(2):
                            kt = 2 * j + k
                            last = pe.matmul(bank(b), C[:, kt * S + b * P:kt * S + (b + 1) * P],
                                             tile(t)[:, k * 512:(k + 1) * 512], start=(kt == 0), stop=(kt == 3))
                    last.then_inc(w_used, 1)
                    t += 1
            pe.wait_ge(kv_ev, 16)
            with pe.Fori(0, HEADS // 2) as hp:
                pe.wait_ge(wq_full, hp * 16 + 16)
                pe.wait_ge(qr_done, hp + 1)
                pe.wait_ge(o_ev, hp * 2 + 2)
                for part, done in ((2, None), (3, qpe_mm), (0, qn_mm), (1, qn_mm)):
                    for k in range(4):
                        last = pe.matmul(bank(part), WQ[:, part * 512 + k * P:part * 512 + (k + 1) * P],
                                         C[:, (4 + k) * S:(5 + k) * S], start=(k == 0), stop=(k == 3))
                    if done is not None:
                        last.then_inc(done, 1)

                def scores(n):
                    e, qb = n // 4, n % 4
                    pe.wait_ge(exp_done, hp * 8 + (n + 1))
                    if n == 0:
                        pe.wait_ge(qr_done, hp + 2)
                        pe.wait_ge(qn_ev, hp * 2 + 1)
                    if n == 4:
                        pe.wait_ge(qn_ev, hp * 2 + 2)
                    pe.matmul(bank(4 + n % 2), QN[e][:, qb * P:(qb + 1) * P], KN[:, bass.ds(hp * 1024 + e * S, S)],
                              start=True, stop=False)
                    pe.matmul(bank(4 + n % 2), QR[e * 64:(e + 1) * 64, qb * P:(qb + 1) * P],
                              KR[e * 64:(e + 1) * 64, :], start=False, stop=True).then_inc(s_mm, 1)

                def turn(n):
                    pe.wait_ge(p_done, hp * 8 + (n + 1))
                    pe.wait_ge(pt_ev, hp * 8 + (n + 1))
                    for k in range(4):
                        last = pe.transpose(ps[:, 6 + n % 2, k * P:(k + 1) * P], PM[n % 2][:, k * P:(k + 1) * P], IDENT)
                    last.then_inc(t_mm, 1)

                def values(e):
                    pe.wait_ge(pt_ev, hp * 8 + (4 * e + 6))
                    pe.wait_ge(vh_done, hp * 2 + (e + 1))
                    for k in range(4):
                        last = pe.matmul(bank(e), VH[e][:, k * P:(k + 1) * P], PT[:, k * S:(k + 1) * S],
                                         start=(k == 0), stop=(k == 3))
                    last.then_inc(pv_mm, 1)

                pe.wait_ge(qn_ev, hp * 2 + 2)
                scores(0)
                for n in range(1, 8):
                    scores(n)
                    turn(n - 1)
                    if n == 4:
                        values(0)
                turn(7)
                values(1)
            squares(8, 8, 2)
            squares(16, 8, 3)
            pe.wait_ge(rms_done, 4)
            pe.wait_ge(o_ev, HEADS + 2)
            with pe.Fori(0, 2) as i:
                for cc in range(2):
                    pe.wait_ge(o_added, i * 8 + (4 * cc + 4))
                    for j in range(8):
                        tile_wait(t + 8 * cc + j, i * 16)
                        for b in range(NB):
                            for k in range(2):
                                kt = 2 * j + k
                                last = pe.matmul(bank(4 * cc + b), Y[:, kt * S + b * P:kt * S + (b + 1) * P],
                                                 tile(t + 8 * cc + j)[:, k * 512:(k + 1) * 512],
                                                 start=(kt == 0), stop=(kt == KT - 1))
                        last.then_inc(w_used, 1)
            t += 32
            assert t == N_ONCE

            with pe.Fori(0, NB) as b:
                def did(ins, name):
                    ins.then_inc(e_mm, 1)
                    order.append(name)

                def seen(name):
                    pe.wait_ge(e_ev, b * len(ACT_STEPS) + ACT_AT[name])

                def told(name):
                    pe.wait_ge(e_dv, b * len(DVE_STEPS) + DVE_AT[name])

                order = []
                tt = [N_ONCE]

                def wtile():
                    tile_wait(tt[0], b * N_BLOCK)
                    return tile(tt[0])

                def used(ins):
                    ins.then_inc(w_used, 1)
                    tt[0] += 1

                def turned(src, q, name):
                    for k in range(4):
                        kt = 4 * q + k
                        last = pe.transpose(ps[:, 4 + q, k * P:(k + 1) * P], src[:, kt * P:(kt + 1) * P], IDENT)
                    did(last, name)

                seen("xs")
                pe.wait_ge(o_added, 24)
                for q in QUAD:
                    turned(XS, q, f"x1T{q}")
                seen("x1T3")
                for name in PE_ORDER[4:]:
                    if name in ("q", "pq0", "pq1", "pq2", "pq3"):
                        if name == "pq0":
                            seen("x2T3")
                        if name == "pq2":
                            seen("pq0")
                        if name == "pq3":
                            seen("pq1")
                        to = 4 if name == "q" else 4 + int(name[2]) % 2
                        for j in range(8):
                            w = wtile()
                            for k in range(2):
                                kt = 2 * j + k
                                last = pe.matmul(bank(to), XT[:, kt * P:(kt + 1) * P], w[:, k * 512:(k + 1) * 512],
                                                 start=(kt == 0), stop=(kt == KT - 1))
                            used(last)
                    elif name == "qT" or name[:3] == "pqT":
                        c = 0 if name == "qT" else int(name[3])
                        seen("q" if name == "qT" else f"pq{c}")
                        if c:
                            seen(f"pqT{c - 1}")
                        for k in range(4):
                            last = pe.transpose(ps[:, 5 if name == "qT" else 6, k * P:(k + 1) * P],
                                                QB[c % 2][:, k * P:(k + 1) * P], IDENT)
                        did(last, name)
                    elif name == "sc":
                        seen("qT")
                        for h in range(MH):
                            last = pe.matmul(ps[:, 6 + h // 2, (h % 2) * MEM:(h % 2 + 1) * MEM],
                                             QT[:, h * P:(h + 1) * P], KM[:, h * MEM:(h + 1) * MEM],
                                             start=True, stop=True)
                        did(last, name)
                    elif name == "pT":
                        told("prob")
                        for n in range(8):
                            last = pe.transpose(ps[:, 4 + n // 4, (n % 4) * P:(n % 4 + 1) * P],
                                                PR[:, n * P:(n + 1) * P], IDENT)
                        did(last, name)
                    elif name == "pv":
                        seen("pT")
                        for h in range(MH):
                            for m in range(2):
                                last = pe.matmul(ps[:, 6, h * P:(h + 1) * P],
                                                 VM[:, m * 512 + h * P:m * 512 + (h + 1) * P],
                                                 PRT[:, (2 * h + m) * P:(2 * h + m + 1) * P],
                                                 start=(m == 0), stop=(m == 1))
                        did(last, name)
                    elif name[:2] == "wo":
                        c = int(name[2])
                        if c == 0:
                            seen("pv")
                        for j in range(2):
                            w = wtile()
                            for k in range(2):
                                kt = 2 * j + k
                                last = pe.matmul(bank(4 + c), OT[:, kt * P:(kt + 1) * P], w[:, k * 512:(k + 1) * 512],
                                                 start=(kt == 0), stop=(kt == 3))
                            used(last)
                    elif name[:3] == "x2T":
                        q = int(name[3])
                        if q == 0:
                            told("x2")
                        turned(XC, q, name)
                    elif name[:3] == "key":
                        c = int(name[3])
                        seen(f"pqT{c}")
                        if c:
                            seen(f"key{c - 1}")
                        for k in range(4):
                            last = pe.matmul(ps[:, 7, k * P:(k + 1) * P], QT[:, k * P:(k + 1) * P],
                                             KEYS[:, (k % 2) * NK:(k % 2 + 1) * NK], start=True, stop=True)
                        did(last, name)
                assert order == PE_STEPS and tt[0] == N_ONCE + N_BLOCK

            pe.wait_ge(routed, NB)
            pe.wait_ge(e_ev, NB * len(ACT_STEPS))
            for k, t4 in enumerate((S14, S24, GATE4)):
                for d in range(DB):
                    b = NB - DB + d
                    n = k * DB + d
                    last = pe.transpose(ps[:, 4 + n // 4, (n % 4) * P:(n % 4 + 1) * P], t4[:, b * HK:(b + 1) * HK], IDENT)
            last.then_inc(tb_mm, 1)
            with pe.Fori(0, DT // 8) as i:
                for h in range(2):
                    pe.wait_ge(oh_ready, i * 8 + (4 * h + 4))
                    pe.wait_ge(ws_ev, i * 2 + (h + 1))
                    for k in range(4):
                        last = pe.matmul(ps[:, 6 + h, k * NK:(k + 1) * NK], OH[h][:, 2 * k * NK:(2 * k + 1) * NK],
                                         OH[h][:, (2 * k + 1) * NK:(2 * k + 2) * NK], start=True, stop=True)
                    last.then_inc(oh_free, 1)

            def dense_tile(k, before):
                t = DENSE0 + k
                pe.wait_ge(w_full[t % NW], before * (16 // NW) + (16 * (t // NW + 1)))
                return tile(t)

            xt2 = XT2.rearrange("p (b k t) -> p b k t", b=DB, k=KT)

            def all_u(g, par, before):
                pe.wait_ge(gl_done, g * 2 + 2)
                for et in range(ET):
                    for half in range(2):
                        w = dense_tile(2 * et + half, before)
                        for k in range(8):
                            kt = half * 8 + k
                            last = pe.matmul(ps[:, par * 2 + et // 2, (et % 2) * DT:(et % 2 + 1) * DT],
                                             w[:, k * P:(k + 1) * P], xt2[:, :, kt, :],
                                             start=(kt == 0), stop=(kt == KT - 1))
                        last.then_inc(w_used, 1)

            def all_v(g, par, before):
                pe.wait_ge(g_ready, g + 2)
                for c in QUAD:
                    pe.wait_ge(x_added, g * 8 + (2 * c + 2))
                    for m in range(2):
                        w = dense_tile(2 * c + m, before)
                        for tb in range(DB):
                            for t in range(2):
                                et = 2 * m + t
                                last = pe.matmul(bank(4 + (c % 2) * 2 + tb), G[par][:, et * DT + tb * P:et * DT + (tb + 1) * P],
                                                 w[:, t * 512:(t + 1) * 512], start=(et == 0), stop=(et == ET - 1))
                        last.then_inc(w_used, 1)

            pe.wait_ge(xt2_ready, 1)
            all_u(0, 0, 0)
            all_u(1, 1, NW)
            all_v(0, 0, 2 * NW)
            with pe.Fori(1, GROUPS // 2) as i:
                for par in range(2):
                    all_u(i * 2 + par, par, i * (4 * NW) + (2 * par - 1) * NW)
                    all_v(i * 2 + par - 1, 1 - par, i * (4 * NW) + 2 * par * NW)
            all_v(GROUPS - 1, 1, (2 * GROUPS - 1) * NW)

        @block.scalar
        def _(act):
            def tick():
                act.sem_inc(act_tick, 1)

            def evict(dst, src):
                return act.activation(dst, src, ACT.Copy)

            act.sem_inc(xbank_free, 2)
            act.sem_inc(gbank_free, 2)
            act.sem_inc(rbank_free, 1)
            act.sem_inc(exp_done, 2)
            act.sem_inc(pt_ev, 2)
            act.sem_inc(o_ev, 2)
            act.sem_inc(gl_done, 4)
            act.sem_inc(ws_ev, 2)
            act.wait_ge(lam_abs, 1)
            act.activation(LM[1], LM[0], ACT.Exp, scale=-1.0).then_inc(lam_exp, 1)
            act.wait_ge(angle, 1)
            act.activation(SINS, RS, ACT.Sin, scale=col(C_SIGN))
            act.activation(COS, COS, ACT.Sin).then_inc(rope_tab, 1)
            for h in range(MH):
                act.wait_ge(w_used, 2 * (h + 1))
                evict(KM[:, h * MEM:(h + 1) * MEM], bank(h, MEM)).then_inc(mem_ev, 1)
            act.wait_ge(w_used, 16)
            for m in range(2):
                evict(VM[:, m * 512:(m + 1) * 512], bank(4 + m)).then_inc(mem_ev, 1)
            for n in range(4 * NB):
                b, q = n // 4, n % 4
                act.wait_ge(x0T_mm, n + 1)
                evict(A.rearrange("p (k s) -> p k s", k=KT)[:, 4 * q:4 * q + 4, b * P:(b + 1) * P],
                      bank(6 + n % 2).rearrange("p (k s) -> p k s", k=4)).then_inc(x0T_ev, 1)
            act.wait_ge(consts_set, 5)
            with act.Fori(0, NL // 2) as i:
                for e in range(2):
                    act.wait_ge(w_used, i * 8 + (16 + 2 * e + 2))
                    act.wait_ge(conv_done, i * 2 + (e + 1))
                    evict(LX[e][:, 2:2 + S], bank(e)).then_inc(xbank_free, 1)
                for e in range(2):
                    act.wait_ge(w_used, i * 8 + (20 + 2 * e + 2))
                    tick()
                    act.activation(Y[:, bass.ds(i * 1024 + (8 + e) * S, S)], bank(2 + e), ACT.Gelu
                                   ).then_inc(gbank_free, 1)
                    act.wait_ge(r_mm, i * 2 + (e + 1))
                    act.wait_ge(lru_done, i * 2 + (e + 1))
                    tick()
                    for q in range(4):
                        dst = (R_ + I_)[q]
                        first = C_BA if q < 2 else C_BX
                        last = act.activation(dst, bank(4 + q), ACT.Sigmoid,
                                              bias=COLS[:, bass.ds(i * 2 + (first + (q % 2) * NL + e), 1)])
                    last.then_inc(rbank_free, 1)
                    act.wait_ge(rbank_free, i * 2 + (e + 2))
                    tick()
                    for d in range(2):
                        last = act.activation(R_[d], R_[d], ACT.Tanh, scale=C4[:, bass.ds(i * 2 + (d * NL + e), 1)])
                    last.then_inc(tanh_done, 1)
                    act.wait_ge(tanh_done, i * 2 + (e + 1))
                    for d in range(2):
                        last = act.activation(H_[d], R_[d], ACT.Sqrt)
                    last.then_inc(u_ready, 1)
            with act.Fori(0, 2) as i:
                for j in range(4):
                    act.wait_ge(w_used, i * 8 + (48 + 2 * j + 2))
                    tick()
                    evict(C[:, bass.ds(i * 2048 + j * S, S)], ps[:, bass.ds(i * 4 + j, 1), :].rearrange("p a n -> p (a n)")
                          ).then_inc(l2_ev, 1)

            def squares(first, count, src):
                for r in range(first, first + count):
                    if r >= 2:
                        act.wait_ge(rms_mm, r - 1)
                    act.activation(SQ[r % 2], src[:, (r - first) * S:(r - first + 1) * S], ACT.Square
                                   ).then_inc(rms_sq, 1)

            act.wait_ge(l2_ev, 8)
            squares(0, 4, C)
            squares(4, 4, C[:, 4 * S:8 * S])
            for hh in range(HEADS // 2):
                act.wait_ge(w_used, 68 + hh + 1)
                for h in (2 * hh, 2 * hh + 1):
                    evict(KN[:, h * S:(h + 1) * S], bank(4 + h % 4)).then_inc(kv_ev, 1)
            for half in range(2):
                act.wait_ge(w_used, 72 + 2 * half + 2)
                for b in range(NB):
                    evict(V[:, b * 1024 + half * 512:b * 1024 + (half + 1) * 512], bank(b)).then_inc(kv_ev, 1)
            act.wait_ge(lru_done, NL + 1)
            with act.Fori(0, HEADS // 2) as hp:
                for e in range(2):
                    act.wait_ge(qn_mm, hp * 2 + (e + 1))
                    evict(QN[e], bank(e)).then_inc(qn_ev, 1)

                def exp(n):
                    act.wait_ge(nmx_done, hp * 8 + (n + 1))
                    act.wait_ge(t_mm, hp * 8 + (n + 1))
                    act.activation(PM[n % 2], bank(4 + n % 2), ACT.Exp, bias=NM2[n % 2], scale=ATT_SCALE,
                                   accum_out=RSM2[n % 2]).then_inc(exp_done, 1)

                def turned(n):
                    act.wait_ge(t_mm, hp * 8 + (n + 3))
                    if n % 4 == 0:
                        act.wait_ge(pv_mm, hp * 2 + (n // 4 + 2))
                    qb = n % 4
                    evict(PT.rearrange("p (k s) -> p k s", k=4)[:, :, qb * P:(qb + 1) * P],
                          bank(6 + n % 2).rearrange("p (k s) -> p k s", k=4)).then_inc(pt_ev, 1)

                def output(e):
                    act.wait_ge(pv_mm, hp * 2 + (e + 3))
                    tick()
                    evict(Y[:, bass.ds(hp * 1024 + e * S, S)], bank(e)).then_inc(o_ev, 1)

                exp(0)
                for n in range(1, 8):
                    exp(n)
                    if n == 5:
                        output(0)
                    turned(n - 1)
                turned(7)
                output(1)
            act.wait_ge(o_ev, HEADS + 2)
            squares(8, 8, Y)
            squares(16, 8, Y[:, 8 * S:16 * S])
            act.wait_ge(ln1_done, NB)

            def gate_exps(n):
                act.wait_ge(top_done, n)
                act.activation(GATE, GATE, ACT.Exp).then_inc(gate_exp, 1)

            def block_stage(b, first=False):
                def product(name):
                    if name in TILES_AT:
                        act.wait_ge(w_used, b * N_BLOCK + (N_ONCE + TILES_AT[name]))
                    else:
                        act.wait_ge(e_mm, b * len(PE_STEPS) + PE_AT[name])

                for name in ACT_STEPS:
                    if name == "xs":
                        last = evict(XS, X[:, bass.ds(b * D, D)])
                    elif name[:3] in ("x1T", "x2T"):
                        q = int(name[3])
                        product(name)
                        last = evict(XT[:, q * 512:(q + 1) * 512], bank(4 + q))
                    elif name == "keep":
                        act.wait_ge(e_ev, b * len(ACT_STEPS) + ACT_AT["x2T3"])
                        tick()
                        evict(X[:, bass.ds(b * D, D)], XC)
                        last = evict(XTA[:, bass.ds(b * D, D)], XT)
                    elif name in ("q", "pq0", "pq1", "pq2", "pq3"):
                        product(name)
                        c = 0 if name == "q" else int(name[2]) % 2
                        last = evict(QB[c], bank(4 + c))
                    elif name == "qT":
                        product(name)
                        last = evict(QT, bank(5))
                    elif name[:3] == "pqT":
                        product(name)
                        last = evict(QT, bank(6))
                    elif name == "exp":
                        act.wait_ge(e_dv, b * len(DVE_STEPS) + DVE_AT["max"])
                        for h in range(MH):
                            last = act.activation(PR[:, h * MEM:(h + 1) * MEM],
                                                  ps[:, 6 + h // 2, (h % 2) * MEM:(h % 2 + 1) * MEM], ACT.Exp,
                                                  bias=NMX[:, h:h + 1], scale=MEM_SCALE, accum_out=RSUM[:, h:h + 1])
                    elif name == "pT":
                        product(name)
                        last = evict(PRT, ps[:, 4:6, :].rearrange("p a n -> p (a n)"))
                    elif name == "pv":
                        product(name)
                        last = evict(OT, bank(6))
                    elif name[:3] == "key":
                        product(name)
                        c = int(name[3])
                        if c == 0:
                            act.wait_ge(sk_free, b + 1)
                        last = evict(SK[:, c * 512:(c + 1) * 512], bank(7))
                    last.then_inc(e_ev, 1)
                    if name == "key1" and not first:
                        gate_exps(b)

            block_stage(0, first=True)
            with act.Fori(0, NB - 1) as i:
                block_stage(i + 1)
            act.wait_ge(e_ev, NB * len(ACT_STEPS))
            evict(XT2, XTA[:, (NB - DB) * D:NB * D]).then_inc(xt2_ready, 1)
            act.wait_ge(w_used, DENSE0)
            act.activation(ACC, X[:, 0:D], ACT.Copy, scale=ALPHA).then_inc(acc_ready, 1)
            act.activation(X[:, 2 * D:4 * D], X[:, 2 * D:4 * D], ACT.Copy, scale=ALPHA).then_inc(scaled, 1)
            gate_exps(NB)
            act.wait_ge(tb_mm, 1)
            evict(TB, ps[:, 4:6, :].rearrange("p a n -> p (a n)")[:, 0:3 * DT]).then_inc(tb_ev, 1)
            with act.Fori(0, DT // TG // 2) as i:
                for par in range(2):
                    act.wait_ge(ws_free, i * 2 + (par + 1))
                    with act.Fori(0, 4) as k:
                        for h in range(2):
                            act.wait_ge(oh_free, i * 16 + k * 2 + (par * 8 + h + 3))
                            tick()
                            evict(WS[par].rearrange("p (a t) -> p a t", t=TG)[:, :, bass.ds(k * 8 + 4 * h, 4)],
                                  bank(6 + h).rearrange("p (t a) -> p a t", t=4)).then_inc(ws_ev, 1)

            def gelu_rows(j, par):
                act.wait_ge(u_free, j * 4 + 8)
                act.wait_ge(act_done, j + 1)
                act.activation(GEL[par], DOT[par], ACT.Gelu).then_inc(gel_done, 1)

            def gelu_dense(g, par, before):
                act.wait_ge(g_ready, g + 1)
                for k in range(2):
                    act.wait_ge(w_used, before + (DENSE0 + 4 * k + 4))
                    act.activation(GL[:, k * 512:(k + 1) * 512], bank(par * 2 + k), ACT.Gelu).then_inc(gl_done, 1)

            def both(i, last=False):
                for par in range(2):
                    gelu_rows(i * 4 + (2 * par + 1), 1)
                    if isinstance(i, int) and i == 0:
                        gelu_dense(par, par, par * NW)
                    else:
                        gelu_dense(i * 2 + par, par, i * (4 * NW) + (2 * par - 1) * NW)
                    if not (last and par == 1):
                        gelu_rows(i * 4 + (2 * par + 2), 0)

            gelu_rows(0, 0)
            both(0)
            with act.Fori(1, GROUPS // 4) as i:
                both(i)
            act.wait_ge(y_ready, 1)
            act.activation(ACC, X[:, D:2 * D], ACT.Copy, scale=ALPHA).then_inc(acc_ready, 1)
            with act.Fori(GROUPS // 4, GROUPS // 2 - 1) as i:
                both(i)
            both(GROUPS // 2 - 1, last=True)

        @block.vector
        def _(dve):
            link = InOrder(dve, dve_done)

            def tick():
                dve.sem_inc(dve_tick, 1)

            def rsqrt(y, v, t):
                link(dve.tensor_scalar(y.bitcast(I32), v.bitcast(I32), 1, None, ALU.logical_shift_right))
                link(dve.tensor_scalar(y.bitcast(I32), y.bitcast(I32), -1.0, float(0x5f3759df), ALU.mult, ALU.add))
                for _ in range(3):
                    link(dve.tensor_tensor(t, y, y, ALU.mult))
                    link(dve.tensor_tensor(t, t, v, ALU.mult))
                    link(dve.tensor_scalar(t, t, -0.5, 1.5, ALU.mult, ALU.add))
                    link(dve.tensor_tensor(y, y, t, ALU.mult))

            def norm(src, dst, gain, bias, hold=None):
                for k in range(4):
                    last = dve.bn_stats(STATS[:, 6 * k:6 * k + 6], src[:, k * 512:(k + 1) * 512])
                link(last, hold)
                link(dve.bn_aggr(MV, STATS))
                link(dve.tensor_scalar(MV[:, 1:2], MV[:, 1:2], LN_EPS, None, ALU.add))
                rsqrt(RSTD, MV[:, 1:2], NEWTON)
                link(dve.tensor_scalar(dst, src, MV[:, 0:1], RSTD, ALU.subtract, ALU.mult))
                link(dve.tensor_tensor(dst, dst, gain, ALU.mult))
                return dve.tensor_tensor(dst, dst, bias, ALU.add)

            dve.sem_inc(conv_done, 2)
            dve.sem_inc(lru_done, 1)
            dve.sem_inc(qr_done, 1)
            dve.sem_inc(o_added, 8)
            dve.sem_inc(sk_free, 1)
            dve.sem_inc(act_done, 2)
            dve.sem_inc(g_ready, 1)
            dve.sem_inc(x_added, 4)
            dve.sem_inc(u_free, 4)
            dve.sem_inc(v_free, 4)
            lam = COLS[:, C_LAM:C_LAM + 16]
            dve.wait_ge(cols_in, 16)
            dve.scalar_tensor_tensor(out=LM[0], in0=lam, scalar=-1.0, in1=lam, op0=ALU.mult, op1=ALU.max
                                     ).then_inc(lam_abs, 1)
            link(dve.tensor_scalar(LM[2], lam, -4.0, 0.0, ALU.mult, ALU.max))
            dve.wait_ge(lam_exp, 1)
            link(dve.tensor_scalar(LM[3], LM[1], 2.0, None, ALU.add))
            link(dve.reciprocal(LM[4], LM[3]))
            link(dve.tensor_tensor(LM[3], LM[1], LM[4], ALU.mult))
            link(dve.tensor_tensor(LM[4], LM[3], LM[3], ALU.mult))
            link(dve.tensor_scalar(LM[5], LM[4], 1.0 / 15, None, ALU.mult))
            for odd in (13, 11, 9, 7, 5, 3):
                link(dve.scalar_tensor_tensor(out=LM[5], in0=LM[5], scalar=1.0 / odd, in1=LM[4],
                                              op0=ALU.add, op1=ALU.mult))
            link(dve.scalar_tensor_tensor(out=LM[5], in0=LM[5], scalar=1.0, in1=LM[3], op0=ALU.add, op1=ALU.mult))
            link(dve.scalar_tensor_tensor(out=C4, in0=LM[5], scalar=8.0, in1=LM[2], op0=ALU.mult, op1=ALU.add))
            dve.wait_ge(pos_in, 16)
            link(dve.tensor_copy(RS, TMP.bitcast(I32)))
            link(dve.tensor_scalar(RS, RS, col(C_FREQ), None, ALU.mult))
            link(dve.tensor_scalar(COS, RS, 1.0 / (2 * math.pi), ROUND, ALU.mult, ALU.add))
            link(dve.tensor_scalar(COS, COS, ROUND, None, ALU.subtract))
            for part in (TWO_PI_A, TWO_PI_B, TWO_PI_C):
                link(dve.scalar_tensor_tensor(out=RS, in0=COS, scalar=-part, in1=RS, op0=ALU.mult, op1=ALU.add))
            link(dve.tensor_scalar(RS, RS, 3.1415925, -3.1415925, ALU.min, ALU.max))
            link(dve.scalar_tensor_tensor(out=COS, in0=RS, scalar=-1.0, in1=RS, op0=ALU.mult, op1=ALU.max))
            dve.tensor_scalar(COS, COS, -1.0, math.pi / 2, ALU.mult, ALU.add).then_inc(angle, 1)
            dve.wait_ge(gain0_in, 32)
            for b in range(NB):
                dve.wait_ge(x_in[b], 16)
                xb = X[:, b * D:(b + 1) * D]
                norm(xb, xb, GAIN_G, GAIN_B).then_inc(ln0_done, 1)

            dve.wait_ge(consts_set, 5)
            with dve.Fori(0, NL // 2) as i:
                link.enter(i, 18)
                for e in range(2):
                    dve.wait_ge(xbank_free, i * 2 + (e + 3))

                    def cw(k):
                        return COLS[:, bass.ds(i * 2 + (C_CONVW + k * NL + e), 1)]

                    link(dve.tensor_scalar(XC1[e], LX[e][:, 0:S], cw(0), COLS[:, bass.ds(i * 2 + (C_CONVB + e), 1)],
                                           ALU.mult, ALU.add))
                    for k in range(1, 4):
                        last = dve.scalar_tensor_tensor(out=XC1[e], in0=LX[e][:, k:k + S], scalar=cw(k), in1=XC1[e],
                                                        op0=ALU.mult, op1=ALU.add)
                        if k < 3:
                            link(last)
                    last.then_inc(conv_done, 1)
                for e in range(2):
                    dve.wait_ge(u_ready, i * 2 + (e + 1))
                    dve.wait_ge(conv_done, i * 2 + 4)
                    for d in range(2):
                        dve.tensor_tensor(I_[d], I_[d], XC1[e], ALU.mult)
                        last = dve.tensor_scalar(D_[d], R_[d], 1.0, None, ALU.add)
                    link(last)
                    for d in range(2):
                        dve.scalar_tensor_tensor(out=I_[d], in0=I_[d], scalar=2.0, in1=H_[d], op0=ALU.mult, op1=ALU.mult)
                        last = dve.reciprocal(D_[d], D_[d])
                    link(last)
                    for d in range(2):
                        last = dve.tensor_tensor(I_[d], I_[d], D_[d], ALU.mult)
                    link(last)
                    for d in range(2):
                        last = dve.tensor_scalar(D_[d], D_[d], 2.0, -1.0, ALU.mult, ALU.add)
                    link(last)
                    dve.tensor_tensor_scan(H_[0], D_[0], I_[0], 0.0, ALU.mult, ALU.add)
                    link(dve.tensor_tensor_scan(H_[1][:, ::-1], D_[1][:, ::-1], I_[1][:, ::-1], 0.0, ALU.mult, ALU.add))
                    link(dve.tensor_tensor(H_[0], H_[0], H_[1], ALU.add))
                    dve.wait_ge(gbank_free, i * 2 + (e + 3))
                    gate = Y[:, bass.ds(i * 1024 + (8 + e) * S, S)]
                    dve.tensor_tensor(gate, gate, H_[0], ALU.mult).then_inc(lru_done, 1)
                link.leave(NL // 2)

            def rms(units, b, count, gains_at, region):
                dve.wait_ge(rms_mm, units)
                link(dve.tensor_scalar(TMP2, bank(b), 1.0 / (count * P), RMS_EPS, ALU.mult, ALU.add))
                rsqrt(RS, TMP2, TMP)
                for k in range(count):
                    r = region[:, k * S:(k + 1) * S]
                    last = dve.scalar_tensor_tensor(out=r, in0=r, scalar=col(gains_at + k), in1=RS,
                                                    op0=ALU.mult, op1=ALU.mult)
                last.then_inc(rms_done, 1)

            dve.wait_ge(rope_tab, 1)
            rms(4, 2, 4, C_KVG, C)
            rms(8, 3, 4, C_QG, C[:, 4 * S:8 * S])
            dve.wait_ge(w_used, 68)
            dve.tensor_tensor(KR, bank(0), COS, ALU.mult)
            link(dve.tensor_tensor(TMP, bank(1), SINS, ALU.mult))
            dve.tensor_tensor(KR, KR, TMP, ALU.add).then_inc(kr_done, 1)
            with dve.Fori(0, HEADS // 2) as hp:
                link.enter(hp, 1 + 8 * 2)
                dve.wait_ge(qpe_mm, hp + 1)
                dve.tensor_tensor(QR, bank(2), COS, ALU.mult)
                link(dve.tensor_tensor(TMP, bank(3), SINS, ALU.mult))
                dve.tensor_tensor(QR, QR, TMP, ALU.add).then_inc(qr_done, 1)

                def row_max(n):
                    dve.wait_ge(s_mm, hp * 8 + (n + 1))
                    link(dve.tensor_reduce(MX2[n % 2], bank(4 + n % 2), AX, ALU.max))
                    dve.tensor_scalar(NM2[n % 2], MX2[n % 2], -ATT_SCALE, None, ALU.mult).then_inc(nmx_done, 1)

                row_max(0)
                for n in range(8):
                    if n < 7:
                        row_max(n + 1)
                    dve.wait_ge(exp_done, hp * 8 + (n + 3))
                    link(dve.reciprocal(RI2[n % 2], RSM2[n % 2]))
                    dve.tensor_scalar(PM[n % 2], PM[n % 2], RI2[n % 2], None, ALU.mult).then_inc(p_done, 1)
                link.leave(HEADS // 2)
            rms(16, 2, 8, C_AG, Y)
            rms(24, 3, 8, C_LG, Y[:, 8 * S:16 * S])
            with dve.Fori(0, 2) as i:
                for cc in range(2):
                    dve.wait_ge(w_used, i * 16 + (76 + 8 * cc + 8))
                    for b in range(NB):
                        xs = X[:, bass.ds(i * 1024 + (b * D + cc * 512), 512)]
                        dve.scalar_tensor_tensor(out=xs, in0=xs, scalar=ALPHA, in1=bank(4 * cc + b),
                                                 op0=ALU.mult, op1=ALU.add).then_inc(o_added, 1)
            dve.wait_ge(o_added, 24)
            dve.wait_ge(gain1_in, 32)
            for b in range(NB):
                xb = X[:, b * D:(b + 1) * D]
                norm(xb, xb, GAIN_G, GAIN_B).then_inc(ln1_done, 1)
            dve.wait_ge(gain2_in, 32)

            def block_stage(b):
                def evicted(name):
                    dve.wait_ge(e_ev, b * len(ACT_STEPS) + ACT_AT[name])

                dve.wait_ge(e_mm, b * len(PE_STEPS) + PE_AT["sc"])
                link(dve.tensor_reduce(MX, ps[:, 6:8, :].rearrange("p a (c m) -> p (a c) m", m=MEM), AX, ALU.max))
                dve.tensor_scalar(NMX, MX, -MEM_SCALE, None, ALU.mult).then_inc(e_dv, 1)
                evicted("exp")
                link(dve.reciprocal(RINV, RSUM))
                pr = PR.rearrange("p (h m) -> p h m", h=MH)
                dve.tensor_tensor(pr, pr, RINV.unsqueeze(2).broadcast_to([P, MH, MEM]), ALU.mult).then_inc(e_dv, 1)
                for c in QUAD:
                    dve.wait_ge(w_used, b * N_BLOCK + (N_ONCE + TILES_AT[f"wo{c}"]))
                    xs = XS[:, c * 512:(c + 1) * 512]
                    dve.scalar_tensor_tensor(out=xs, in0=xs, scalar=ALPHA, in1=bank(4 + c),
                                             op0=ALU.mult, op1=ALU.add).then_inc(e_dv, 1)
                dve.wait_ge(e_dv, b * len(DVE_STEPS) + DVE_AT["wo3"])
                norm(XS, XC, GAIN_G, GAIN_B, dve_tick).then_inc(e_dv, 1)

            def routing(b):
                def top16(src, width, vals, idxs, count):
                    for half in range(2):
                        def at(t, n):
                            return t[:, n * TOPK + half * 8:n * TOPK + half * 8 + 8]
                        for n in range(count):
                            last = dve.max(at(vals, n), src[:, n * width:(n + 1) * width])
                        link(last, dve_tick)
                        for n in range(count):
                            last = dve.max_index(at(idxs, n), at(vals, n), src[:, n * width:(n + 1) * width])
                        link(last, dve_tick)
                        if half == 0:
                            for n in range(count):
                                w = src[:, n * width:(n + 1) * width]
                                last = dve.match_replace(w, at(vals, n), w, -3.0e38)
                            link(last, dve_tick)

                dve.wait_ge(e_ev, b * len(ACT_STEPS) + ACT_AT["key3"])
                tick()
                top16(SK, NK, TV, TI, HALVES)
                dve.sem_inc(sk_free, 1)
                tv = TV.rearrange("p (h t k) -> p h t k", t=2, k=TOPK)
                shape = [P, PH, TOPK, TOPK]

                def four(t):
                    return t.rearrange("p (h k a) -> p h k a", h=PH, k=TOPK)

                link(dve.tensor_tensor(four(CAND), tv[:, :, 0, :].unsqueeze(3).broadcast_to(shape),
                                       tv[:, :, 1, :].unsqueeze(2).broadcast_to(shape), ALU.add), dve_tick)
                top16(CAND, TOPK * TOPK, CV, CP, PH)
                cv = CV.rearrange("p (h k) -> p h k", k=TOPK)
                gate = GATE.rearrange("p (h k) -> p h k", k=TOPK)
                dve.tensor_tensor(gate, cv, cv[:, :, 0:1].broadcast_to([P, PH, TOPK]), ALU.subtract
                                  ).then_inc(top_done, 1)
                dve.tensor_scalar(CA, CP, 4, None, ALU.logical_shift_right)
                dve.tensor_scalar(CB, CP, 15, None, ALU.bitwise_and)
                link(dve.tensor_copy(TIF, TI))
                dve.tensor_copy(CAF, CA)
                link(dve.tensor_copy(CBF, CB))
                tif = TIF.rearrange("p (h t k) -> p h t k", t=2, k=TOPK)
                iota = IOTA[:, 0:TOPK].unsqueeze(1).unsqueeze(1).broadcast_to(shape)
                for half, place_f, number in ((0, CAF, S1), (1, CBF, S2)):
                    link(dve.tensor_tensor(four(EQ), place_f.rearrange("p (h k) -> p h k", k=TOPK).unsqueeze(3)
                                           .broadcast_to(shape), iota, ALU.is_equal))
                    link(dve.tensor_tensor(four(EQ), four(EQ), tif[:, :, half, :].unsqueeze(2).broadcast_to(shape),
                                           ALU.mult))
                    link(dve.tensor_reduce(number, EQ.rearrange("p (n a) -> p n a", a=TOPK), AX, ALU.add))
                here = bass.ds(b * HK, HK)
                dve.scalar_tensor_tensor(out=IDX4[:, here], in0=S1, scalar=float(NK), in1=S2, op0=ALU.mult, op1=ALU.add)
                dve.tensor_scalar(S14[:, here], S1, 1.0, None, ALU.mult)
                dve.tensor_scalar(S24[:, here], S2, 1.0, None, ALU.mult)
                dve.wait_ge(gate_exp, b + 1)
                link(dve.tensor_reduce(GS, gate, AX, ALU.add))
                link(dve.reciprocal(GR, GS))
                dve.tensor_tensor(GATE4[:, here].rearrange("p (h k) -> p h k", k=TOPK), gate,
                                  GR.unsqueeze(2).broadcast_to([P, PH, TOPK]), ALU.mult).then_inc(routed, 1)

            block_stage(0)
            with dve.Fori(0, NB - 1) as i:
                link.enter(i, 42)
                block_stage(i + 1)
                routing(i)
                link.leave(NB - 1)
            routing(NB - 1)

            dve.wait_ge(tb_ev, 1)
            with dve.Fori(0, DT // 8) as i:
                for h in range(2):
                    dve.wait_ge(oh_free, i * 2 + (h + 1))
                    for k in range(4):
                        def tcol(part):
                            return TB[:, bass.ds(i * 8 + (part * DT + 4 * h + k), 1)]
                        dve.tensor_scalar(OH[h][:, 2 * k * NK:(2 * k + 1) * NK], IOTA, tcol(1), None, ALU.is_equal)
                        dve.tensor_scalar(OH[h][:, (2 * k + 1) * NK:(2 * k + 2) * NK], IOTA, tcol(0), tcol(2),
                                          ALU.is_equal, ALU.mult).then_inc(oh_ready, 1)

            def dot(j, par, s, b):
                dve.wait_ge(u_full[s], j * 16 + 16)
                r = U_RING[:, s * D:(s + 1) * D]
                dve.tensor_tensor_reduce(r, r, X[:, b * D:(b + 1) * D], 1.0, 0.0, ALU.mult, ALU.add,
                                         DOT[par][:, s:s + 1]).then_inc(u_free, 1)

            def add_row(j, par, s):
                dve.wait_ge(v_full[s], j * 16 + 16)
                dve.wait_ge(v_free, j * 4 + (s + 4))
                dve.scalar_tensor_tensor(out=ACC, in0=V_RING[:, s * D:(s + 1) * D], scalar=AV[par][:, s:s + 1],
                                         in1=ACC, op0=ALU.mult, op1=ALU.add).then_inc(v_free, 1)

            def step(j, par, b):
                if b is not None:
                    dot(j + 1, 1 - par, 0, b)
                dve.wait_ge(gel_done, j + 1)
                dve.tensor_tensor(AV[par], GEL[par], GATE4[:, bass.ds(j * 4, 4)], ALU.mult).then_inc(act_done, 1)
                if b is not None:
                    dot(j + 1, 1 - par, 1, b)
                dve.wait_ge(act_done, j + 3)
                add_row(j, par, 0)
                for s in (1, 2):
                    if b is not None:
                        dot(j + 1, 1 - par, s + 1, b)
                    add_row(j, par, s)
                add_row(j, par, 3)

            def weigh(g, par, n):
                dve.wait_ge(gl_done, g * 2 + 6)
                dve.wait_ge(wd_in[par], n)
                dve.tensor_tensor(G[par].rearrange("p (e g t) -> p e g t", e=ET, t=TG),
                                  GL.rearrange("p (e g t) -> p e g t", e=ET, t=TG),
                                  WD[par].rearrange("p (g e t) -> p e g t", e=ET, t=TG), ALU.mult).then_inc(g_ready, 1)

            def add_dense(before, chunks):
                for c in chunks:
                    dve.wait_ge(w_used, before + (DENSE0 + 2 * c + 2))
                    for tb in range(DB):
                        xs = X[:, (NB - DB + tb) * D + c * 512:(NB - DB + tb) * D + (c + 1) * 512]
                        dve.tensor_tensor(xs, xs, bank(4 + (c % 2) * 2 + tb), ALU.add).then_inc(x_added, 1)

            def both(i, b, after=0):
                for par in range(2):
                    g = i * 2 + par
                    before = i * (4 * NW) + 2 * par * NW
                    step(i * 4 + 2 * par, 0, b)
                    weigh(g, par, i * 16 + 16)
                    if not (isinstance(g, int) and g == 0):
                        add_dense(before, (0, 1))
                    step(i * 4 + (2 * par + 1), 1, after if par == 1 and after != 0 else b)
                    if not (isinstance(g, int) and g == 0):
                        add_dense(before, (2, 3))

            for s in range(4):
                dot(0, 0, s, 0)
            dve.wait_ge(acc_ready, 1)
            dve.wait_ge(scaled, 1)
            both(0, 0)
            with dve.Fori(1, GROUPS // 4 - 1) as i:
                both(i, 0)
            both(GROUPS // 4 - 1, 0, after=1)
            dve.wait_ge(gain3_in, 32)
            dve.wait_ge(v_free, JG // 2 * 4 + 4)
            norm(ACC, X[:, 0:D], GAIN_G, GAIN_B, dve_tick).then_inc(y_ready, 1)
            dve.wait_ge(acc_ready, 2)
            with dve.Fori(GROUPS // 4, GROUPS // 2 - 1) as i:
                both(i, 1)
            both(GROUPS // 2 - 1, 1, after=None)
            dve.wait_ge(v_free, JG * 4 + 4)
            norm(ACC, X[:, D:2 * D], GAIN_G, GAIN_B, dve_tick).then_inc(y_ready, 1)
            add_dense((2 * GROUPS - 1) * NW, QUAD)
            dve.wait_ge(x_added, GROUPS * 8 + 4)
            for b in (2, 3):
                norm(X[:, b * D:(b + 1) * D], X[:, b * D:(b + 1) * D], GAIN_G, GAIN_B, dve_tick).then_inc(y_ready, 1)


def kernel(**a):
    import concourse.bacc as bacc
    from concourse.bass_utils import run_bass_kernel_spmd as run

    def f(name):
        return np.asarray(a[name])

    def tiles(w):
        k, n = w.shape[0] // P, w.shape[1]
        t = w.reshape(k, P, n).transpose(1, 0, 2).reshape(P, k * n)
        return t.reshape(P, -1, TW).transpose(1, 0, 2)

    def columns(v):
        return v.reshape(-1, P).T

    w_in, w_uq, w_ukv, w_out = f("w_in")[0], f("w_uq")[0], f("w_ukv")[0], f("w_out")[0]
    kpe = w_in[:, CKV:KPE]
    swap = np.concatenate([kpe[:, ROPE // 2:], kpe[:, :ROPE // 2]], 1)
    once = [tiles(f("w_mk")[0][:, h * P:(h + 1) * P]) for h in range(MH)] + [tiles(f("w_mv")[0])]
    for n in range(0, NL, 2):
        for first in (KPE, LRUX):
            for m in (n, n + 1):
                once.append(tiles(w_in[:, first + m * P:first + (m + 1) * P]))
    for first in (CQ, 0):
        for j in range(4):
            once.append(tiles(w_in[:, first + j * P:first + (j + 1) * P]))
    once += [tiles(np.concatenate([kpe, kpe], 1)), tiles(np.concatenate([swap, swap], 1))]
    ukv = w_ukv.reshape(LORA, HEADS, 2 * P)
    for h in range(0, HEADS, 2):
        once.append(np.concatenate([ukv[:, h + e, :P].reshape(4, P, P).transpose(1, 0, 2).reshape(1, P, 512)
                                    for e in range(2)], 2))
    v_cols = ukv[:, :, P:].reshape(LORA, HEADS * P)
    once += [tiles(v_cols[:, half * 512:(half + 1) * 512]) for half in range(2)]
    once += [tiles(w_out[:, c * 512:(c + 1) * 512]) for c in range(4)]
    w_once = np.concatenate(once, 0)
    w_mo, w_pq = f("w_mo")[0], f("w_pq")[0]
    w_block = np.concatenate([tiles(f("w_mq")[0])] + [tiles(w_mo[:, c * 512:(c + 1) * 512]) for c in range(4)]
                             + [tiles(w_pq[:, c * 512:(c + 1) * 512]) for c in range(4)], 0)
    uq = w_uq.reshape(4, P, HEADS, NOPE + ROPE).transpose(1, 2, 0, 3)
    pairs = []
    for h in range(0, HEADS, 2):
        half = ROPE // 2
        pe = np.concatenate([uq[:, h, :, NOPE:], uq[:, h + 1, :, NOPE:]], 2)
        sw = np.concatenate([uq[:, h + e, :, NOPE + o:NOPE + o + half] for e in range(2) for o in (half, 0)], 2)
        pairs.append(np.stack([uq[:, h, :, :NOPE], uq[:, h + 1, :, :NOPE], pe, sw], 1).reshape(P, 2048))
    wa, wx = f("lru_wa")[0], f("lru_wx")[0]
    lru_w = np.stack([wa[0], wa[1], wx[0], wx[1]], 1).transpose(0, 2, 1, 3).reshape(NL, P, 4 * P)
    part = np.arange(P) % ROPE
    freq = np.float32(10000.0) ** (-(np.arange(0, ROPE, 2, dtype=np.float32)) / np.float32(ROPE))
    consts = np.stack([freq[part % (ROPE // 2)], np.where(part < ROPE // 2, -1.0, 1.0)], 1).astype(np.float32)
    cols = np.concatenate([columns(f(n)[0]) for n in ("conv_w", "conv_b", "lru_ba", "lru_bx", "lru_lambda", "q_norm_g",
                                                      "kv_norm_g", "attn_out_g", "lru_out_g")] + [consts], 1)
    arrays = {
        "x": f("x")[0],
        "memT": f("mem")[0].T.reshape(KT, P, MEM).transpose(1, 0, 2).reshape(P, KT * MEM),
        "pos": f("positions")[0],
        "cols": cols, "w_once": w_once, "w_block": w_block, "wq_pairs": np.stack(pairs), "lru_w": lru_w,
        "keysT": np.concatenate([f("sub_keys1")[0].T, f("sub_keys2")[0].T], 1),
        "gains": np.stack([f("in_ln_g"), f("in_ln_b"), f("ln1_g")[0], f("ln1_b")[0], f("ln2_g")[0], f("ln2_b")[0],
                           f("ln3_g")[0], f("ln3_b")[0]]),
        "peer_u": f("peer_u")[0], "peer_v": f("peer_v")[0],
        "peer_ut": f("peer_u")[0].reshape(P, P, 2, 8, P).transpose(0, 2, 4, 3, 1).reshape(2 * P, P, TW),
    }
    arrays = {k: np.ascontiguousarray(v) for k, v in arrays.items()}
    nc = bacc.Bacc("TRN2", target_bir_lowering=False, num_devices=1)
    args = [nc.dram_tensor(k, v.shape, mybir.dt.from_np(v.dtype), kind="ExternalInput").ap() for k, v in arrays.items()]
    out = nc.dram_tensor("y", (S, D), F32, kind="ExternalOutput").ap()
    gates_d = nc.dram_tensor("dense_gates", (DT // TG, P, NK * TG), F32, kind="Internal").ap()
    build(nc, *args, gates_d, out)
    r = run(nc, [arrays], core_ids=[0])
    return r.results[0]["y"].reshape(1, S, D)
```

```python
import math
from contextlib import ExitStack

import numpy as np

import concourse.bass as bass
from concourse import mybir

F32 = mybir.dt.float32
I32 = mybir.dt.int32
U32 = mybir.dt.uint32
ALU = mybir.AluOpType
ACT = mybir.ActivationFunctionType
AX = mybir.AxisListType.X

P = 128
D = 2048
S = 512
NB = S // P
KT = D // P
MEM = 256
MH = 4
HEADS = 8
NOPE = 128
ROPE = 64
LORA = 512
LW = 1024
NL = LW // P
PH = 8
NK = 128
TOPK = 16
HK = PH * TOPK
CQ, CKV, KPE, LRUX = 512, 1024, 1088, 2112
ALPHA = 2.0 ** 0.25
LN_EPS = 1e-5
RMS_EPS = 1e-6
ATT_SCALE = (NOPE + ROPE) ** -0.5
MEM_SCALE = 128.0 ** -0.5

TW = 1024
NW = 8
BANK = 512
ARENA = 53 * 1000

C_CONVW, C_CONVB, C_BA, C_BX, C_LAM, C_QG, C_KVG, C_AG, C_LG, C_FREQ, C_SIGN = 0, 32, 40, 56, 72, 88, 92, 96, 104, 112, 113
NCOL = 114

TWO_PI_A = 6.28125
TWO_PI_B = float(np.float32(round((2 * math.pi - TWO_PI_A) * 2 ** 20) / 2 ** 20))
TWO_PI_C = float(2 * math.pi - TWO_PI_A - TWO_PI_B)
ROUND = 12582912.0

SCORE_BANKS = [4, 5, 2, 3]

QUAD = [0, 1, 2, 3]
PE_ORDER = ([f"x1T{q}" for q in QUAD] + ["q", "qT", "sc", "pT", "pv"] + [f"wo{c}" for c in QUAD]
            + [f"x2T{q}" for q in QUAD]
            + ["pq0", "pq1", "pqT0", "key0", "pq2", "pqT1", "key1", "pq3", "pqT2", "key2", "pqT3", "key3"])
TILES_AT = {"q": 8, "wo0": 10, "wo1": 12, "wo2": 14, "wo3": 16, "pq0": 24, "pq1": 32, "pq2": 40, "pq3": 48}
PE_STEPS = [n for n in PE_ORDER if n not in TILES_AT]
ACT_STEPS = (["xs"] + [f"x1T{q}" for q in QUAD] + ["q", "qT", "exp", "pT", "pv"] + [f"x2T{q}" for q in QUAD]
             + ["keep", "pq0", "pq1", "pqT0", "key0", "pq2", "pqT1", "key1", "pq3", "pqT2", "key2", "pqT3", "key3"])
DVE_STEPS = ["max", "prob"] + [f"wo{c}" for c in QUAD] + ["x2"]
PE_AT = {n: k + 1 for k, n in enumerate(PE_STEPS)}
ACT_AT = {n: k + 1 for k, n in enumerate(ACT_STEPS)}
DVE_AT = {n: k + 1 for k, n in enumerate(DVE_STEPS)}

DB = 2
DT = DB * P
ET = 4
GROUPS = P // ET
JG = (NB - DB) * HK // 4
JB = HK // 4
TG = 32
JE, JM, JD = 4, 4, 6
J0 = JE * (NB - 1) + JM
STEPS = [[0, 1], [2], [3, 4], [5]]
assert J0 + JD * GROUPS // 4 == JG
HC = PH // 4
CH = HC * TOPK


class InOrder:

    def __init__(self, eng, sem):
        self.eng, self.sem, self.base, self.k, self.outer = eng, sem, 0, 0, []

    def __call__(self, ins, tick=None):
        ins.then_inc(self.sem, 1)
        self.k += 1
        self.eng.wait_ge(self.sem, self.base + self.k)
        if tick is not None:
            self.eng.sem_inc(tick, 1)

    def enter(self, i, per):
        self.outer.append((self.base + self.k, per))
        self.base, self.k = self.base + self.k + i * per, 0

    def leave(self, count):
        start, per = self.outer.pop()
        assert self.k == per, (self.k, per)
        self.base, self.k = start + count * per, 0


def build(nc, x, memT, pos, cols_d, w_once, w_block, wq_pairs, lru_w, keysT, gains, peer_u, peer_v, peer_ut,
          gates_d, out):
    N_ONCE = w_once.shape[0]
    N_BLOCK = w_block.shape[0]
    DENSE0 = N_ONCE + NB * N_BLOCK
    with ExitStack() as ctx:
        def sem(name):
            return ctx.enter_context(nc.semaphore(name))

        base = nc.sbuf_base
        arena = ctx.enter_context(nc.sbuf_tensor("arena", [P, ARENA], F32))
        at0 = [0]
        at_of = {}

        def place(name, cols, at=None, dt=F32):
            at = at0[0] if at is None else at
            at0[0] = at + cols
            at_of[name] = at
            assert at + cols <= ARENA
            v = arena[:, at:at + cols]
            return v if dt == F32 else v.bitcast(dt)

        X = place("X", NB * D, 0)
        A = place("A", KT * S, 8192)
        KN, V = A[:, 0:4096], A[:, 4096:8192]
        U_RING = A
        Y = place("Y", KT * S, 16384)
        MEMT = Y[:, 0:KT * MEM]
        V_RING = Y
        W = place("W", NW * TW, 24576)
        KM = place("KM", MH * MEM, 32768)
        VM = place("VM", 2 * 512, 33792)
        WD = [place(f"wd{e}", ET * DT, 32768 + e * ET * DT) for e in range(2)]
        C = place("C", 8 * S, 34816)
        GAIN_G, GAIN_B = C[:, 0:D], C[:, D:2 * D]
        GAIN1_G, GAIN1_B = A[:, 0:D], A[:, D:2 * D]
        at0[0] = 38912
        COLS = place("cols", NCOL)
        IDENT = place("ident", P)
        ONES = place("ones", P)
        KEYS = place("keys", 2 * NK)
        IOTA = place("iota", NK)
        C4 = place("c4", 16)
        SM = place("small", 256)
        IU = [place(f"iu{e}", 4, dt=I32) for e in range(2)]
        IV = [place(f"iv{e}", 4, dt=I32) for e in range(2)]
        DOT = [place(f"dot{e}", 4) for e in range(2)]
        GEL = [place(f"gel{e}", 4) for e in range(2)]
        AV = [place(f"act{e}", 4) for e in range(2)]
        SC = at0[0]
        COS, SINS, KR = (place(n, S) for n in ("cos", "sins", "kr"))
        RS = place("rs", S)
        SQ = [place(f"sq{e}", S) for e in range(2)]
        TMP, TMP2 = place("tmp", S), place("tmp2", S)
        SC2 = at0[0]
        LX = [place(f"lx{e}", S + 4) for e in range(2)]
        XC1 = [place(f"xc{e}", S) for e in range(2)]
        LWT = [place(f"lw{e}", 4 * P) for e in range(2)]
        R_ = [place(f"r{d}", S) for d in range(2)]
        I_ = [place(f"i{d}", S) for d in range(2)]
        D_ = [place(f"d{d}", S) for d in range(2)]
        H_ = [place(f"h{d}", S) for d in range(2)]
        at0[0] = SC2
        WQ = place("wq", 2048)
        QN = [place(f"qn{e}", S) for e in range(2)]
        QR = place("qr", S)
        PM = [place(f"pm{e}", S) for e in range(4)]
        PT = place("pt", 4 * S)
        VH = [place(f"vh{e}", 4 * P) for e in range(2)]
        at0[0] = SC
        XC = place("xc", D)
        XT = place("xT", D)
        PR, PRT = place("pr", 1024), place("prT", 1024)
        QB = [PR[:, e * 512:(e + 1) * 512] for e in range(2)]
        QT, OT = PRT[:, 0:512], PRT[:, 512:1024]
        SK = [place(f"key scores{e}", 512) for e in range(2)]
        CAND = place("cand", CH * TOPK)
        EQ = CAND
        TV = place("top values", 2 * CH)
        TI = place("top index", 2 * CH, dt=U32)
        TIF = place("top index as float", 2 * CH)
        CP = place("chosen places", CH, dt=U32)
        CA = place("first part", CH, dt=U32)
        CB = place("second part", CH, dt=U32)
        CAF, CBF = place("caf", CH), place("cbf", CH)
        S1, S2 = place("s1", CH), place("s2", CH)
        CV, GATE = place("chosen sums", HK), place("gate", HK)
        IDX4 = place("idx", NB * HK, dt=I32)
        GATE4 = place("gates", NB * HK)
        S14, S24 = place("first keys", NB * HK), place("second keys", NB * HK)
        ACC = place("acc", D)
        XT2 = place("xT dense", DB * D, SC)
        TB = arena[:, at_of["first keys"]:at_of["first keys"] + 3 * DT]
        WS = [place("ws0", NK * TG, 34816), place("ws1", NK * TG, at_of["pr"])]
        assert at0[0] <= at_of["idx"]
        OH = [place(f"one-hot{e}", 4 * 2 * NK, 32768 + e * 1024) for e in range(2)]
        at0[0] = at_of["pr"]
        G = [place(f"g{e}", ET * DT) for e in range(2)]
        GL = place("gelu", ET * DT)

        STATS, MV, RSTD, NEWTON = SM[:, 0:24], SM[:, 24:26], SM[:, 26:27], SM[:, 27:28]
        MX, NMX, RSUM, RINV = SM[:, 32:36], SM[:, 36:40], SM[:, 40:44], SM[:, 44:48]
        LM = [SM[:, 64 + 16 * k:80 + 16 * k] for k in range(6)]
        GS, GR = SM[:, 48:56], SM[:, 56:64]
        MX2 = [SM[:, 160 + 8 * e:161 + 8 * e] for e in range(4)]
        NM2 = [SM[:, 161 + 8 * e:162 + 8 * e] for e in range(4)]
        RSM2 = [SM[:, 162 + 8 * e:163 + 8 * e] for e in range(4)]
        RI2 = [SM[:, 163 + 8 * e:164 + 8 * e] for e in range(4)]

        ps = ctx.enter_context(nc.psum_tensor("ps", [P, 8, BANK], F32))

        def bank(k, n=BANK):
            return ps[:, k, 0:n]

        def col(k):
            return COLS[:, k:k + 1]

        consts_set = sem("consts_set")
        consts2_set = sem("consts2_set")
        cols_in = sem("cols_in")
        keys_in = sem("keys_in")
        x_in = [sem(f"x_in{b}") for b in range(NB)]
        mem_in = sem("mem_in")
        pos_in = sem("pos_in")
        gain0_in, gain1_in, gain2_in, gain3_in = (sem(f"gain{k}_in") for k in range(4))
        w_full = [sem(f"w_full{s}") for s in range(NW)]
        w_used = sem("w_used")
        mem_ev = sem("mem_ev")
        ln0_done = sem("ln0_done")
        x0T_mm, x0T_ev = sem("x0T_mm"), sem("x0T_ev")
        lw_full = [sem(f"lw_full{e}") for e in range(2)]
        r_mm = sem("r_mm")
        xbank_free, gbank_free, rbank_free = sem("xbank_free"), sem("gbank_free"), sem("rbank_free")
        conv_done, lru_done, u_ready = sem("conv_done"), sem("lru_done"), sem("u_ready")
        tanh_done, lam_abs, lam_exp = sem("tanh_done"), sem("lam_abs"), sem("lam_exp")
        angle, rope_tab = sem("angle"), sem("rope_tab")
        l2_ev = sem("l2_ev")
        rms_sq, rms_mm, rms_done = sem("rms_sq"), sem("rms_mm"), sem("rms_done")
        kr_done = sem("kr_done")
        kv_ev = sem("kv_ev")
        wq_full = sem("wq_full")
        qpe_mm, qn_mm, qn_ev, qr_done = sem("qpe_mm"), sem("qn_mm"), sem("qn_ev"), sem("qr_done")
        s_mm, nmx_done, exp_done, p_done = sem("s_mm"), sem("nmx_done"), sem("exp_done"), sem("p_done")
        t_mm, pt_ev, pv_mm, o_ev, vh_done = sem("t_mm"), sem("pt_ev"), sem("pv_mm"), sem("o_ev"), sem("vh_done")
        o_added = sem("o_added")
        ln1_done = sem("ln1_done")
        e_mm, e_ev, e_dv = sem("e_mm"), sem("e_ev"), sem("e_dv")
        u_full = [sem(f"u_full{s}") for s in range(4)]
        v_full = [sem(f"v_full{s}") for s in range(4)]
        u_free, v_free = sem("u_free"), sem("v_free")
        gel_done, act_done = sem("gel_done"), sem("act_done")
        sk_free, top_done, gate_exp, routed = sem("sk_free"), sem("top_done"), sem("gate_exp"), sem("routed")
        tb_mm, tb_ev, xt_mm, xt_ev, scaled = sem("tb_mm"), sem("tb_ev"), sem("xt_mm"), sem("xt_ev"), sem("scaled")
        oh_ready, oh_free, ws_ev, ws_free = sem("oh_ready"), sem("oh_free"), sem("ws_ev"), sem("ws_free")
        gates_out = sem("gates_out")
        wd_in = [sem(f"wd_in{e}") for e in range(2)]
        gl_done, g_ready, x_added, acc_ready = sem("gl_done"), sem("g_ready"), sem("x_added"), sem("acc_ready")
        y_ready, y_out = sem("y_ready"), sem("y_out")
        iu_set, iv_set, pool_tick = sem("iu_set"), sem("iv_set"), sem("pool_tick")
        dve_done, dve_tick, act_tick = sem("dve_done"), sem("dve_tick"), sem("act_tick")

        block = ctx.enter_context(nc.Block())

        @block.sync
        def _(sp):
            sp.sem_inc(ws_free, 2)
            sp.dma_start(COLS, cols_d).then_inc(cols_in, 16)
            sp.dma_start(MEMT, memT).then_inc(mem_in, 16)
            for s in range(NW):
                sp.dma_start(W[:, s * TW:(s + 1) * TW], w_once[s]).then_inc(w_full[s], 16)
            for b in range(NB):
                sp.dma_start(X[:, b * D:(b + 1) * D], x[b * P:(b + 1) * P, :]).then_inc(x_in[b], 16)
                if b == 0:
                    sp.dma_start(GAIN_G, gains[0:1, :].partition_broadcast(P)).then_inc(gain0_in, 16)
                    sp.dma_start(GAIN_B, gains[1:2, :].partition_broadcast(P)).then_inc(gain0_in, 16)
            sp.dma_start(KEYS, keysT).then_inc(keys_in, 16)
            sp.dma_start(TMP.bitcast(I32), pos.partition_broadcast(P)).then_inc(pos_in, 16)
            with sp.Fori(1, N_ONCE // NW) as i:
                for s in range(NW):
                    sp.wait_ge(w_used, i * NW + (s - NW + 1))
                    sp.dma_start(W[:, s * TW:(s + 1) * TW],
                                 w_once[bass.ds(i * NW + s, 1), :, :].rearrange("t p n -> p (t n)")
                                 ).then_inc(w_full[s], 16)
            done = N_ONCE // NW * NW
            for t in range(done, N_ONCE):
                sp.wait_ge(w_used, t - NW + 1)
                sp.dma_start(W[:, (t - done) * TW:(t - done + 1) * TW], w_once[t]).then_inc(w_full[t - done], 16)
            with sp.Fori(0, NB) as b:
                with sp.Fori(0, N_BLOCK // NW) as i:
                    for k in range(NW):
                        s = (N_ONCE + k) % NW
                        sp.wait_ge(w_used, b * N_BLOCK + i * NW + (N_ONCE + k - NW + 1))
                        sp.dma_start(W[:, s * TW:(s + 1) * TW],
                                     w_block[bass.ds(i * NW + k, 1), :, :].rearrange("t p n -> p (t n)")
                                     ).then_inc(w_full[s], 16)

            def ring(k, before, src, split=False):
                s = (DENSE0 + k) % NW
                dst = W[:, s * TW:(s + 1) * TW]
                if split:
                    dst = dst.rearrange("p (t n) -> p t n", t=2)
                sp.wait_ge(w_used, before + (k - NW + 1))
                sp.dma_start(dst, src).then_inc(w_full[s], 16)

            def load_u(g, before):
                for k in range(NW):
                    ring(k, before, peer_ut[bass.ds(g * NW + k, 1), :, :].rearrange("t p n -> p (t n)"))

            def load_v(g, before):
                for k in range(NW):
                    c, m = k // 2, k % 2
                    ring(k, before, v_tiles[bass.ds(g * ET + 2 * m, 2), :, c * 512:(c + 1) * 512
                                            ].rearrange("t p n -> p t n"), True)

            def load_gates(g, par):
                sp.dma_start(WD[par].rearrange("p (g n) -> p g n", g=DT // TG),
                             gates_d[:, :, bass.ds(g * (ET * TG), ET * TG)].rearrange("g p n -> p g n")
                             ).then_inc(wd_in[par], 16)

            v_tiles = peer_v.rearrange("(t p) d -> t p d", p=P)
            load_u(0, DENSE0)
            load_u(1, DENSE0 + NW)
            load_v(0, DENSE0 + 2 * NW)
            with sp.Fori(0, DT // TG // 2) as i:
                for par in range(2):
                    sp.wait_ge(ws_ev, i * 16 + (par * 8 + 10))
                    sp.dma_start(gates_d[bass.ds(i * 2 + par, 1), :, :].rearrange("g p n -> p (g n)"), WS[par]
                                 ).then_inc(gates_out, 16)
                    sp.wait_ge(gates_out, i * 32 + (par * 16 + 16))
                    sp.sem_inc(ws_free, 1)
            load_gates(0, 0)
            load_gates(1, 1)
            sp.dma_start(GAIN_G, gains[6:7, :].partition_broadcast(P)).then_inc(gain3_in, 16)
            sp.dma_start(GAIN_B, gains[7:8, :].partition_broadcast(P)).then_inc(gain3_in, 16)
            with sp.Fori(1, GROUPS // 2) as i:
                for par in range(2):
                    g = i * 2 + par
                    sp.wait_ge(g_ready, g)
                    load_gates(g, par)
                    load_u(g, i * (4 * NW) + (DENSE0 - NW + par * 2 * NW))
                    load_v(g - 1, i * (4 * NW) + (DENSE0 + par * 2 * NW))
            load_v(GROUPS - 1, DENSE0 + (2 * GROUPS - 1) * NW)
            for b in range(NB):
                sp.wait_ge(y_ready, b + 1)
                sp.dma_start(out[b * P:(b + 1) * P, :], X[:, b * D:(b + 1) * D]).then_inc(y_out, 16)
            sp.wait_ge(y_out, 16 * NB)

        @block.gpsimd
        def _(pool):
            pool.memset(IDENT, 0.0).then_inc(consts_set, 1)
            pool.memset(ONES, 1.0).then_inc(consts_set, 1)
            for e in range(2):
                pool.memset(LX[e], 0.0).then_inc(consts_set, 1)
            pool.iota(IOTA, pattern=[[1, NK]], base=0, channel_multiplier=0,
                      allow_small_or_imprecise_dtypes=True).then_inc(consts_set, 1)
            pool.wait_ge(consts_set, 5)
            pool.affine_select(out=IDENT, in_=IDENT, compare_op=ALU.not_equal, fill=1.0, base=0,
                               pattern=[[-1, P]], channel_multiplier=1).then_inc(consts2_set, 1)
            for n in range(NL):
                if n >= 2:
                    pool.wait_ge(r_mm, n - 1)
                pool.dma_start(LWT[n % 2], lru_w[n]).then_inc(lw_full[n % 2], 16)
            pool.wait_ge(lru_done, NL + 1)
            pool.dma_start(WQ, wq_pairs[0]).then_inc(wq_full, 16)
            pool.wait_ge(kv_ev, 16)

            def copy_v(hp):
                for e in range(2):
                    pool.wait_ge(pv_mm, hp * 2 + (e + 1))
                    pool.sem_inc(pool_tick, 1)
                    pool.tensor_copy(VH[e].rearrange("p (t v) -> p t v", t=4),
                                     V.rearrange("p (t w) -> p t w", t=4)[:, :, bass.ds(hp * 256 + e * P, P)]
                                     ).then_inc(vh_done, 1)

            with pool.Fori(0, HEADS // 2 - 1) as hp:
                copy_v(hp)
                pool.wait_ge(qn_mm, hp * 2 + 2)
                pool.sem_inc(pool_tick, 1)
                pool.dma_start(WQ, wq_pairs[bass.ds(hp + 1, 1), :, :].rearrange("a p n -> p (a n)")
                               ).then_inc(wq_full, 16)
            copy_v(HEADS // 2 - 1)
            pool.wait_ge(qn_mm, HEADS)
            pool.dma_start(GAIN_G, gains[4:5, :].partition_broadcast(P)).then_inc(gain2_in, 16)
            pool.dma_start(GAIN_B, gains[5:6, :].partition_broadcast(P)).then_inc(gain2_in, 16)
            pool.wait_ge(pv_mm, HEADS + 2)
            pool.dma_start(GAIN1_G, gains[2:3, :].partition_broadcast(P)).then_inc(gain1_in, 16)
            pool.dma_start(GAIN1_B, gains[3:4, :].partition_broadcast(P)).then_inc(gain1_in, 16)

            def index(dst, j, ready, n):
                pool.tensor_copy(dst, IDX4[:, bass.ds(j * 4, 4)]).then_inc(ready, 1)
                pool.wait_ge(ready, n)
                pool.sem_inc(pool_tick, 1)

            def row(ring, table, idx, s, full, free, need):
                pool.wait_ge(free, need)
                pool.sem_inc(pool_tick, 1)
                pool.indirect_dma_start(ring[:, s * D:(s + 1) * D], None, table,
                                        bass.IndirectOffsetOnAxis(ap=idx[:, s:s + 1], axis=0)
                                        ).then_inc(full[s], 16)

            def rows(j, par, last=False):
                if not last:
                    index(IU[1 - par], j + 1, iu_set, j + 2)
                index(IV[par], j, iv_set, j + 1)
                for s in range(4):
                    if not last:
                        row(U_RING, peer_u, IU[1 - par], s, u_full, u_free, j * 4 + (s + 5))
                    row(V_RING, peer_v, IV[par], s, v_full, v_free, j * 4 + (s + 1))

            pool.wait_ge(routed, 1)
            index(IU[0], 0, iu_set, 1)
            for s in range(4):
                row(U_RING, peer_u, IU[0], s, u_full, u_free, s + 1)
            with pool.Fori(0, JG // 2 - 1) as i:
                for par in range(2):
                    rows(i * 2 + par, par)
            rows(JG - 2, 0)
            rows(JG - 1, 1, last=True)

        @block.tensor
        def _(pe):
            def tile_wait(t, ahead=0):
                pe.wait_ge(w_full[t % NW], ahead * (16 // NW) + 16 * (t // NW + 1))

            def tile(t):
                return W[:, (t % NW) * TW:(t % NW + 1) * TW]

            pe.sem_inc(t_mm, 4)
            pe.sem_inc(pv_mm, 2)
            pe.sem_inc(oh_free, 2)
            pe.wait_ge(mem_in, 16)
            t = 0
            for h in range(MH):
                for half in range(2):
                    tile_wait(t)
                    for k in range(8):
                        kt = half * 8 + k
                        last = pe.matmul(bank(h, MEM), tile(t)[:, k * P:(k + 1) * P], MEMT[:, kt * MEM:(kt + 1) * MEM],
                                         start=(kt == 0), stop=(kt == KT - 1))
                    last.then_inc(w_used, 1)
                    t += 1
            for j in range(8):
                tile_wait(t)
                for m in range(2):
                    for k in range(2):
                        kt = 2 * j + k
                        last = pe.matmul(bank(4 + m), MEMT[:, kt * MEM + m * P:kt * MEM + (m + 1) * P],
                                         tile(t)[:, k * 512:(k + 1) * 512], start=(kt == 0), stop=(kt == KT - 1))
                last.then_inc(w_used, 1)
                t += 1
            pe.wait_ge(consts2_set, 1)
            for b in range(NB):
                pe.wait_ge(ln0_done, b + 1)
                for q in range(4):
                    n = 4 * b + q
                    if n >= 2:
                        pe.wait_ge(x0T_ev, n - 1)
                    for k in range(4):
                        kt = 4 * q + k
                        last = pe.transpose(ps[:, 6 + n % 2, k * P:(k + 1) * P],
                                            X[:, b * D + kt * P:b * D + (kt + 1) * P], IDENT)
                    last.then_inc(x0T_mm, 1)
            pe.wait_ge(x0T_ev, 4 * NB)
            pe.wait_ge(mem_ev, 6)

            def from_x0(out_ap, t, ahead):
                for half in range(2):
                    tile_wait(t + half, ahead)
                    for k in range(8):
                        kt = half * 8 + k
                        last = pe.matmul(out_ap, tile(t + half)[:, k * P:(k + 1) * P], A[:, kt * S:(kt + 1) * S],
                                         start=(kt == 0), stop=(kt == KT - 1))
                    last.then_inc(w_used, 1)

            with pe.Fori(0, NL // 2) as i:
                for e in range(2):
                    pe.wait_ge(xbank_free, i * 2 + (e + 1))
                    from_x0(bank(e), t + 2 * e, i * 8)
                for e in range(2):
                    pe.wait_ge(gbank_free, i * 2 + (e + 1))
                    from_x0(bank(2 + e), t + 4 + 2 * e, i * 8)
                    pe.wait_ge(conv_done, i * 2 + (e + 3))
                    pe.wait_ge(rbank_free, i * 2 + (e + 1))
                    pe.wait_ge(lw_full[e], i * 16 + 16)
                    for q in range(4):
                        last = pe.matmul(bank(4 + q), LWT[e][:, q * P:(q + 1) * P], XC1[e], start=True, stop=True)
                    last.then_inc(r_mm, 1)
            t += 8 * (NL // 2)
            pe.wait_ge(xbank_free, NL + 2)
            pe.wait_ge(gbank_free, NL + 2)
            pe.wait_ge(rbank_free, NL + 1)
            with pe.Fori(0, 2) as i:
                for j in range(4):
                    from_x0(ps[:, bass.ds(i * 4 + j, 1), :].rearrange("p a n -> p (a n)"), t + 2 * j, i * 8)
            t += 16
            pe.wait_ge(l2_ev, 2)
            for j in range(2):
                from_x0(bank(j), t + 2 * j, 0)
            t += 4

            def squares(first, count, b):
                for r in range(count):
                    pe.wait_ge(rms_sq, first + r + 1)
                    pe.matmul(bank(b), ONES, SQ[(first + r) % 2], start=(r == 0), stop=(r == count - 1)
                              ).then_inc(rms_mm, 1)

            pe.wait_ge(l2_ev, 8)
            squares(0, 4, 2)
            squares(4, 4, 3)
            pe.wait_ge(rms_done, 1)
            for hh in range(HEADS // 2):
                if hh >= 2:
                    pe.wait_ge(kv_ev, 2 * hh - 2)
                tile_wait(t)
                for e in range(2):
                    for k in range(4):
                        last = pe.matmul(bank(4 + (2 * hh + e) % 4), tile(t)[:, e * 512 + k * P:e * 512 + (k + 1) * P],
                                         C[:, k * S:(k + 1) * S], start=(k == 0), stop=(k == 3))
                last.then_inc(w_used, 1)
                t += 1
            pe.wait_ge(rms_done, 2)
            pe.wait_ge(kr_done, 1)
            for half in range(2):
                if half:
                    pe.wait_ge(kv_ev, 12)
                for j in range(2):
                    tile_wait(t)
                    for b in range(NB):
                        for k in range(2):
                            kt = 2 * j + k
                            last = pe.matmul(bank(b), C[:, kt * S + b * P:kt * S + (b + 1) * P],
                                             tile(t)[:, k * 512:(k + 1) * 512], start=(kt == 0), stop=(kt == 3))
                    last.then_inc(w_used, 1)
                    t += 1
            pe.wait_ge(kv_ev, 16)
            squares(8, 8, 7)
            with pe.Fori(0, HEADS // 2) as hp:
                pe.wait_ge(wq_full, hp * 16 + 16)
                pe.wait_ge(qr_done, hp + 1)
                pe.wait_ge(o_ev, hp * 2 + 2)
                for part, done in ((2, None), (3, qpe_mm), (0, qn_mm), (1, qn_mm)):
                    for k in range(4):
                        last = pe.matmul(bank(part), WQ[:, part * 512 + k * P:part * 512 + (k + 1) * P],
                                         C[:, (4 + k) * S:(5 + k) * S], start=(k == 0), stop=(k == 3))
                    if done is not None:
                        last.then_inc(done, 1)

                def scores(n):
                    e, qb = n // 4, n % 4
                    to = bank(SCORE_BANKS[n % 4])
                    pe.wait_ge(exp_done, hp * 8 + (n + 1))
                    if n == 0:
                        pe.wait_ge(qr_done, hp + 2)
                        pe.wait_ge(qn_ev, hp * 2 + 1)
                    if n == 4:
                        pe.wait_ge(qn_ev, hp * 2 + 2)
                    pe.matmul(to, QN[e][:, qb * P:(qb + 1) * P], KN[:, bass.ds(hp * 1024 + e * S, S)],
                              start=True, stop=False)
                    pe.matmul(to, QR[e * 64:(e + 1) * 64, qb * P:(qb + 1) * P],
                              KR[e * 64:(e + 1) * 64, :], start=False, stop=True).then_inc(s_mm, 1)

                def turn(n):
                    pe.wait_ge(p_done, hp * 8 + (n + 1))
                    pe.wait_ge(pt_ev, hp * 8 + (n + 1))
                    if n == 1:
                        pe.wait_ge(rms_done, 3)
                    for k in range(4):
                        last = pe.transpose(ps[:, 6 + n % 2, k * P:(k + 1) * P], PM[n % 4][:, k * P:(k + 1) * P], IDENT)
                    last.then_inc(t_mm, 1)

                def values(e):
                    pe.wait_ge(pt_ev, hp * 8 + (4 * e + 6))
                    pe.wait_ge(vh_done, hp * 2 + (e + 1))
                    for k in range(4):
                        last = pe.matmul(bank(e), VH[e][:, k * P:(k + 1) * P], PT[:, k * S:(k + 1) * S],
                                         start=(k == 0), stop=(k == 3))
                    last.then_inc(pv_mm, 1)

                pe.wait_ge(qn_ev, hp * 2 + 2)
                scores(0)
                scores(1)
                for n in range(2, 8):
                    scores(n)
                    turn(n - 2)
                    if n == 5:
                        values(0)
                turn(6)
                turn(7)
                values(1)
            squares(16, 8, 7)
            pe.wait_ge(o_ev, HEADS + 2)
            with pe.Fori(0, 2) as i:
                for cc in range(2):
                    pe.wait_ge(o_added, i * 8 + (4 * cc + 4))
                    for j in range(8):
                        if j == 4:
                            pe.wait_ge(rms_done, 4)
                        tile_wait(t + 8 * cc + j, i * 16)
                        for b in range(NB):
                            for k in range(2):
                                kt = (2 * j + k + NL) % KT
                                last = pe.matmul(bank(4 * cc + b), Y[:, kt * S + b * P:kt * S + (b + 1) * P],
                                                 tile(t + 8 * cc + j)[:, k * 512:(k + 1) * 512],
                                                 start=(kt == NL), stop=(kt == NL - 1))
                        last.then_inc(w_used, 1)
            t += 32
            assert t == N_ONCE

            with pe.Fori(0, NB) as b:
                def did(ins, name):
                    ins.then_inc(e_mm, 1)
                    order.append(name)

                def seen(name):
                    pe.wait_ge(e_ev, b * len(ACT_STEPS) + ACT_AT[name])

                def told(name):
                    pe.wait_ge(e_dv, b * len(DVE_STEPS) + DVE_AT[name])

                order = []
                tt = [N_ONCE]

                def wtile():
                    tile_wait(tt[0], b * N_BLOCK)
                    return tile(tt[0])

                def used(ins):
                    ins.then_inc(w_used, 1)
                    tt[0] += 1

                def turned(src, q, name):
                    for k in range(4):
                        kt = 4 * q + k
                        last = pe.transpose(ps[:, 4 + q, k * P:(k + 1) * P], src[:, kt * P:(kt + 1) * P], IDENT)
                    did(last, name)

                seen("xs")
                pe.wait_ge(o_added, 24)
                for q in QUAD:
                    turned(XC, q, f"x1T{q}")
                seen("x1T3")
                for name in PE_ORDER[4:]:
                    if name in ("q", "pq0", "pq1", "pq2", "pq3"):
                        if name == "pq0":
                            seen("x2T3")
                        if name == "pq2":
                            seen("pq0")
                        if name == "pq3":
                            seen("pq1")
                        to = 4 if name == "q" else 4 + int(name[2]) % 2
                        for j in range(8):
                            w = wtile()
                            for k in range(2):
                                kt = 2 * j + k
                                last = pe.matmul(bank(to), XT[:, kt * P:(kt + 1) * P], w[:, k * 512:(k + 1) * 512],
                                                 start=(kt == 0), stop=(kt == KT - 1))
                            used(last)
                    elif name == "qT" or name[:3] == "pqT":
                        c = 0 if name == "qT" else int(name[3])
                        seen("q" if name == "qT" else f"pq{c}")
                        if c:
                            seen(f"pqT{c - 1}")
                        for k in range(4):
                            last = pe.transpose(ps[:, 5 if name == "qT" else 6, k * P:(k + 1) * P],
                                                QB[c % 2][:, k * P:(k + 1) * P], IDENT)
                        did(last, name)
                    elif name == "sc":
                        seen("qT")
                        for h in range(MH):
                            last = pe.matmul(ps[:, 6 + h // 2, (h % 2) * MEM:(h % 2 + 1) * MEM],
                                             QT[:, h * P:(h + 1) * P], KM[:, h * MEM:(h + 1) * MEM],
                                             start=True, stop=True)
                        did(last, name)
                    elif name == "pT":
                        told("prob")
                        for n in range(8):
                            last = pe.transpose(ps[:, 4 + n // 4, (n % 4) * P:(n % 4 + 1) * P],
                                                PR[:, n * P:(n + 1) * P], IDENT)
                        did(last, name)
                    elif name == "pv":
                        seen("pT")
                        for h in range(MH):
                            for m in range(2):
                                last = pe.matmul(ps[:, 6, h * P:(h + 1) * P],
                                                 VM[:, m * 512 + h * P:m * 512 + (h + 1) * P],
                                                 PRT[:, (2 * h + m) * P:(2 * h + m + 1) * P],
                                                 start=(m == 0), stop=(m == 1))
                        did(last, name)
                    elif name[:2] == "wo":
                        c = int(name[2])
                        if c == 0:
                            seen("pv")
                        for j in range(2):
                            w = wtile()
                            for k in range(2):
                                kt = 2 * j + k
                                last = pe.matmul(bank(4 + c), OT[:, kt * P:(kt + 1) * P], w[:, k * 512:(k + 1) * 512],
                                                 start=(kt == 0), stop=(kt == 3))
                            used(last)
                    elif name[:3] == "x2T":
                        q = int(name[3])
                        if q == 0:
                            told("x2")
                        turned(XC, q, name)
                    elif name[:3] == "key":
                        c = int(name[3])
                        seen(f"pqT{c}")
                        if c:
                            seen(f"key{c - 1}")
                        for k in range(4):
                            last = pe.matmul(ps[:, 7, k * P:(k + 1) * P], QT[:, k * P:(k + 1) * P],
                                             KEYS[:, (k % 2) * NK:(k % 2 + 1) * NK], start=True, stop=True)
                        did(last, name)
                assert order == PE_STEPS and tt[0] == N_ONCE + N_BLOCK

            def dense_tile(k, before):
                t = DENSE0 + k
                pe.wait_ge(w_full[t % NW], before * (16 // NW) + (16 * (t // NW + 1)))
                return tile(t)

            xt2 = XT2.rearrange("p (b k t) -> p b k t", b=DB, k=KT)

            def all_u(g, par, before):
                pe.wait_ge(gl_done, g * 2 + 2)
                for et in range(ET):
                    for half in range(2):
                        w = dense_tile(2 * et + half, before)
                        for k in range(8):
                            kt = half * 8 + k
                            last = pe.matmul(ps[:, par * 2 + et // 2, (et % 2) * DT:(et % 2 + 1) * DT],
                                             w[:, k * P:(k + 1) * P], xt2[:, :, kt, :],
                                             start=(kt == 0), stop=(kt == KT - 1))
                        last.then_inc(w_used, 1)

            def all_v(g, par, before):
                pe.wait_ge(g_ready, g + 2)
                for c in QUAD:
                    pe.wait_ge(x_added, g * 8 + (2 * c + 2))
                    for m in range(2):
                        w = dense_tile(2 * c + m, before)
                        for tb in range(DB):
                            for t in range(2):
                                et = 2 * m + t
                                last = pe.matmul(bank(4 + (c % 2) * 2 + tb), G[par][:, et * DT + tb * P:et * DT + (tb + 1) * P],
                                                 w[:, t * 512:(t + 1) * 512], start=(et == 0), stop=(et == ET - 1))
                        last.then_inc(w_used, 1)

            pe.wait_ge(e_ev, NB * len(ACT_STEPS))
            for n in range(4 * DB):
                if n >= 4:
                    pe.wait_ge(xt_ev, n - 3)
                for k in range(4):
                    at = (NB - DB) * D + (4 * n + k) * P
                    last = pe.transpose(ps[:, n % 4, k * P:(k + 1) * P], X[:, at:at + P], IDENT)
                last.then_inc(xt_mm, 1)
            pe.wait_ge(xt_ev, 4 * DB)
            all_u(0, 0, 0)
            all_u(1, 1, NW)
            pe.wait_ge(routed, NB)
            for k, t4 in enumerate((S14, S24, GATE4)):
                for d in range(DB):
                    b = NB - DB + d
                    n = k * DB + d
                    last = pe.transpose(ps[:, 4 + n // 4, (n % 4) * P:(n % 4 + 1) * P], t4[:, b * HK:(b + 1) * HK], IDENT)
            last.then_inc(tb_mm, 1)
            with pe.Fori(0, DT // 8) as i:
                for h in range(2):
                    pe.wait_ge(oh_ready, i * 2 + (h + 1))
                    pe.wait_ge(ws_ev, i * 2 + (h + 1))
                    for k in range(4):
                        last = pe.matmul(ps[:, 6 + h, k * NK:(k + 1) * NK], OH[h][:, (4 + k) * NK:(5 + k) * NK],
                                         OH[h][:, k * NK:(k + 1) * NK], start=True, stop=True)
                    last.then_inc(oh_free, 1)

            all_v(0, 0, 2 * NW)
            with pe.Fori(1, GROUPS // 2) as i:
                for par in range(2):
                    all_u(i * 2 + par, par, i * (4 * NW) + (2 * par - 1) * NW)
                    all_v(i * 2 + par - 1, 1 - par, i * (4 * NW) + 2 * par * NW)
            all_v(GROUPS - 1, 1, (2 * GROUPS - 1) * NW)

        @block.scalar
        def _(act):
            def tick():
                act.sem_inc(act_tick, 1)

            def evict(dst, src):
                return act.activation(dst, src, ACT.Copy)

            act.sem_inc(xbank_free, 2)
            act.sem_inc(gbank_free, 2)
            act.sem_inc(rbank_free, 1)
            act.sem_inc(exp_done, 4)
            act.sem_inc(pt_ev, 2)
            act.sem_inc(o_ev, 2)
            act.sem_inc(gl_done, 4)
            act.sem_inc(ws_ev, 2)
            act.wait_ge(lam_abs, 1)
            act.activation(LM[1], LM[0], ACT.Exp, scale=-1.0).then_inc(lam_exp, 1)
            act.wait_ge(angle, 1)
            act.activation(SINS, RS, ACT.Sin, scale=col(C_SIGN))
            act.activation(COS, COS, ACT.Sin).then_inc(rope_tab, 1)
            for h in range(MH):
                act.wait_ge(w_used, 2 * (h + 1))
                evict(KM[:, h * MEM:(h + 1) * MEM], bank(h, MEM)).then_inc(mem_ev, 1)
            act.wait_ge(w_used, 16)
            for m in range(2):
                evict(VM[:, m * 512:(m + 1) * 512], bank(4 + m)).then_inc(mem_ev, 1)
            for n in range(4 * NB):
                b, q = n // 4, n % 4
                act.wait_ge(x0T_mm, n + 1)
                evict(A.rearrange("p (k s) -> p k s", k=KT)[:, 4 * q:4 * q + 4, b * P:(b + 1) * P],
                      bank(6 + n % 2).rearrange("p (k s) -> p k s", k=4)).then_inc(x0T_ev, 1)
            act.wait_ge(consts_set, 5)
            with act.Fori(0, NL // 2) as i:
                for e in range(2):
                    act.wait_ge(w_used, i * 8 + (16 + 2 * e + 2))
                    act.wait_ge(conv_done, i * 2 + (e + 1))
                    evict(LX[e][:, 2:2 + S], bank(e)).then_inc(xbank_free, 1)
                for e in range(2):
                    act.wait_ge(w_used, i * 8 + (20 + 2 * e + 2))
                    tick()
                    act.activation(Y[:, bass.ds(i * 1024 + (8 + e) * S, S)], bank(2 + e), ACT.Gelu
                                   ).then_inc(gbank_free, 1)
                    act.wait_ge(r_mm, i * 2 + (e + 1))
                    act.wait_ge(lru_done, i * 2 + (e + 1))
                    tick()
                    for q in range(4):
                        dst = (R_ + I_)[q]
                        first = C_BA if q < 2 else C_BX
                        last = act.activation(dst, bank(4 + q), ACT.Sigmoid,
                                              bias=COLS[:, bass.ds(i * 2 + (first + (q % 2) * NL + e), 1)])
                    last.then_inc(rbank_free, 1)
                    act.wait_ge(rbank_free, i * 2 + (e + 2))
                    tick()
                    for d in range(2):
                        last = act.activation(R_[d], R_[d], ACT.Tanh, scale=C4[:, bass.ds(i * 2 + (d * NL + e), 1)])
                    last.then_inc(tanh_done, 1)
                    act.wait_ge(tanh_done, i * 2 + (e + 1))
                    for d in range(2):
                        last = act.activation(H_[d], R_[d], ACT.Sqrt)
                    last.then_inc(u_ready, 1)
            with act.Fori(0, 2) as i:
                for j in range(4):
                    act.wait_ge(w_used, i * 8 + (48 + 2 * j + 2))
                    tick()
                    evict(C[:, bass.ds(i * 2048 + j * S, S)], ps[:, bass.ds(i * 4 + j, 1), :].rearrange("p a n -> p (a n)")
                          ).then_inc(l2_ev, 1)

            def squares(first, count, src):
                for r in range(first, first + count):
                    if r >= 2:
                        act.wait_ge(rms_mm, r - 1)
                    act.activation(SQ[r % 2], src[:, (r - first) * S:(r - first + 1) * S], ACT.Square
                                   ).then_inc(rms_sq, 1)

            act.wait_ge(l2_ev, 8)
            squares(0, 4, C)
            squares(4, 4, C[:, 4 * S:8 * S])
            for hh in range(HEADS // 2):
                act.wait_ge(w_used, 68 + hh + 1)
                for h in (2 * hh, 2 * hh + 1):
                    evict(KN[:, h * S:(h + 1) * S], bank(4 + h % 4)).then_inc(kv_ev, 1)
            for half in range(2):
                act.wait_ge(w_used, 72 + 2 * half + 2)
                for b in range(NB):
                    evict(V[:, b * 1024 + half * 512:b * 1024 + (half + 1) * 512], bank(b)).then_inc(kv_ev, 1)
            act.wait_ge(lru_done, NL + 1)
            squares(8, 8, Y[:, 8 * S:16 * S])
            with act.Fori(0, HEADS // 2) as hp:
                for e in range(2):
                    act.wait_ge(qn_mm, hp * 2 + (e + 1))
                    evict(QN[e], bank(e)).then_inc(qn_ev, 1)

                def exp(n):
                    act.wait_ge(nmx_done, hp * 8 + (n + 1))
                    act.wait_ge(t_mm, hp * 8 + (n + 1))
                    act.activation(PM[n % 4], bank(SCORE_BANKS[n % 4]), ACT.Exp, bias=NM2[n % 4], scale=ATT_SCALE,
                                   accum_out=RSM2[n % 4]).then_inc(exp_done, 1)

                def turned(n):
                    act.wait_ge(t_mm, hp * 8 + (n + 5))
                    if n % 4 == 0:
                        act.wait_ge(pv_mm, hp * 2 + (n // 4 + 2))
                    qb = n % 4
                    evict(PT.rearrange("p (k s) -> p k s", k=4)[:, :, qb * P:(qb + 1) * P],
                          bank(6 + n % 2).rearrange("p (k s) -> p k s", k=4)).then_inc(pt_ev, 1)

                def output(e):
                    act.wait_ge(pv_mm, hp * 2 + (e + 3))
                    tick()
                    evict(Y[:, bass.ds(hp * 1024 + e * S, S)], bank(e)).then_inc(o_ev, 1)

                exp(0)
                exp(1)
                for n in range(2, 8):
                    exp(n)
                    if n == 6:
                        output(0)
                    turned(n - 2)
                turned(6)
                turned(7)
                output(1)
            act.wait_ge(o_ev, HEADS + 2)
            squares(16, 8, Y)

            def gate_exps(n):
                act.wait_ge(top_done, n)
                act.activation(GATE, GATE, ACT.Exp).then_inc(gate_exp, 1)

            def gelu_rows(j, par):
                act.wait_ge(u_free, j * 4 + 8)
                act.wait_ge(act_done, j + 1)
                act.activation(GEL[par], DOT[par], ACT.Gelu).then_inc(gel_done, 1)

            def steps(b, names, between=None):
                def product(name):
                    if name in TILES_AT:
                        act.wait_ge(w_used, b * N_BLOCK + (N_ONCE + TILES_AT[name]))
                    else:
                        act.wait_ge(e_mm, b * len(PE_STEPS) + PE_AT[name])

                for name in names:
                    if name == "xs":
                        act.wait_ge(ln1_done, b + 1)
                        tick()
                        last = evict(XC, X[:, bass.ds(b * D, D)])
                    elif name[:3] in ("x1T", "x2T"):
                        q = int(name[3])
                        product(name)
                        last = evict(XT[:, q * 512:(q + 1) * 512], bank(4 + q))
                    elif name == "keep":
                        act.wait_ge(e_ev, b * len(ACT_STEPS) + ACT_AT["x2T3"])
                        tick()
                        last = evict(X[:, bass.ds(b * D, D)], XC)
                    elif name in ("q", "pq0", "pq1", "pq2", "pq3"):
                        product(name)
                        c = 0 if name == "q" else int(name[2]) % 2
                        last = evict(QB[c], bank(4 + c))
                    elif name == "qT":
                        product(name)
                        last = evict(QT, bank(5))
                    elif name[:3] == "pqT":
                        product(name)
                        last = evict(QT, bank(6))
                    elif name == "exp":
                        act.wait_ge(e_dv, b * len(DVE_STEPS) + DVE_AT["max"])
                        for h in range(MH):
                            last = act.activation(PR[:, h * MEM:(h + 1) * MEM],
                                                  ps[:, 6 + h // 2, (h % 2) * MEM:(h % 2 + 1) * MEM], ACT.Exp,
                                                  bias=NMX[:, h:h + 1], scale=MEM_SCALE, accum_out=RSUM[:, h:h + 1])
                    elif name == "pT":
                        product(name)
                        last = evict(PRT, ps[:, 4:6, :].rearrange("p a n -> p (a n)"))
                    elif name == "pv":
                        product(name)
                        last = evict(OT, bank(6))
                    elif name[:3] == "key":
                        product(name)
                        c = int(name[3])
                        act.wait_ge(sk_free, b * 4 + (c + 1))
                        last = evict(SK[c % 2], bank(7))
                    last.then_inc(e_ev, 1)
                    if between and name in between:
                        gelu_rows(*between[name])

            HEAD = ACT_STEPS[:ACT_AT["qT"]]
            TAIL = ACT_STEPS[ACT_AT["qT"]:]
            steps(0, HEAD)
            steps(0, TAIL)
            act.wait_ge(e_ev, ACT_AT["keep"])
            act.activation(ACC, X[:, 0:D], ACT.Copy, scale=ALPHA).then_inc(acc_ready, 1)
            steps(1, HEAD)
            gate_exps(1)
            gelu_rows(0, 0)

            def with_rows(b, j, after):
                steps(b, TAIL, {"pv": (j + 1, 1), "pq0": (j + 2, 0), "key1": (j + 3, 1)})
                after()
                gelu_rows(j + 4, 0)
                gate_exps(b + 1)

            with act.Fori(0, NB - 2) as i:
                with_rows(i + 1, i * JE, lambda: steps(i + 2, HEAD))

            def dense_tokens():
                for n in range(4 * DB):
                    act.wait_ge(xt_mm, n + 1)
                    evict(XT2[:, n * 512:(n + 1) * 512], bank(n % 4)).then_inc(xt_ev, 1)
                act.activation(X[:, 2 * D:4 * D], X[:, 2 * D:4 * D], ACT.Copy, scale=ALPHA).then_inc(scaled, 1)

            with_rows(NB - 1, (NB - 2) * JE, dense_tokens)
            gelu_rows(J0 - 3, 1)
            gelu_rows(J0 - 2, 0)
            act.wait_ge(tb_mm, 1)
            evict(TB, ps[:, 4:6, :].rearrange("p a n -> p (a n)")[:, 0:3 * DT]).then_inc(tb_ev, 1)
            for half in range(2):
                with act.Fori(half * (DT // TG // 4), (half + 1) * (DT // TG // 4)) as i:
                    for par in range(2):
                        act.wait_ge(ws_free, i * 2 + (par + 1))
                        with act.Fori(0, 4) as k:
                            for h in range(2):
                                act.wait_ge(oh_free, i * 16 + k * 2 + (par * 8 + h + 3))
                                tick()
                                evict(WS[par].rearrange("p (a t) -> p a t", t=TG)[:, :, bass.ds(k * 8 + 4 * h, 4)],
                                      bank(6 + h).rearrange("p (t a) -> p a t", t=4)).then_inc(ws_ev, 1)
                gelu_rows(J0 - 1 + half, 1 - half)

            def gelu_dense(g, par, before):
                act.wait_ge(g_ready, g + 1)
                for k in range(2):
                    act.wait_ge(w_used, before + (DENSE0 + 4 * k + 4))
                    act.activation(GL[:, k * 512:(k + 1) * 512], bank(par * 2 + k), ACT.Gelu).then_inc(gl_done, 1)

            def four_groups(i, switch=False, last=False):
                for k in range(4):
                    def rows(n):
                        j = i * JD + (J0 + n + 1)
                        if last and n == JD - 1:
                            return
                        gelu_rows(j, (J0 + n + 1) % 2)
                        if switch and j == JB:
                            act.wait_ge(y_ready, 1)
                            act.activation(ACC, X[:, D:2 * D], ACT.Copy, scale=ALPHA).then_inc(acc_ready, 1)

                    rows(STEPS[k][0])
                    if isinstance(i, int) and i == 0 and k == 0:
                        gelu_dense(0, 0, 0)
                    else:
                        gelu_dense(i * 4 + k, k % 2, i * (8 * NW) + (2 * k - 1) * NW)
                    for n in STEPS[k][1:]:
                        rows(n)

            act.wait_ge(gates_out, 16 * (DT // TG))
            four_groups(0)
            four_groups(1)
            four_groups(2, switch=True)
            with act.Fori(3, GROUPS // 4 - 1) as i:
                four_groups(i)
            four_groups(GROUPS // 4 - 1, last=True)

        @block.vector
        def _(dve):
            link = InOrder(dve, dve_done)

            def tick():
                dve.sem_inc(dve_tick, 1)

            def rsqrt(y, v, t):
                link(dve.tensor_scalar(y.bitcast(I32), v.bitcast(I32), 1, None, ALU.logical_shift_right))
                link(dve.tensor_scalar(y.bitcast(I32), y.bitcast(I32), -1.0, float(0x5f3759df), ALU.mult, ALU.add))
                for _ in range(3):
                    link(dve.tensor_tensor(t, y, y, ALU.mult))
                    link(dve.tensor_tensor(t, t, v, ALU.mult))
                    link(dve.tensor_scalar(t, t, -0.5, 1.5, ALU.mult, ALU.add))
                    link(dve.tensor_tensor(y, y, t, ALU.mult))

            def norm(src, dst, gain, bias, hold=None):
                for k in range(4):
                    last = dve.bn_stats(STATS[:, 6 * k:6 * k + 6], src[:, k * 512:(k + 1) * 512])
                link(last, hold)
                link(dve.bn_aggr(MV, STATS))
                link(dve.tensor_scalar(MV[:, 1:2], MV[:, 1:2], LN_EPS, None, ALU.add))
                rsqrt(RSTD, MV[:, 1:2], NEWTON)
                link(dve.tensor_scalar(dst, src, MV[:, 0:1], RSTD, ALU.subtract, ALU.mult))
                link(dve.tensor_tensor(dst, dst, gain, ALU.mult))
                return dve.tensor_tensor(dst, dst, bias, ALU.add)

            dve.sem_inc(conv_done, 2)
            dve.sem_inc(lru_done, 1)
            dve.sem_inc(qr_done, 1)
            dve.sem_inc(o_added, 8)
            dve.sem_inc(sk_free, 2)
            dve.sem_inc(act_done, 2)
            dve.sem_inc(g_ready, 1)
            dve.sem_inc(x_added, 4)
            dve.sem_inc(u_free, 4)
            dve.sem_inc(v_free, 4)
            lam = COLS[:, C_LAM:C_LAM + 16]
            dve.wait_ge(cols_in, 16)
            dve.scalar_tensor_tensor(out=LM[0], in0=lam, scalar=-1.0, in1=lam, op0=ALU.mult, op1=ALU.max
                                     ).then_inc(lam_abs, 1)
            link(dve.tensor_scalar(LM[2], lam, -4.0, 0.0, ALU.mult, ALU.max))
            dve.wait_ge(lam_exp, 1)
            link(dve.tensor_scalar(LM[3], LM[1], 2.0, None, ALU.add))
            link(dve.reciprocal(LM[4], LM[3]))
            link(dve.tensor_tensor(LM[3], LM[1], LM[4], ALU.mult))
            link(dve.tensor_tensor(LM[4], LM[3], LM[3], ALU.mult))
            link(dve.tensor_scalar(LM[5], LM[4], 1.0 / 15, None, ALU.mult))
            for odd in (13, 11, 9, 7, 5, 3):
                link(dve.scalar_tensor_tensor(out=LM[5], in0=LM[5], scalar=1.0 / odd, in1=LM[4],
                                              op0=ALU.add, op1=ALU.mult))
            link(dve.scalar_tensor_tensor(out=LM[5], in0=LM[5], scalar=1.0, in1=LM[3], op0=ALU.add, op1=ALU.mult))
            link(dve.scalar_tensor_tensor(out=C4, in0=LM[5], scalar=8.0, in1=LM[2], op0=ALU.mult, op1=ALU.add))
            dve.wait_ge(pos_in, 16)
            link(dve.tensor_copy(RS, TMP.bitcast(I32)))
            link(dve.tensor_scalar(RS, RS, col(C_FREQ), None, ALU.mult))
            link(dve.tensor_scalar(COS, RS, 1.0 / (2 * math.pi), ROUND, ALU.mult, ALU.add))
            link(dve.tensor_scalar(COS, COS, ROUND, None, ALU.subtract))
            for part in (TWO_PI_A, TWO_PI_B, TWO_PI_C):
                link(dve.scalar_tensor_tensor(out=RS, in0=COS, scalar=-part, in1=RS, op0=ALU.mult, op1=ALU.add))
            link(dve.tensor_scalar(RS, RS, 3.1415925, -3.1415925, ALU.min, ALU.max))
            link(dve.scalar_tensor_tensor(out=COS, in0=RS, scalar=-1.0, in1=RS, op0=ALU.mult, op1=ALU.max))
            dve.tensor_scalar(COS, COS, -1.0, math.pi / 2, ALU.mult, ALU.add).then_inc(angle, 1)
            dve.wait_ge(gain0_in, 32)
            for b in range(NB):
                dve.wait_ge(x_in[b], 16)
                xb = X[:, b * D:(b + 1) * D]
                norm(xb, xb, GAIN_G, GAIN_B).then_inc(ln0_done, 1)

            dve.wait_ge(consts_set, 5)
            with dve.Fori(0, NL // 2) as i:
                link.enter(i, 18)
                for e in range(2):
                    dve.wait_ge(xbank_free, i * 2 + (e + 3))

                    def cw(k):
                        return COLS[:, bass.ds(i * 2 + (C_CONVW + k * NL + e), 1)]

                    link(dve.tensor_scalar(XC1[e], LX[e][:, 0:S], cw(0), COLS[:, bass.ds(i * 2 + (C_CONVB + e), 1)],
                                           ALU.mult, ALU.add))
                    for k in range(1, 4):
                        last = dve.scalar_tensor_tensor(out=XC1[e], in0=LX[e][:, k:k + S], scalar=cw(k), in1=XC1[e],
                                                        op0=ALU.mult, op1=ALU.add)
                        if k < 3:
                            link(last)
                    last.then_inc(conv_done, 1)
                for e in range(2):
                    dve.wait_ge(u_ready, i * 2 + (e + 1))
                    dve.wait_ge(conv_done, i * 2 + 4)
                    for d in range(2):
                        dve.tensor_tensor(I_[d], I_[d], XC1[e], ALU.mult)
                        last = dve.tensor_scalar(D_[d], R_[d], 1.0, None, ALU.add)
                    link(last)
                    for d in range(2):
                        dve.scalar_tensor_tensor(out=I_[d], in0=I_[d], scalar=2.0, in1=H_[d], op0=ALU.mult, op1=ALU.mult)
                        last = dve.reciprocal(D_[d], D_[d])
                    link(last)
                    for d in range(2):
                        last = dve.tensor_tensor(I_[d], I_[d], D_[d], ALU.mult)
                    link(last)
                    for d in range(2):
                        last = dve.tensor_scalar(D_[d], D_[d], 2.0, -1.0, ALU.mult, ALU.add)
                    link(last)
                    dve.tensor_tensor_scan(H_[0], D_[0], I_[0], 0.0, ALU.mult, ALU.add)
                    link(dve.tensor_tensor_scan(H_[1][:, ::-1], D_[1][:, ::-1], I_[1][:, ::-1], 0.0, ALU.mult, ALU.add))
                    link(dve.tensor_tensor(H_[0], H_[0], H_[1], ALU.add))
                    dve.wait_ge(gbank_free, i * 2 + (e + 3))
                    gate = Y[:, bass.ds(i * 1024 + (8 + e) * S, S)]
                    dve.tensor_tensor(gate, gate, H_[0], ALU.mult).then_inc(lru_done, 1)
                link.leave(NL // 2)

            def rms(units, b, count, gains_at, region):
                dve.wait_ge(rms_mm, units)
                link(dve.tensor_scalar(TMP2, bank(b), 1.0 / (count * P), RMS_EPS, ALU.mult, ALU.add))
                rsqrt(RS, TMP2, TMP)
                for k in range(count):
                    r = region[:, k * S:(k + 1) * S]
                    last = dve.scalar_tensor_tensor(out=r, in0=r, scalar=col(gains_at + k), in1=RS,
                                                    op0=ALU.mult, op1=ALU.mult)
                last.then_inc(rms_done, 1)

            dve.wait_ge(rope_tab, 1)
            rms(4, 2, 4, C_KVG, C)
            rms(8, 3, 4, C_QG, C[:, 4 * S:8 * S])
            dve.wait_ge(w_used, 68)
            dve.tensor_tensor(KR, bank(0), COS, ALU.mult)
            link(dve.tensor_tensor(TMP, bank(1), SINS, ALU.mult))
            dve.tensor_tensor(KR, KR, TMP, ALU.add).then_inc(kr_done, 1)
            rms(16, 7, 8, C_LG, Y[:, 8 * S:16 * S])
            with dve.Fori(0, HEADS // 2) as hp:
                link.enter(hp, 1 + 8 * 2)
                dve.wait_ge(qpe_mm, hp + 1)
                dve.tensor_tensor(QR, bank(2), COS, ALU.mult)
                link(dve.tensor_tensor(TMP, bank(3), SINS, ALU.mult))
                dve.tensor_tensor(QR, QR, TMP, ALU.add).then_inc(qr_done, 1)

                def row_max(n):
                    dve.wait_ge(s_mm, hp * 8 + (n + 1))
                    link(dve.tensor_reduce(MX2[n % 4], bank(SCORE_BANKS[n % 4]), AX, ALU.max))
                    dve.tensor_scalar(NM2[n % 4], MX2[n % 4], -ATT_SCALE, None, ALU.mult).then_inc(nmx_done, 1)

                row_max(0)
                for n in range(8):
                    if n < 7:
                        row_max(n + 1)
                    dve.wait_ge(exp_done, hp * 8 + (n + 5))
                    link(dve.reciprocal(RI2[n % 4], RSM2[n % 4]))
                    dve.tensor_scalar(PM[n % 4], PM[n % 4], RI2[n % 4], None, ALU.mult).then_inc(p_done, 1)
                link.leave(HEADS // 2)
            rms(24, 7, 8, C_AG, Y)
            with dve.Fori(0, 2) as i:
                for cc in range(2):
                    dve.wait_ge(w_used, i * 16 + (76 + 8 * cc + 8))
                    for b in range(NB):
                        xs = X[:, bass.ds(i * 1024 + (b * D + cc * 512), 512)]
                        dve.scalar_tensor_tensor(out=xs, in0=xs, scalar=ALPHA, in1=bank(4 * cc + b),
                                                 op0=ALU.mult, op1=ALU.add).then_inc(o_added, 1)
            dve.wait_ge(o_added, 24)
            dve.wait_ge(gain1_in, 32)

            def first_norm(b):
                xb = X[:, b * D:(b + 1) * D]
                norm(xb, xb, GAIN1_G, GAIN1_B).then_inc(ln1_done, 1)

            first_norm(0)
            dve.wait_ge(gain2_in, 32)

            def soft(b):
                def evicted(name):
                    dve.wait_ge(e_ev, b * len(ACT_STEPS) + ACT_AT[name])

                dve.wait_ge(e_mm, b * len(PE_STEPS) + PE_AT["sc"])
                link(dve.tensor_reduce(MX, ps[:, 6:8, :].rearrange("p a (c m) -> p (a c) m", m=MEM), AX, ALU.max))
                dve.tensor_scalar(NMX, MX, -MEM_SCALE, None, ALU.mult).then_inc(e_dv, 1)
                evicted("exp")
                link(dve.reciprocal(RINV, RSUM))
                pr = PR.rearrange("p (h m) -> p h m", h=MH)
                dve.tensor_tensor(pr, pr, RINV.unsqueeze(2).broadcast_to([P, MH, MEM]), ALU.mult).then_inc(e_dv, 1)

            def second_norm(b):
                for c in QUAD:
                    dve.wait_ge(w_used, b * N_BLOCK + (N_ONCE + TILES_AT[f"wo{c}"]))
                    xs = XC[:, c * 512:(c + 1) * 512]
                    dve.scalar_tensor_tensor(out=xs, in0=xs, scalar=ALPHA, in1=bank(4 + c),
                                             op0=ALU.mult, op1=ALU.add).then_inc(e_dv, 1)
                dve.wait_ge(e_dv, b * len(DVE_STEPS) + DVE_AT["wo3"])
                norm(XC, XC, GAIN_G, GAIN_B, dve_tick).then_inc(e_dv, 1)

            def routing(b, c):
                def top16(src, width, vals, idxs, count):
                    for half in range(2):
                        def at(t, n):
                            return t[:, n * TOPK + half * 8:n * TOPK + half * 8 + 8]
                        for n in range(count):
                            last = dve.max(at(vals, n), src[:, n * width:(n + 1) * width])
                        link(last, dve_tick)
                        for n in range(count):
                            last = dve.max_index(at(idxs, n), at(vals, n), src[:, n * width:(n + 1) * width])
                        link(last, dve_tick)
                        if half == 0:
                            for n in range(count):
                                w = src[:, n * width:(n + 1) * width]
                                last = dve.match_replace(w, at(vals, n), w, -3.0e38)
                            link(last, dve_tick)

                dve.wait_ge(e_ev, b * len(ACT_STEPS) + ACT_AT[f"key{c}"])
                tick()
                top16(SK[c % 2], NK, TV, TI, 2 * HC)
                dve.sem_inc(sk_free, 1)
                tv = TV.rearrange("p (h t k) -> p h t k", t=2, k=TOPK)
                shape = [P, HC, TOPK, TOPK]

                def four(t):
                    return t.rearrange("p (h k a) -> p h k a", h=HC, k=TOPK)

                link(dve.tensor_tensor(four(CAND), tv[:, :, 0, :].unsqueeze(3).broadcast_to(shape),
                                       tv[:, :, 1, :].unsqueeze(2).broadcast_to(shape), ALU.add), dve_tick)
                top16(CAND, TOPK * TOPK, CV[:, c * CH:(c + 1) * CH], CP, HC)
                dve.tensor_scalar(CA, CP, 4, None, ALU.logical_shift_right)
                dve.tensor_scalar(CB, CP, 15, None, ALU.bitwise_and)
                link(dve.tensor_copy(TIF, TI))
                dve.tensor_copy(CAF, CA)
                link(dve.tensor_copy(CBF, CB))
                tif = TIF.rearrange("p (h t k) -> p h t k", t=2, k=TOPK)
                iota = IOTA[:, 0:TOPK].unsqueeze(1).unsqueeze(1).broadcast_to(shape)
                for half, place_f, number in ((0, CAF, S1), (1, CBF, S2)):
                    link(dve.tensor_tensor(four(EQ), place_f.rearrange("p (h k) -> p h k", k=TOPK).unsqueeze(3)
                                           .broadcast_to(shape), iota, ALU.is_equal))
                    link(dve.tensor_tensor(four(EQ), four(EQ), tif[:, :, half, :].unsqueeze(2).broadcast_to(shape),
                                           ALU.mult))
                    link(dve.tensor_reduce(number, EQ.rearrange("p (n a) -> p n a", a=TOPK), AX, ALU.add))
                here = bass.ds(b * HK + c * CH, CH)
                dve.scalar_tensor_tensor(out=IDX4[:, here], in0=S1, scalar=float(NK), in1=S2, op0=ALU.mult, op1=ALU.add)
                dve.tensor_scalar(S14[:, here], S1, 1.0, None, ALU.mult)
                link(dve.tensor_scalar(S24[:, here], S2, 1.0, None, ALU.mult))

            cv = CV.rearrange("p (h k) -> p h k", k=TOPK)
            gate = GATE.rearrange("p (h k) -> p h k", k=TOPK)

            def below_top():
                dve.tensor_tensor(gate, cv, cv[:, :, 0:1].broadcast_to([P, PH, TOPK]), ALU.subtract
                                  ).then_inc(top_done, 1)

            def gates(b):
                dve.wait_ge(gate_exp, b + 1)
                link(dve.tensor_reduce(GS, gate, AX, ALU.add))
                link(dve.reciprocal(GR, GS))
                dve.tensor_tensor(GATE4[:, bass.ds(b * HK, HK)].rearrange("p (h k) -> p h k", k=TOPK), gate,
                                  GR.unsqueeze(2).broadcast_to([P, PH, TOPK]), ALU.mult).then_inc(routed, 1)

            soft(0)
            second_norm(0)
            for b in range(1, NB):
                first_norm(b)
            for c in range(4):
                routing(0, c)
            below_top()
            gates(0)

            def dot(j, par, s, b):
                dve.wait_ge(u_full[s], j * 16 + 16)
                r = U_RING[:, s * D:(s + 1) * D]
                dve.tensor_tensor_reduce(r, r, X[:, b * D:(b + 1) * D], 1.0, 0.0, ALU.mult, ALU.add,
                                         DOT[par][:, s:s + 1]).then_inc(u_free, 1)

            def add_row(j, par, s):
                dve.wait_ge(v_full[s], j * 16 + 16)
                dve.wait_ge(v_free, j * 4 + (s + 4))
                dve.scalar_tensor_tensor(out=ACC, in0=V_RING[:, s * D:(s + 1) * D], scalar=AV[par][:, s:s + 1],
                                         in1=ACC, op0=ALU.mult, op1=ALU.add).then_inc(v_free, 1)

            def step(j, par, b):
                if b is not None:
                    dot(j + 1, 1 - par, 0, b)
                dve.wait_ge(gel_done, j + 1)
                dve.tensor_tensor(AV[par], GEL[par], GATE4[:, bass.ds(j * 4, 4)], ALU.mult).then_inc(act_done, 1)
                if b is not None:
                    dot(j + 1, 1 - par, 1, b)
                dve.wait_ge(act_done, j + 3)
                add_row(j, par, 0)
                for s in (1, 2):
                    if b is not None:
                        dot(j + 1, 1 - par, s + 1, b)
                    add_row(j, par, s)
                add_row(j, par, 3)

            def rest(b, j):
                step(j, 0, 0)
                second_norm(b)
                step(j + 1, 1, 0)
                routing(b, 0)
                step(j + 2, 0, 0)
                routing(b, 1)
                routing(b, 2)
                step(j + 3, 1, 0)
                routing(b, 3)
                below_top()
                gates(b)

            for s in range(4):
                dot(0, 0, s, 0)
            dve.wait_ge(acc_ready, 1)
            soft(1)
            with dve.Fori(0, NB - 2) as i:
                link.enter(i, 103)
                rest(i + 1, i * JE)
                soft(i + 2)
                link.leave(NB - 2)
            rest(NB - 1, (NB - 2) * JE)
            step(J0 - 4, 0, 0)
            step(J0 - 3, 1, 0)
            dve.wait_ge(routed, NB)

            dve.wait_ge(tb_ev, 1)
            turned = TB.rearrange("p (a t) -> p a t", a=3)
            for half in range(2):
                first = half * (DT // 16)
                with dve.Fori(first, first + DT // 16) as i:
                    link.enter(i - first if first else i, 2)
                    for h in range(2):
                        dve.wait_ge(oh_free, i * 2 + (h + 1))
                        oh = OH[h].rearrange("p (a t n) -> p a t n", a=2, t=4)
                        here = bass.ds(i * 8 + 4 * h, 4)
                        link(dve.tensor_tensor(oh, IOTA.unsqueeze(1).unsqueeze(1).broadcast_to([P, 2, 4, NK]),
                                               turned[:, 0:2, here].unsqueeze(3).broadcast_to([P, 2, 4, NK]),
                                               ALU.is_equal))
                        dve.tensor_tensor(oh[:, 0], oh[:, 0],
                                          turned[:, 2, here].unsqueeze(2).broadcast_to([P, 4, NK]), ALU.mult
                                          ).then_inc(oh_ready, 1)
                    link.leave(DT // 16)
                step(J0 - 2 + half, half, 0)

            def weigh(g, par, n):
                dve.wait_ge(gl_done, g * 2 + 6)
                dve.wait_ge(wd_in[par], n)
                dve.tensor_tensor(G[par].rearrange("p (e g t) -> p e g t", e=ET, t=TG),
                                  GL.rearrange("p (e g t) -> p e g t", e=ET, t=TG),
                                  WD[par].rearrange("p (g e t) -> p e g t", e=ET, t=TG), ALU.mult).then_inc(g_ready, 1)

            def add_dense(before, chunks):
                for c in chunks:
                    dve.wait_ge(w_used, before + (DENSE0 + 2 * c + 2))
                    for tb in range(DB):
                        xs = X[:, (NB - DB + tb) * D + c * 512:(NB - DB + tb) * D + (c + 1) * 512]
                        dve.tensor_tensor(xs, xs, bank(4 + (c % 2) * 2 + tb), ALU.add).then_inc(x_added, 1)

            def four_groups(i, b, switch=False, last=False):
                for k in range(4):
                    g = i * 4 + k
                    before = i * (8 * NW) + 2 * k * NW
                    started = not (isinstance(g, int) and g == 0)

                    def rows(n):
                        j = i * JD + (J0 + n)
                        block = b
                        if switch:
                            block = 1 if j + 1 >= JB else 0
                        if last and n == JD - 1:
                            block = None
                        step(j, (J0 + n) % 2, block)
                        if switch and j + 1 == JB:
                            dve.wait_ge(gain3_in, 32)
                            dve.wait_ge(v_free, JB * 4 + 4)
                            norm(ACC, X[:, 0:D], GAIN_G, GAIN_B, dve_tick).then_inc(y_ready, 1)
                            dve.wait_ge(acc_ready, 2)

                    rows(STEPS[k][0])
                    weigh(g, k % 2, i * 32 + (16 * (k // 2) + 16))
                    if started:
                        add_dense(before, (0, 1))
                    for n in STEPS[k][1:]:
                        rows(n)
                    if started:
                        add_dense(before, (2, 3))

            dve.wait_ge(scaled, 1)
            four_groups(0, 0)
            four_groups(1, 0)
            four_groups(2, None, switch=True)
            with dve.Fori(3, GROUPS // 4 - 1) as i:
                four_groups(i, 1)
            four_groups(GROUPS // 4 - 1, 1, last=True)
            dve.wait_ge(v_free, JG * 4 + 4)
            norm(ACC, X[:, D:2 * D], GAIN_G, GAIN_B, dve_tick).then_inc(y_ready, 1)
            add_dense((2 * GROUPS - 1) * NW, QUAD)
            dve.wait_ge(x_added, GROUPS * 8 + 4)
            for b in (2, 3):
                norm(X[:, b * D:(b + 1) * D], X[:, b * D:(b + 1) * D], GAIN_G, GAIN_B, dve_tick).then_inc(y_ready, 1)


def kernel(**a):
    import concourse.bacc as bacc
    from concourse.bass_utils import run_bass_kernel_spmd as run

    def f(name):
        return np.asarray(a[name])

    def tiles(w):
        k, n = w.shape[0] // P, w.shape[1]
        t = w.reshape(k, P, n).transpose(1, 0, 2).reshape(P, k * n)
        return t.reshape(P, -1, TW).transpose(1, 0, 2)

    def columns(v):
        return v.reshape(-1, P).T

    w_in, w_uq, w_ukv, w_out = f("w_in")[0], f("w_uq")[0], f("w_ukv")[0], f("w_out")[0]
    kpe = w_in[:, CKV:KPE]
    swap = np.concatenate([kpe[:, ROPE // 2:], kpe[:, :ROPE // 2]], 1)
    once = [tiles(f("w_mk")[0][:, h * P:(h + 1) * P]) for h in range(MH)] + [tiles(f("w_mv")[0])]
    for n in range(0, NL, 2):
        for first in (KPE, LRUX):
            for m in (n, n + 1):
                once.append(tiles(w_in[:, first + m * P:first + (m + 1) * P]))
    for first in (CQ, 0):
        for j in range(4):
            once.append(tiles(w_in[:, first + j * P:first + (j + 1) * P]))
    once += [tiles(np.concatenate([kpe, kpe], 1)), tiles(np.concatenate([swap, swap], 1))]
    ukv = w_ukv.reshape(LORA, HEADS, 2 * P)
    for h in range(0, HEADS, 2):
        once.append(np.concatenate([ukv[:, h + e, :P].reshape(4, P, P).transpose(1, 0, 2).reshape(1, P, 512)
                                    for e in range(2)], 2))
    v_cols = ukv[:, :, P:].reshape(LORA, HEADS * P)
    once += [tiles(v_cols[:, half * 512:(half + 1) * 512]) for half in range(2)]
    w_mix = np.roll(w_out, w_out.shape[0] // 2, 0)
    once += [tiles(w_mix[:, c * 512:(c + 1) * 512]) for c in range(4)]
    w_once = np.concatenate(once, 0)
    w_mo, w_pq = f("w_mo")[0], f("w_pq")[0]
    w_block = np.concatenate([tiles(f("w_mq")[0])] + [tiles(w_mo[:, c * 512:(c + 1) * 512]) for c in range(4)]
                             + [tiles(w_pq[:, c * 512:(c + 1) * 512]) for c in range(4)], 0)
    uq = w_uq.reshape(4, P, HEADS, NOPE + ROPE).transpose(1, 2, 0, 3)
    pairs = []
    for h in range(0, HEADS, 2):
        half = ROPE // 2
        pe = np.concatenate([uq[:, h, :, NOPE:], uq[:, h + 1, :, NOPE:]], 2)
        sw = np.concatenate([uq[:, h + e, :, NOPE + o:NOPE + o + half] for e in range(2) for o in (half, 0)], 2)
        pairs.append(np.stack([uq[:, h, :, :NOPE], uq[:, h + 1, :, :NOPE], pe, sw], 1).reshape(P, 2048))
    wa, wx = f("lru_wa")[0], f("lru_wx")[0]
    lru_w = np.stack([wa[0], wa[1], wx[0], wx[1]], 1).transpose(0, 2, 1, 3).reshape(NL, P, 4 * P)
    part = np.arange(P) % ROPE
    freq = np.float32(10000.0) ** (-(np.arange(0, ROPE, 2, dtype=np.float32)) / np.float32(ROPE))
    consts = np.stack([freq[part % (ROPE // 2)], np.where(part < ROPE // 2, -1.0, 1.0)], 1).astype(np.float32)
    cols = np.concatenate([columns(f(n)[0]) for n in ("conv_w", "conv_b", "lru_ba", "lru_bx", "lru_lambda", "q_norm_g",
                                                      "kv_norm_g", "attn_out_g", "lru_out_g")] + [consts], 1)
    arrays = {
        "x": f("x")[0],
        "memT": f("mem")[0].T.reshape(KT, P, MEM).transpose(1, 0, 2).reshape(P, KT * MEM),
        "pos": f("positions")[0],
        "cols": cols, "w_once": w_once, "w_block": w_block, "wq_pairs": np.stack(pairs), "lru_w": lru_w,
        "keysT": np.concatenate([f("sub_keys1")[0].T, f("sub_keys2")[0].T], 1),
        "gains": np.stack([f("in_ln_g"), f("in_ln_b"), f("ln1_g")[0], f("ln1_b")[0], f("ln2_g")[0], f("ln2_b")[0],
                           f("ln3_g")[0], f("ln3_b")[0]]),
        "peer_u": f("peer_u")[0], "peer_v": f("peer_v")[0],
        "peer_ut": f("peer_u")[0].reshape(P, P, 2, 8, P).transpose(0, 2, 4, 3, 1).reshape(2 * P, P, TW),
    }
    arrays = {k: np.ascontiguousarray(v) for k, v in arrays.items()}
    nc = bacc.Bacc("TRN2", target_bir_lowering=False, num_devices=1)
    args = [nc.dram_tensor(k, v.shape, mybir.dt.from_np(v.dtype), kind="ExternalInput").ap() for k, v in arrays.items()]
    out = nc.dram_tensor("y", (S, D), F32, kind="ExternalOutput").ap()
    gates_d = nc.dram_tensor("dense_gates", (DT // TG, P, NK * TG), F32, kind="Internal").ap()
    build(nc, *args, gates_d, out)
    r = run(nc, [arrays], core_ids=[0])
    return r.results[0]["y"].reshape(1, S, D)
```
